# Optimizing a Trainium2 kernel written in Bass

```python
import math
import jax, jax.numpy as jnp
from jax import lax
import numpy as np

D_MODEL = 1024
BATCH = 1
SEQ = 512
DEPTH = 1
DEC_BATCH = 8
DEC_SEQ = 4
PAST_LEN = 256
PAGE_SIZE = 128

MIX_WIDTH = D_MODEL
ATTN_WIDTH = MIX_WIDTH // 2
SSM_WIDTH = MIX_WIDTH - ATTN_WIDTH
DIFF_HEAD_DIM = 64
N_DIFF_HEADS = ATTN_WIDTH // (2 * DIFF_HEAD_DIM)
SSM_GROUP = 16
N_SSM_GROUPS = SSM_WIDTH // SSM_GROUP
SSM_STATE = 64
N_MEM = 256
N_MEM_HEADS = 4
MEM_HEAD_DIM = D_MODEL // N_MEM_HEADS
D_FF = -(-8 * D_MODEL // (3 * 256)) * 256
IN_COLS = 3 * ATTN_WIDTH + SSM_WIDTH
Q_BLOCK = 128
RMS_EPS = 1e-6
DT_MIN = 1e-3
DT_MAX = 1e-1

kernel_name = "hybrid_diffattn_s5_memory_decoder_step"

def rms_norm(x, g):
    xf = x.astype(jnp.float32)
    xf = xf * lax.rsqrt(jnp.mean(jnp.square(xf), axis=-1, keepdims=True) + RMS_EPS)
    return (xf * g.astype(jnp.float32)).astype(x.dtype)

def alibi_slopes():
    return 2.0 ** (-8.0 * jnp.arange(1, N_DIFF_HEADS + 1, dtype=jnp.float32) / N_DIFF_HEADS)

def diff_lambda(lq1, lk1, lq2, lk2, layer):
    lam_init = 0.8 - 0.6 * math.exp(-0.3 * layer)
    dot_exp = lambda a, b: jnp.exp(jnp.sum(a.astype(jnp.float32) * b.astype(jnp.float32)))
    return dot_exp(lq1, lk1) - dot_exp(lq2, lk2) + lam_init, lam_init

def project_mixer(hn, w_in):
    b, t, _ = hn.shape
    proj = hn @ w_in
    q, k, v, u = jnp.split(proj, [ATTN_WIDTH, 2 * ATTN_WIDTH, 3 * ATTN_WIDTH], axis=-1)
    q = q.reshape(b, t, N_DIFF_HEADS, 2, DIFF_HEAD_DIM)
    k = k.reshape(b, t, N_DIFF_HEADS, 2 * DIFF_HEAD_DIM)
    v = v.reshape(b, t, N_DIFF_HEADS, 2 * DIFF_HEAD_DIM)
    return q, k, v, u

def diff_attn_core(q, k, v, q_pos, k_pos, lam):
    s = jnp.einsum("bqhcd,bkhcd->bhcqk", q, k, preferred_element_type=jnp.float32)
    s = s * (DIFF_HEAD_DIM ** -0.5)
    dist = (q_pos[:, None] - k_pos[None, :]).astype(jnp.float32)
    bias = -alibi_slopes()[:, None, None] * dist
    s = jnp.where(dist >= 0, s + bias[:, None], -jnp.inf)
    p = jax.nn.softmax(s, axis=-1)
    p = p[:, :, 0] - lam * p[:, :, 1]
    return jnp.einsum("bhqk,bkhe->bqhe", p.astype(v.dtype), v)

def prompt_diff_attention(q, k, v, lam):
    b, t = q.shape[:2]
    nb = t // Q_BLOCK
    kk = k.reshape(b, t, N_DIFF_HEADS, 2, DIFF_HEAD_DIM)
    pos = jnp.arange(t, dtype=jnp.int32)
    qb = q.reshape(b, nb, Q_BLOCK, N_DIFF_HEADS, 2, DIFF_HEAD_DIM).swapaxes(0, 1)
    pb = pos.reshape(nb, Q_BLOCK)
    ob = lax.map(lambda a: diff_attn_core(a[0], kk, v, a[1], pos, lam), (qb, pb))
    return ob.swapaxes(0, 1).reshape(b, t, N_DIFF_HEADS, 2 * DIFF_HEAD_DIM)

def sample_diff_attention(q, k_new, v_new, ck, cv, page_table, lam):
    db, t = q.shape[:2]
    past = page_table.shape[1] * PAGE_SIZE
    k_past = ck[page_table].reshape(db, past, N_DIFF_HEADS, 2 * DIFF_HEAD_DIM)
    v_past = cv[page_table].reshape(db, past, N_DIFF_HEADS, 2 * DIFF_HEAD_DIM)
    k_all = jnp.concatenate([k_past, k_new.astype(k_past.dtype)], axis=1)
    k_all = k_all.reshape(db, past + t, N_DIFF_HEADS, 2, DIFF_HEAD_DIM)
    v_all = jnp.concatenate([v_past, v_new.astype(v_past.dtype)], axis=1)
    q_pos = past + jnp.arange(t, dtype=jnp.int32)
    k_pos = jnp.arange(past + t, dtype=jnp.int32)
    return diff_attn_core(q, k_all, v_all, q_pos, k_pos, lam)

def finish_diff_heads(o, g_subln, lam_init):
    o = rms_norm(o, g_subln) * (1.0 - lam_init)
    return o.reshape(o.shape[0], o.shape[1], ATTN_WIDTH)

def s5_mix(u, h0_re, h0_im, lam_re, lam_im, log_dt, b_re, b_im, c_re, c_im, d_skip):
    b, t, _ = u.shape
    f32 = jnp.float32
    uf = u.astype(f32).reshape(b, t, N_SSM_GROUPS, SSM_GROUP)
    lam = lax.complex(lam_re.astype(f32), lam_im.astype(f32))
    dt = jnp.exp(log_dt.astype(f32))[:, None]
    lam_bar = jnp.exp(lam * dt)
    b_bar = ((lam_bar - 1.0) / lam)[..., None] * lax.complex(b_re.astype(f32), b_im.astype(f32))
    bu = jnp.einsum("btgh,gph->btgp", uf.astype(jnp.complex64), b_bar)
    h0 = lax.complex(h0_re.astype(f32), h0_im.astype(f32))
    bu = bu.at[:, 0].add(lam_bar * h0)
    a = jnp.broadcast_to(lam_bar, bu.shape)

    def combine(e1, e2):
        a1, b1 = e1
        a2, b2 = e2
        return a1 * a2, a2 * b1 + b2

    _, h = lax.associative_scan(combine, (a, bu), axis=1)
    c = lax.complex(c_re.astype(f32), c_im.astype(f32))
    y = jnp.real(jnp.einsum("btgp,ghp->btgh", h, c)) + d_skip.astype(f32) * uf
    h_last = h[:, -1]
    return y.reshape(b, t, SSM_WIDTH).astype(u.dtype), jnp.real(h_last), jnp.imag(h_last)

def merge_groups(attn_o, ssm_y, w_glu, g_ssm_out, w_out):
    y = jax.nn.gelu(ssm_y)
    y = y * jax.nn.sigmoid(y @ w_glu)
    y = rms_norm(y, g_ssm_out)
    return jnp.concatenate([attn_o, y.astype(attn_o.dtype)], axis=-1) @ w_out

def mem_kv(mem, g_mem_kv, w_mk, w_mv):
    b = mem.shape[0]
    mn = rms_norm(mem, g_mem_kv)
    k = (mn @ w_mk).reshape(b, N_MEM, N_MEM_HEADS, MEM_HEAD_DIM)
    v = (mn @ w_mv).reshape(b, N_MEM, N_MEM_HEADS, MEM_HEAD_DIM)
    return k, v

def mem_attend(hn, mk, mv, w_mq, w_mo):
    b, t, _ = hn.shape
    q = (hn @ w_mq).reshape(b, t, N_MEM_HEADS, MEM_HEAD_DIM)
    s = jnp.einsum("bqhd,bkhd->bhqk", q, mk.astype(q.dtype), preferred_element_type=jnp.float32)
    p = jax.nn.softmax(s * (MEM_HEAD_DIM ** -0.5), axis=-1)
    o = jnp.einsum("bhqk,bkhd->bqhd", p.astype(q.dtype), mv.astype(q.dtype)).reshape(b, t, D_MODEL)
    return o @ w_mo

def swiglu(hn, w_gate, w_up, w_down):
    return (jax.nn.silu(hn @ w_gate) * (hn @ w_up)) @ w_down

def setup_inputs(seed: int = 0) -> dict:
    key = jax.random.key(seed)
    keys = iter(jax.random.split(key, 64))
    f32 = jnp.float32
    n_pages = PAST_LEN // PAGE_SIZE
    n_phys = (DEC_BATCH * n_pages * 5) // 4

    def normal(shape, scale):
        return jax.random.normal(next(keys), shape, f32) * scale

    def gain(shape):
        return 1.0 + normal(shape, 0.02)

    d = {}
    d["x_prompt"] = normal((BATCH, SEQ, D_MODEL), 1.0)
    d["x_sample"] = normal((DEC_BATCH, DEC_SEQ, D_MODEL), 1.0)
    d["mem_prompt"] = normal((BATCH, N_MEM, D_MODEL), 1.0)
    d["cache_k"] = normal((DEPTH, n_phys, PAGE_SIZE, N_DIFF_HEADS, 2 * DIFF_HEAD_DIM), 1.0)
    d["cache_v"] = normal((DEPTH, n_phys, PAGE_SIZE, N_DIFF_HEADS, 2 * DIFF_HEAD_DIM), 1.0)
    d["page_table"] = jax.random.permutation(next(keys), n_phys)[: DEC_BATCH * n_pages].reshape(DEC_BATCH, n_pages).astype(jnp.int32)
    d["state_ssm_re"] = normal((DEPTH, DEC_BATCH, N_SSM_GROUPS, SSM_STATE), 0.1)
    d["state_ssm_im"] = normal((DEPTH, DEC_BATCH, N_SSM_GROUPS, SSM_STATE), 0.1)
    d["cache_mem_k"] = normal((DEPTH, DEC_BATCH, N_MEM, N_MEM_HEADS, MEM_HEAD_DIM), 1.0)
    d["cache_mem_v"] = normal((DEPTH, DEC_BATCH, N_MEM, N_MEM_HEADS, MEM_HEAD_DIM), 1.0)
    d["g_mix_pre"] = gain((DEPTH, D_MODEL))
    d["g_mix_post"] = gain((DEPTH, D_MODEL))
    d["w_in"] = normal((DEPTH, D_MODEL, IN_COLS), D_MODEL ** -0.5)
    d["lam_q1"] = normal((DEPTH, DIFF_HEAD_DIM), 0.1)
    d["lam_k1"] = normal((DEPTH, DIFF_HEAD_DIM), 0.1)
    d["lam_q2"] = normal((DEPTH, DIFF_HEAD_DIM), 0.1)
    d["lam_k2"] = normal((DEPTH, DIFF_HEAD_DIM), 0.1)
    d["g_subln"] = gain((DEPTH, 2 * DIFF_HEAD_DIM))
    n_idx = jnp.arange(SSM_STATE, dtype=f32)
    d["ssm_lam_re"] = -0.5 + normal((DEPTH, N_SSM_GROUPS, SSM_STATE), 0.01)
    d["ssm_lam_im"] = jnp.pi * n_idx + normal((DEPTH, N_SSM_GROUPS, SSM_STATE), 0.01)
    d["ssm_log_dt"] = jax.random.uniform(next(keys), (DEPTH, N_SSM_GROUPS), f32, minval=math.log(DT_MIN), maxval=math.log(DT_MAX))
    d["ssm_b_re"] = normal((DEPTH, N_SSM_GROUPS, SSM_STATE, SSM_GROUP), (0.5 / SSM_GROUP) ** 0.5)
    d["ssm_b_im"] = normal((DEPTH, N_SSM_GROUPS, SSM_STATE, SSM_GROUP), (0.5 / SSM_GROUP) ** 0.5)
    d["ssm_c_re"] = normal((DEPTH, N_SSM_GROUPS, SSM_GROUP, SSM_STATE), (0.5 / SSM_STATE) ** 0.5)
    d["ssm_c_im"] = normal((DEPTH, N_SSM_GROUPS, SSM_GROUP, SSM_STATE), (0.5 / SSM_STATE) ** 0.5)
    d["ssm_d"] = normal((DEPTH, N_SSM_GROUPS, SSM_GROUP), 1.0)
    d["w_glu"] = normal((DEPTH, SSM_WIDTH, SSM_WIDTH), SSM_WIDTH ** -0.5)
    d["g_ssm_out"] = gain((DEPTH, SSM_WIDTH))
    d["w_out"] = normal((DEPTH, MIX_WIDTH, D_MODEL), MIX_WIDTH ** -0.5)
    d["g_mem_pre"] = gain((DEPTH, D_MODEL))
    d["g_mem_post"] = gain((DEPTH, D_MODEL))
    d["g_mem_kv"] = gain((DEPTH, D_MODEL))
    d["w_mq"] = normal((DEPTH, D_MODEL, D_MODEL), D_MODEL ** -0.5)
    d["w_mk"] = normal((DEPTH, D_MODEL, D_MODEL), D_MODEL ** -0.5)
    d["w_mv"] = normal((DEPTH, D_MODEL, D_MODEL), D_MODEL ** -0.5)
    d["w_mo"] = normal((DEPTH, D_MODEL, D_MODEL), D_MODEL ** -0.5)
    d["g_ffn_pre"] = gain((DEPTH, D_MODEL))
    d["g_ffn_post"] = gain((DEPTH, D_MODEL))
    d["w_gate"] = normal((DEPTH, D_MODEL, D_FF), D_MODEL ** -0.5)
    d["w_up"] = normal((DEPTH, D_MODEL, D_FF), D_MODEL ** -0.5)
    d["w_down"] = normal((DEPTH, D_FF, D_MODEL), D_FF ** -0.5)
    return d

def reference(x_prompt, x_sample, mem_prompt, cache_k, cache_v, page_table, state_ssm_re, state_ssm_im,
              cache_mem_k, cache_mem_v, g_mix_pre, g_mix_post, w_in, lam_q1, lam_k1, lam_q2, lam_k2, g_subln,
              ssm_lam_re, ssm_lam_im, ssm_log_dt, ssm_b_re, ssm_b_im, ssm_c_re, ssm_c_im, ssm_d, w_glu, g_ssm_out,
              w_out, g_mem_pre, g_mem_post, g_mem_kv, w_mq, w_mk, w_mv, w_mo, g_ffn_pre, g_ffn_post,
              w_gate, w_up, w_down):
    y_p, y_s = x_prompt, x_sample
    kp_l, vp_l, ks_l, vs_l = [], [], [], []
    rp_l, ip_l, rs_l, is_l = [], [], [], []
    mkp_l, mvp_l = [], []
    for l in range(DEPTH):
        lam, lam_init = diff_lambda(lam_q1[l], lam_k1[l], lam_q2[l], lam_k2[l], l)
        ssm_p = (ssm_lam_re[l], ssm_lam_im[l], ssm_log_dt[l], ssm_b_re[l], ssm_b_im[l],
                 ssm_c_re[l], ssm_c_im[l], ssm_d[l])
        hp = rms_norm(y_p, g_mix_pre[l])
        hs = rms_norm(y_s, g_mix_pre[l])
        qp, kp, vp, up = project_mixer(hp, w_in[l])
        qs, ks, vs, us = project_mixer(hs, w_in[l])
        att_p = finish_diff_heads(prompt_diff_attention(qp, kp, vp, lam), g_subln[l], lam_init)
        att_s = finish_diff_heads(sample_diff_attention(qs, ks, vs, cache_k[l], cache_v[l], page_table, lam),
                                  g_subln[l], lam_init)
        zeros = jnp.zeros((x_prompt.shape[0], N_SSM_GROUPS, SSM_STATE), jnp.float32)
        ssm_yp, rp, ip = s5_mix(up, zeros, zeros, *ssm_p)
        ssm_ys, rs, is_ = s5_mix(us, state_ssm_re[l], state_ssm_im[l], *ssm_p)
        y_p = y_p + rms_norm(merge_groups(att_p, ssm_yp, w_glu[l], g_ssm_out[l], w_out[l]), g_mix_post[l])
        y_s = y_s + rms_norm(merge_groups(att_s, ssm_ys, w_glu[l], g_ssm_out[l], w_out[l]), g_mix_post[l])
        mkp, mvp = mem_kv(mem_prompt, g_mem_kv[l], w_mk[l], w_mv[l])
        hp = rms_norm(y_p, g_mem_pre[l])
        hs = rms_norm(y_s, g_mem_pre[l])
        y_p = y_p + rms_norm(mem_attend(hp, mkp, mvp, w_mq[l], w_mo[l]), g_mem_post[l])
        y_s = y_s + rms_norm(mem_attend(hs, cache_mem_k[l], cache_mem_v[l], w_mq[l], w_mo[l]), g_mem_post[l])
        hp = rms_norm(y_p, g_ffn_pre[l])
        hs = rms_norm(y_s, g_ffn_pre[l])
        y_p = y_p + rms_norm(swiglu(hp, w_gate[l], w_up[l], w_down[l]), g_ffn_post[l])
        y_s = y_s + rms_norm(swiglu(hs, w_gate[l], w_up[l], w_down[l]), g_ffn_post[l])
        kp_l.append(kp); vp_l.append(vp); ks_l.append(ks); vs_l.append(vs)
        rp_l.append(rp); ip_l.append(ip); rs_l.append(rs); is_l.append(is_)
        mkp_l.append(mkp); mvp_l.append(mvp)
    new_k_prompt = jnp.stack(kp_l, 0)
    new_v_prompt = jnp.stack(vp_l, 0)
    new_k_sample = jnp.stack(ks_l, 0)
    new_v_sample = jnp.stack(vs_l, 0)
    ssm_re_prompt = jnp.stack(rp_l, 0)
    ssm_im_prompt = jnp.stack(ip_l, 0)
    ssm_re_sample = jnp.stack(rs_l, 0)
    ssm_im_sample = jnp.stack(is_l, 0)
    mem_k_prompt = jnp.stack(mkp_l, 0)
    mem_v_prompt = jnp.stack(mvp_l, 0)
    return (y_p, y_s, new_k_prompt, new_v_prompt, new_k_sample, new_v_sample,
            ssm_re_prompt, ssm_im_prompt, ssm_re_sample, ssm_im_sample, mem_k_prompt, mem_v_prompt)


_drawn_inputs = setup_inputs


def setup_inputs(seed=0):
    import zlib

    import numpy as np

    out = dict(_drawn_inputs(seed))
    spreads = {}
    factors = {'g_mix_pre': 2.771,
     'g_mix_post': 3.524,
     'lam_k1': 3.136,
     'lam_k2': 2.821,
     'g_subln': 5.773,
     'ssm_lam_re': 16.25,
     'g_ssm_out': 4.515,
     'g_mem_pre': 4.626,
     'g_mem_post': 12.602,
     'g_mem_kv': 2.909,
     'g_ffn_pre': 10.065,
     'g_ffn_post': 21.181}
    for name, (base, spread) in spreads.items():
        noise = np.random.default_rng([zlib.crc32(name.encode()), seed]).standard_normal(out[name].shape)
        drawn = base * np.exp(spread * noise) if base else spread * noise
        out[name] = __import__('jax').numpy.asarray(drawn.astype(out[name].dtype))
    for name, factor in factors.items():
        out[name] = (out[name] * factor).astype(out[name].dtype)
    return out
```

```python
import math
import numpy as np
import concourse.bass as bass
from concourse import mybir
from concourse.alu_op_type import AluOpType as ALU
from contextlib import ExitStack

F32 = mybir.dt.float32
F32R = mybir.dt.float32r
I32 = mybir.dt.int32
ACT = mybir.ActivationFunctionType
AX_X = mybir.AxisListType.X

P = 128
D = 1024
KT = D // P
NP_TOK = 512
DB, DT = 8, 4
NS_TOK = DB * DT
TOK = NP_TOK + NS_TOK
HALF = TOK // 2
PAGES, PAGE = 2, 128
PAST = PAGES * PAGE
NH, HD = 4, 64
NMEM, MH, MD = 256, 4, 256
NG, GH, SP_ = 32, 16, 64
CT_N = NG * SP_ // P
SF = NG * GH // P
BLK = 128
DFF = 2816
FT = DFF // P
EPS = 1e-6
LAM_INIT = 0.8 - 0.6 * math.exp(-0.3 * 0)
NEG = -1e30
N_ROW_LOADS = 12
N_PAR_LOADS = 1 + 2 + 4 + 2 + 4 + 1
SLOPES = [2.0 ** (-8.0 * (h + 1) / NH) for h in range(NH)]

G_MIX_PRE, G_MIX_POST, G_MEM_PRE, G_MEM_POST, G_MEM_KV, G_FFN_PRE, G_FFN_POST = range(0, 56, 8)
G_SSM, SSM_D, G_SUB, LAM_RE, LAM_IM, N_PAR = 56, 60, 64, 65, 81, 97

ALIBI_W = NP_TOK
DEC_W = PAST + NS_TOK


def shape_tables():
    ident = np.eye(P, dtype=np.float32)
    ones = np.ones((P, P), np.float32)
    p = np.arange(P)[:, None]
    x = np.arange(ALIBI_W)[None, :]
    dist = (p + (NP_TOK - P) - x).astype(np.float32)
    alibi = np.stack([np.where(dist >= 0, -s * dist, NEG) for s in SLOPES], 1).astype(np.float32)
    dec = np.full((P, 2, DEC_W), NEG, np.float32)
    sel = np.zeros((P, 2), np.float32)
    for r in range(P):
        h, q = (r % 16) // 4, r % 4
        sel[r, (r % 32) // 16] = 1.0
        for t in range(2):
            b = 4 * t + r // 32
            dec[r, t, :PAST] = -SLOPES[h] * (PAST + q - np.arange(PAST)).astype(np.float32)
            for j in range(q + 1):
                dec[r, t, PAST + b * DT + j] = -SLOPES[h] * float(q - j)
    return {"t_ident": ident, "t_ones": ones, "t_alibi": alibi, "t_dec": dec, "t_sel": sel}


def build(nc, A, O):
    ctx = ExitStack()
    sems = {}

    def sem(name):
        if name not in sems:
            sems[name] = ctx.enter_context(nc.semaphore(name))
        return sems[name]

    S = sem

    base = [16512]

    def at(name, shape, dtype, off):
        return nc.alloc_sbuf_tensor_at(name, shape, dtype, offset=off)

    def take(nbytes):
        o = base[0]
        base[0] += (nbytes + 31) // 32 * 32
        return o

    TOKB = TOK * 4
    yT = at("yT", [P, KT, TOK], F32, take(KT * TOKB))
    w_raw = at("w_raw", [P, 2, 2048], F32, take(16384))
    w_hi = at("w_hi", [P, 2, 2048], F32R, take(16384))
    w_lo = at("w_lo", [P, 2, 2048], F32R, take(16384))
    ident = at("ident", [P, P], F32, take(512))
    ones = at("ones", [P, P], F32, take(512))
    TMP = take(4 * TOKB)
    sq = at("sq", [P, 2, TOK], F32, TMP)
    tt = at("tt", [P, 2, TOK], F32, TMP + 2 * TOKB)
    W03 = at("W03", [P, 4, 512], F32, TMP)
    sqacc = at("sqacc", [P, TOK], F32, take(TOKB))
    rstd = at("rstd", [P, TOK], F32, take(TOKB))
    par = at("par", [P, N_PAR], F32, take(N_PAR * 4))
    small = at("small", [P, 64], F32, take(256))
    lam3 = at("lam3", [P, 3, CT_N], F32, take(192))
    sel = at("sel", [P, 2], F32, take(32))
    carry = at("carry", [P, CT_N, 2], F32, take(128))
    B0 = take(2 * KT * TOKB)
    C0 = take(0)
    assert nc.sbuf_usable_end - C0 >= 2 * FT * TOKB, (nc.sbuf_usable_end - C0, 2 * FT * TOKB)

    x_hi = at("x_hi", [P, KT, TOK], F32R, B0)
    x_lo = at("x_lo", [P, KT, TOK], F32R, B0 + KT * TOKB)
    alibi = at("alibi", [P, NH, ALIBI_W], F32, B0)
    decb = at("decb", [P, 2, DEC_W], F32, B0 + 8192)
    a_s = at("a_s", [P, 2, 2, 512], F32, B0 + 10496)
    a_p = at("a_p", [P, 2, 512], F32, B0 + 18688)
    a_pT = at("a_pT", [P, 4, 512], F32, B0 + 22784)
    k_tok = at("k_tok", [P, 512], F32, B0 + 30976)
    d_qz = at("d_qz", [P, DB, NH, 32], F32, B0)
    d_p = at("d_p", [P, 2, DEC_W], F32, B0 + 4096)
    d_pTn = at("d_pTn", [NS_TOK, DB, 32], F32, B0 + 6400)
    d_k = at("d_k", [P, 2, PAGES, 512], F32, B0 + 10496)
    d_v = at("d_v", [P, 2, PAGES, 512], F32, B0 + 18688)
    d_kT = at("d_kT", [P, NH, PAST], F32, B0 + 26880)
    d_o = at("d_o", [P, 2, 512], F32, B0 + 26880)
    d_pT = at("d_pT", [P, PAGES, DB, 32], F32, B0 + 30976)
    mem_nat = at("mem_nat", [P, 2, D], F32, B0)
    z_ffn = at("z_ffn", [P, KT, TOK], F32, B0)
    y_out = at("y_out", [P, 2, D], F32, B0 + KT * TOKB)

    qT = at("qT", [P, NH, TOK], F32, C0)
    kT = at("kT", [P, NH, TOK], F32, C0 + 8704)
    v_tok = at("v_tok", [P, 4, 512], F32, C0 + 17408)
    v_new = at("v_new", [NS_TOK, 512], F32, C0 + 25600)
    vT = at("vT", [P, NH, TOK], F32, C0 + 27648)
    oT = at("oT", [P, NH, TOK], F32, C0 + 27648)
    uT = at("uT", [P, SF, TOK], F32, C0 + 36352)
    rot = at("rot", [P, 2, CT_N, BLK], F32, C0 + 45056)
    b_lhs = at("b_lhs", [P, CT_N, 2, P], F32, C0 + 61440)
    c_lhs = at("c_lhs", [P, CT_N, 2, 32], F32, C0 + 77824)
    W47 = at("W47", [P, 4, 512], F32, C0 + 81920)
    b_pad = at("b_pad", [P, CT_N, P], F32, C0 + 81920)
    H_dec = at("H_dec", [P, CT_N, 2, NS_TOK], F32, C0 + 90112)
    st = at("st", [P, 2, P], F32, C0 + 94208)
    st_nat = at("st_nat", [P, 2, P], F32, C0 + 90112)
    x_nat = at("x_nat", [P, 5, D], F32, C0)
    xs = at("xs", [P, 5, D], F32, C0 + 45056)
    p_rows = at("p_rows", [N_PAR, P], F32, C0 + 20480)
    b_nat = at("b_nat", [P, 2, CT_N, GH], F32, C0 + 20992)
    c_nat = at("c_nat", [P, 2, SF, 2, SP_], F32, C0 + 23040)
    b_bar = at("b_bar", [P, 2, CT_N, GH], F32, C0 + 27136)
    b_tmp = at("b_tmp", [P, 2, CT_N, GH], F32, C0 + 29184)
    sp = at("sp", [P, 28, CT_N], F32, C0 + 31232)
    dt2 = at("dt2", [CT_N, 2], F32, C0 + 33024)
    dt_rows = at("dt_rows", [CT_N, 2, SP_], F32, C0 + 33056)
    lamv = at("lamv", [P, 4, HD], F32, C0 + 33568)
    lamp = at("lamp", [P, 2, HD], F32, C0 + 34592)
    att_hi = at("att_hi", [P, NH, TOK], F32R, C0)
    att_lo = at("att_lo", [P, NH, TOK], F32R, C0 + 8704)
    y1_hi = at("y1_hi", [P, SF, TOK], F32R, C0 + 45056)
    y1_lo = at("y1_lo", [P, SF, TOK], F32R, C0 + 53760)
    ssm_hi = at("ssm_hi", [P, SF, TOK], F32R, C0 + 62464)
    ssm_lo = at("ssm_lo", [P, SF, TOK], F32R, C0 + 71168)
    z = at("z", [P, KT, TOK], F32, C0 + 17408)
    mn_hi = at("mn_hi", [P, KT, NMEM], F32R, C0 + 45056)
    mn_lo = at("mn_lo", [P, KT, NMEM], F32R, C0 + 53248)
    qm = at("qm", [P, KT, TOK], F32, C0)
    m_p = at("m_p", [P, 2, NMEM], F32, C0 + 17408)
    m_pT = at("m_pT", [P, 2, 512], F32, C0 + 19456)
    dm_p = at("dm_p", [P, 2, NMEM], F32, C0 + 23552)
    dm_pT = at("dm_pT", [P, 2, 2, P], F32, C0 + 25600)
    KV_N = 3
    dm_kv = at("dm_kv", [P, KV_N, 2, D], F32, C0 + 34816)
    mkT = at("mkT", [P, KT, NMEM], F32, C0 + 61440)
    mv_tok = at("mv_tok", [P, 2, D], F32, C0 + 69632)
    mk_tok = at("mk_tok", [P, 2, D], F32, C0 + 77824)
    dm_kT = at("dm_kT", [P, KT, NMEM], F32, C0 + 77824)
    dm_o = at("dm_o", [P, 2, D], F32, C0 + 77824)
    dm_qz = at("dm_qz", [P, DB, KT, 32], F32, C0 + 86016)
    g_hi = at("g_hi", [P, FT, TOK], F32R, C0)
    g_lo = at("g_lo", [P, FT, TOK], F32R, C0 + FT * TOKB)

    pall = ctx.enter_context(nc.psum_tensor("pall", [P, 8, 512], F32))

    def bank(i):
        return pall[:, i, :]

    def banks(i):
        return pall[:, i:i + 2, :].rearrange("p a b -> p (a b)")[:, 0:TOK]

    def halves(i):
        return pall[:, i:i + 2, 0:HALF]

    def acc(j):
        return halves(2 * (j % 2))

    def two(ap):
        return ap.rearrange("p (a b) -> p a b", a=2)

    def view(name, k0, kts, c0, cols):
        return A[name][0, k0 * P:(k0 + kts) * P, c0:c0 + cols].rearrange("(k p) c -> p k c", p=P)

    units = []

    def add_units(name, cols_list, kts=KT, cols=256):
        first = len(units)
        for c in cols_list:
            units.append((view(name, 0, kts, c, cols), kts, cols))
        return first

    U_W_IN = add_units("w_in", [1536, 1792] + list(range(0, 1536, 256)))
    U_GLU = add_units("w_glu", [0], kts=SF, cols=512)
    U_OUT = add_units("w_out", range(0, D, 256))
    U_MK = add_units("w_mk", range(0, D, 256))
    U_MV = add_units("w_mv", range(0, D, 256))
    U_MQ = add_units("w_mq", range(0, D, 256))
    U_MO = add_units("w_mo", range(0, D, 256))
    U_FFN = len(units)
    assert U_FFN == 29
    PAIRS = DFF // 256
    U_DOWN = U_FFN + 2 * PAIRS
    DOWN_K = [(0, 8), (8, 8), (16, 6)]
    DOWN_C = D // 256
    N_UNITS = U_DOWN + DOWN_C * len(DOWN_K)

    J_W_IN = 0
    J_GLU = J_W_IN + 16
    J_OUT = J_GLU + 4
    J_MK = J_OUT + 8
    J_MV = J_MK + 8
    J_MQ = J_MV + 8
    J_MO = J_MQ + 8
    J_FFN = J_MO + 8
    J_DOWN = J_FFN + 4 * PAIRS
    assert J_FFN % 2 == 0 and J_DOWN % 2 == 0

    def used(n):
        if n <= U_OUT - 1:
            return J_W_IN + 2 * (n + 1) if n < U_GLU else J_OUT
        return J_OUT + 2 * (n - U_OUT + 1)

    NORMS = [("ssmn", SF), ("n1", KT), ("n2", KT), ("n3", KT), ("n4", KT), ("n5", KT)]
    SPLIT, RESID = ("ssmn", "n2", "n4"), ("n1", "n3", "n5")

    def counted(name, what, n):
        before = NORMS[:[x for x, _ in NORMS].index(name)]
        if what in ("sq", "add"):
            n += sum(t - (what == "add") for _, t in before)
        elif what in ("t", "hi", "lo"):
            n += sum(t for x, t in before if x in SPLIT)
        elif what == "y":
            n += sum(t for x, t in before if x in RESID)
        else:
            n += len(before)
        return S("norm_" + what), n

    parts_lo, LO_FFN = counted("n4", "lo", KT)

    S5_UNITS = [(f, k) for k in range(NP_TOK // BLK) for f in range(SF)]
    ATT = [(h, i) for h in range(NH) for i in range(4)]
    MATT = [(h, i) for h in range(MH) for i in range(4)]

    order = [("main", 0), ("par", 0), ("main", 1), ("mats", 0), ("xT", 0)]
    s5 = [(half, n) for n in range(16) for half in ("s5a", "s5b")]
    for u in range(2, 8):
        order.append(("main", u))
        order += [s5.pop(0), s5.pop(0)]
    for t in range(5):
        order += [("vtr", t), ("ktr", t)]
    for n in range(16):
        order.append(("att", n))
        if s5:
            order.append(s5.pop(0))
    order.append(("att_end", 0))
    order += s5
    order += [("s5_end", 0), ("s5d", 0), ("gelu", 0)]
    order += [("dk", b) for b in range(DB)] + [("dsoft", 0)] + [("dv", b) for b in range(DB)] + [("dout", 0)]
    order += [("subln", 0), ("glu", 0), ("mem_in", 0), ("out", 0)]

    w_loaded = [S("w_loaded0"), S("w_loaded1")]
    w_hi_ready, w_lo_ready = S("w_hi_ready"), S("w_lo_ready")
    acc_full, acc_out = S("acc_full"), S("acc_out")
    consts_in, x_in, rows_in, par_in, mem_in = S("consts_in"), S("x_in"), S("rows_in"), S("par_in"), S("mem_in")
    stored = S("stored")
    act_own, dve_own, pool_own, pe_own = S("act_own"), S("dve_own"), S("pool_own"), S("pe_own")
    n_stores = [0]

    block = ctx.enter_context(nc.Block())

    @block.sync
    def _(sp_eng):
        e = sp_eng

        def load_unit(n):
            dram, kts, cols = units[n]
            if n >= 2:
                e.wait_ge(w_lo_ready, n - 1)
            e.dma_start(w_raw[:, n % 2, 0:kts * cols].rearrange("p (k c) -> p k c", k=kts), dram)\
                .then_inc(w_loaded[n % 2], 16)

        def store(dst, src):
            n_stores[0] += 1
            e.dma_start(dst, src).then_inc(stored, 16)

        x_view = A["x_prompt"].rearrange("b (t p) d -> p (b t) d", p=P)
        for t in range(4):
            e.dma_start(x_nat[:, t, :], x_view[:, t, :]).then_inc(x_in, 16)
        e.dma_start(x_nat[0:NS_TOK, 4, :], A["x_sample"].rearrange("b t d -> (b t) d")).then_inc(x_in, 16)
        e.dma_start(ident[:], A["t_ident"]).then_inc(consts_in, 16)
        e.dma_start(ones[:], A["t_ones"]).then_inc(consts_in, 16)
        for name, row, n in (("g_mix_pre", G_MIX_PRE, 8), ("g_mix_post", G_MIX_POST, 8), ("g_mem_pre", G_MEM_PRE, 8),
                             ("g_mem_post", G_MEM_POST, 8), ("g_mem_kv", G_MEM_KV, 8), ("g_ffn_pre", G_FFN_PRE, 8),
                             ("g_ffn_post", G_FFN_POST, 8), ("g_ssm_out", G_SSM, 4)):
            e.dma_start(p_rows[row:row + n, :], A[name][0].rearrange("(k p) -> k p", p=P)).then_inc(rows_in, 16)
        e.dma_start(p_rows[SSM_D:SSM_D + 4, :], A["ssm_d"][0].rearrange("(k g) h -> k (g h)", k=4)).then_inc(rows_in, 16)
        e.dma_start(p_rows[G_SUB:G_SUB + 1, :], A["g_subln"]).then_inc(rows_in, 16)
        e.dma_start(p_rows[LAM_RE:LAM_RE + 16, :], A["ssm_lam_re"][0].rearrange("(c g) s -> c (g s)", g=2)).then_inc(rows_in, 16)
        e.dma_start(p_rows[LAM_IM:LAM_IM + 16, :], A["ssm_lam_im"][0].rearrange("(c g) s -> c (g s)", g=2)).then_inc(rows_in, 16)
        e.dma_start(dt2[:], A["ssm_log_dt"][0].rearrange("(c g) -> c g", g=2)).then_inc(par_in, 16)
        load_unit(0)
        load_unit(1)
        for r, name in enumerate(("ssm_b_re", "ssm_b_im")):
            e.dma_start(b_nat[:, r], A[name][0].rearrange("(c g) s h -> (g s) c h", g=2)).then_inc(par_in, 16)
        for r, name in enumerate(("ssm_c_re", "ssm_c_im")):
            for dup in range(2):
                e.dma_start(c_nat[:, r, :, dup, :], A[name][0].rearrange("(f g) h s -> (g h) f s", f=SF)).then_inc(par_in, 16)
        for r, name in enumerate(("state_ssm_re", "state_ssm_im")):
            e.dma_start(st_nat[:, r, :], A[name][0].rearrange("b (c g) s -> (b c) (g s)", g=2)).then_inc(par_in, 16)
        for i, name in enumerate(("lam_q1", "lam_k1", "lam_q2", "lam_k2")):
            e.dma_start(lamv[:, i, :], A[name].broadcast_to([P, HD])).then_inc(par_in, 16)
        e.dma_start(sel[:], A["t_sel"]).then_inc(par_in, 16)
        nxt = [2]

        def ahead(n):
            while nxt[0] <= min(n, U_FFN + 1):
                if nxt[0] < U_FFN:
                    load_unit(nxt[0])
                    nxt[0] += 1
                else:
                    break

        out_kp = O["new_k_prompt"].rearrange("l b (t p) h d -> t p (l b h d)", p=P)
        out_ks = O["new_k_sample"].rearrange("l b t h d -> (l b t) (h d)")
        out_vp = O["new_v_prompt"].rearrange("l b (t p) h d -> t p (l b h d)", p=P)
        out_vs = O["new_v_sample"].rearrange("l b t h d -> (l b t) (h d)")
        ck = A["cache_k"].rearrange("l n t h d -> (l n) t (h d)")
        cv = A["cache_v"].rearrange("l n t h d -> (l n) t (h d)")
        n_phys = ck.shape[0]

        def page_load(dst, cache, b, waits, done):
            for pg in range(PAGES):
                page = e.value_load(A["page_table"][b:b + 1, pg:pg + 1], min_val=0, max_val=n_phys - 1)
                if pg == 0:
                    for s_, v_ in waits:
                        e.wait_ge(s_, v_)
                e.dma_start(dst[:, b % 2, pg, :], cache[bass.ds(page, 1), :, :].rearrange("n t c -> t (n c)")).then_inc(done, 16)

        for kind, n in order:
            if kind == "main":
                ahead(n + 2)
                if n == 7:
                    e.wait_ge(acc_full, used(7))
                    e.dma_start(alibi[:], A["t_alibi"]).then_inc(S("alibi_in"), 16)
                    e.dma_start(decb[:], A["t_dec"]).then_inc(S("alibi_in"), 16)
            elif kind == "vtr":
                if n == 0:
                    ahead(9)
                e.wait_ge(S("v_tok_ready"), n + 1)
                if n < 4:
                    store(out_vp[n], v_tok[:, n, :])
                else:
                    store(out_vs, v_new[:])
            elif kind == "ktr":
                e.wait_ge(S("k_tok_ready"), n + 1)
                if n < 4:
                    e.dma_start(out_kp[n], k_tok[:]).then_inc(S("k_stored"), 16)
                else:
                    e.dma_start(out_ks, k_tok[0:NS_TOK, :]).then_inc(S("k_stored"), 16)
            elif kind == "s5_end":
                e.wait_ge(S("fin_ready"), 1)
                for r, name in enumerate(("ssm_re_prompt", "ssm_im_prompt")):
                    store(O[name].rearrange("l b (c g) s -> (l b c) (g s)", g=2), W47[0:CT_N, 0, r * P:(r + 1) * P])
            elif kind == "s5d":
                e.wait_ge(S("fin_ready"), 2)
                for r, name in enumerate(("ssm_re_sample", "ssm_im_sample")):
                    store(O[name].rearrange("l b (c g) s -> (l b c) (g s)", g=2), W47[:, 1, r * P:(r + 1) * P])
            elif kind == "dk":
                if n == 0:
                    for b in range(2):
                        page_load(d_k, ck, b, [(S("att_pT"), 16)], S(f"dk_in{b % 2}"))
                if n + 2 < DB:
                    page_load(d_k, ck, n + 2, [(S("dkT_full"), 2 * (n + 1))], S(f"dk_in{n % 2}"))
                if n < 2:
                    page_load(d_v, cv, n, [(S("att_pT"), 16)], S(f"dv_in{n % 2}"))
            elif kind == "dv":
                if n + 2 < DB:
                    page_load(d_v, cv, n + 2, [(S("dv_done"), n + 1)], S(f"dv_in{n % 2}"))
            elif kind == "mem_in":
                e.wait_ge(S("subln_lo"), 4)
                e.wait_ge(S("dT_out"), 2)
                e.dma_start(mem_nat[:], A["mem_prompt"].rearrange("b (t p) d -> p (b t) d", p=P)).then_inc(mem_in, 16)
            elif kind == "out":
                ahead(U_MQ + 1)
        e.wait_ge(S("mk_tok_ready"), 4)
        e.dma_start(O["mem_k_prompt"].rearrange("l b (t p) h d -> p (l b t) (h d)", p=P), mk_tok[:]).then_inc(S("mk_stored"), 16)
        e.wait_ge(acc_out, J_MQ)
        store(O["mem_v_prompt"].rearrange("l b (t p) h d -> p (l b t) (h d)", p=P), mv_tok[:])
        ahead(U_MQ + 3)
        mk_view = A["cache_mem_k"].rearrange("l b (t p) h d -> (l b) p t (h d)", p=P)
        mv_view = A["cache_mem_v"].rearrange("l b (t p) h d -> (l b) p t (h d)", p=P)

        def kv_load(i):
            if i == 0:
                e.wait_ge(acc_full, used(U_MQ - 1))
            if i >= KV_N:
                j = i - KV_N
                if j < DB:
                    e.wait_ge(S("dmT_pe"), 4 * (j + 1))
                else:
                    e.wait_ge(S("dm_pv"), j - DB + 1)
            src = mk_view[i] if i < DB else mv_view[i - DB]
            e.dma_start(dm_kv[:, i % KV_N], src).then_inc(S(f"kv_in{i % KV_N}"), 16)

        for i in range(KV_N):
            kv_load(i)
        ahead(U_MO - 1)
        ahead(U_MO + 1)
        for i in range(KV_N, 2 * DB):
            kv_load(i)
        ahead(U_FFN - 1)
        gate = A["w_gate"][0].rearrange("(k p) c -> p k c", p=P)
        up = A["w_up"][0].rearrange("(k p) c -> p k c", p=P)
        with e.Fori(0, PAIRS) as i:
            for s_, w in enumerate((gate, up)):
                slot = (U_FFN + s_) % 2
                e.wait_ge(w_lo_ready, i * 2 + (U_FFN + s_ - 1))
                e.dma_start(w_raw[:, slot, :].rearrange("p (k c) -> p k c", k=KT), w[:, :, bass.ds(i * 256, 256)])\
                    .then_inc(w_loaded[slot], 16)
        down = A["w_down"][0].rearrange("(k p) c -> p k c", p=P)
        for n in range(U_DOWN, N_UNITS):
            c, (k0, kts) = (n - U_DOWN) // 3, DOWN_K[(n - U_DOWN) % 3]
            e.wait_ge(w_lo_ready, n - 1)
            e.dma_start(w_raw[:, n % 2, 0:kts * 256].rearrange("p (k c) -> p k c", k=kts),
                        down[:, k0:k0 + kts, c * 256:(c + 1) * 256]).then_inc(w_loaded[n % 2], 16)
        out_y = O["y_prompt"].rearrange("b (t p) d -> (b t) p d", p=P)
        for t in range(5):
            e.wait_ge(S("y_out_ready"), 4 * (t + 1))
            if t < 4:
                e.dma_start(out_y[t], y_out[:, t % 2, :]).then_inc(S(f"y_stored{t % 2}"), 16)
            else:
                e.dma_start(O["y_sample"].rearrange("b t d -> (b t) d"), y_out[0:NS_TOK, 0, :]).then_inc(S("y_stored0"), 16)
        e.wait_ge(S("y_stored0"), 48)
        e.wait_ge(S("y_stored1"), 32)
        e.wait_ge(S("k_stored"), 16 * 5)
        e.wait_ge(S("mk_stored"), 16)
        e.wait_ge(stored, 16 * n_stores[0])

    @block.gpsimd
    def _(pool):
        e = pool

        def split_lo(n, kts, cols, i=None, per=0):
            off = 0 if i is None else i * per
            e.wait_ge(w_hi_ready, off + (n + 1))
            w = kts * cols
            e.tensor_tensor(w_lo[:, n % 2, 0:w], w_raw[:, n % 2, 0:w], w_hi[:, n % 2, 0:w].bitcast(F32), ALU.subtract)\
                .then_inc(w_lo_ready, 1)

        todo = [0]

        def lo_ahead(n):
            while todo[0] <= min(n, U_FFN - 1):
                _, kts, cols = units[todo[0]]
                split_lo(todo[0], kts, cols)
                todo[0] += 1

        lo_ahead(1)
        for kind, n in order:
            if kind == "main":
                lo_ahead(n + 1)
            elif kind == "s5a":
                e.wait_ge(S("s5_in_mul"), n + 1)
                if n > 0:
                    e.wait_ge(S("s5_y"), n)
                    e.wait_ge(S("s5_carry"), n)
                e.tensor_tensor(W47[:, 0], W03[:, 0], W03[:, 1], ALU.add)
                e.tensor_tensor(W47[:, 1], W03[:, 2], W03[:, 3], ALU.subtract).then_inc(S("s5_in_sum"), 1)
            elif kind == "s5b":
                e.wait_ge(S("s5_out_mul"), n + 1)
                e.tensor_tensor(W47[:, 0], W03[:, 0], W03[:, 1], ALU.subtract)
                e.tensor_tensor(W47[:, 1], W03[:, 2], W03[:, 3], ALU.add).then_inc(S("s5_h"), 1)
            elif kind == "vtr" and n == 0:
                lo_ahead(9)
            elif kind == "out":
                lo_ahead(U_MQ - 1)
        lo_ahead(U_FFN - 1)
        with e.Fori(0, PAIRS) as i:
            for s_ in range(2):
                split_lo(U_FFN + s_, KT, 256, i, 2)
        for n in range(U_DOWN, N_UNITS):
            split_lo(n, DOWN_K[(n - U_DOWN) % 3][1], 256)

    @block.scalar
    def _(act):
        e = act
        own = [0]

        def done(ins):
            own[0] += 1
            ins.then_inc(act_own, 1)
            e.wait_ge(act_own, own[0])

        def split_hi(n, kts, cols, i=None, per=0):
            off = 0 if i is None else i * per
            loads = (0 if i is None else i * (8 * per)) + 16 * (n // 2 + 1)
            e.wait_ge(w_loaded[n % 2], loads)
            if n >= 2:
                e.wait_ge(acc_full, off * 2 + used(n - 2))
            w = kts * cols
            e.activation(w_hi[:, n % 2, 0:w], w_raw[:, n % 2, 0:w], ACT.Copy).then_inc(w_hi_ready, 1)

        todo = [0]

        def hi_ahead(n):
            while todo[0] <= min(n, U_FFN - 1):
                _, kts, cols = units[todo[0]]
                split_hi(todo[0], kts, cols)
                todo[0] += 1

        def square_stats(name, src, tiles, ready):
            for k in range(tiles):
                for s_, v_ in ready(k):
                    e.wait_ge(s_, v_)
                if k >= 2:
                    e.wait_ge(*counted(name, "add", max(1, k - 2)))
                e.activation(sq[:, k % 2, :], src[:, k, :], ACT.Square).then_inc(S("norm_sq"), 1)

        def root(name):
            e.wait_ge(*counted(name, "ms", 1))
            e.activation(rstd[:], rstd[:], ACT.Sqrt).then_inc(S("norm_root"), 1)

        def scaled_hi(name, hi, tiles, gcol):
            for k in range(tiles):
                e.wait_ge(*counted(name, "t", k + 1))
                e.activation(hi[:, k, :], tt[:, k % 2, :], ACT.Copy, scale=gcol(k)).then_inc(S("norm_hi"), 1)

        def evac(j, dst, func=ACT.Copy, scale=1.0, n=HALF, full=None):
            e.wait_ge(acc_full, full or j + 1)
            src = acc(j) if n == HALF else bank(2 * (j % 2))[:, 0:n]
            e.activation(dst, src, func, scale=scale).then_inc(acc_out, 1)

        def att_tail(n):
            h, i = ATT[n]
            e.wait_ge(S("att_pT"), n + 1)
            if i == 0 and h > 0:
                e.wait_ge(S("att_pv"), h)
            e.activation(a_pT[:, 0:i + 1, i * P:(i + 1) * P], bank(2)[:, 0:(i + 1) * P].rearrange("p (a b) -> p a b", b=P), ACT.Copy)\
                .then_inc(S("att_pTo"), 1)
            if i == 3:
                e.wait_ge(S("att_pv"), h + 1)
                e.activation(oT[:, h, 0:NP_TOK], bank(3), ACT.Copy).then_inc(S("att_oT"), 1)

        def ma_tail(n):
            h, i = MATT[n]
            e.wait_ge(S("ma_pT"), n + 1)
            if i == 0 and h > 0:
                e.wait_ge(S("ma_pv"), 2 * h)
            e.activation(m_pT[:, :, i * P:(i + 1) * P], bank(6)[:, 0:NMEM].rearrange("p (a b) -> p a b", a=2), ACT.Copy)\
                .then_inc(S("ma_pTo"), 1)

        for t in range(5):
            rows = P if t < 4 else NS_TOK
            e.wait_ge(x_in, 16 * 5)
            e.activation(xs[0:rows, t, :], x_nat[0:rows, t, :], ACT.Square, accum_out=small[0:rows, t:t + 1]).then_inc(S("x_ss"), 1)
        e.wait_ge(S("x_ms"), 2)
        e.activation(small[:, 8:12], small[:, 8:12], ACT.Sqrt)
        e.activation(small[0:NS_TOK, 12:13], small[0:NS_TOK, 12:13], ACT.Sqrt).then_inc(S("x_root"), 1)
        e.wait_ge(S("x_rstd"), 2)
        e.wait_ge(S("x_ss"), 5)
        for t in range(5):
            rows = P if t < 4 else NS_TOK
            e.activation(xs[0:rows, t, :], x_nat[0:rows, t, :], ACT.Copy, scale=small[0:rows, 16 + t:17 + t]).then_inc(S("xs_ready"), 1)
        hi_ahead(1)
        e.wait_ge(S("par_ready"), 1)
        for k in range(KT):
            e.wait_ge(S("xsT_full"), k + 1)
            e.activation(x_hi[:, k, :], banks(4 + 2 * (k % 2)), ACT.Copy, scale=par[:, G_MIX_PRE + k:G_MIX_PRE + k + 1])\
                .then_inc(S("xs_hi"), 1)

        for kind, n in order:
            if kind == "main":
                for m in range(2):
                    if m == 0:
                        hi_ahead(n + 1)
                    j = J_W_IN + 2 * n + m
                    t = j % 4
                    dst = {0: uT, 1: qT, 2: kT, 3: vT}[j // 4]
                    evac(j, two(dst[:, t, :]), scale=HD ** -0.5 if dst is qT else 1.0)
            elif kind == "par":
                e.wait_ge(S("dtT_ready"), 1)
                e.activation(sp[:, 1], sp[:, 0], ACT.Exp).then_inc(S("p_dt"), 1)
                e.wait_ge(S("lam_dots"), 2)
                e.activation(small[:, 24:26], small[:, 24:26], ACT.Exp).then_inc(S("lam_exp"), 1)
                e.wait_ge(S("p_arg"), 2)
                e.activation(sp[:, 4], sp[:, 2], ACT.Tanh, scale=0.5).then_inc(S("p_trig"), 1)
                e.activation(sp[:, 5], sp[:, 3], ACT.Sin).then_inc(S("p_trig"), 1)
                e.activation(sp[:, 6], sp[:, 3], ACT.Sin, scale=0.5).then_inc(S("p_trig"), 1)
            elif kind == "mats":
                for g in range(2 * SF):
                    r, f = g // SF, g % SF
                    e.wait_ge(S("bT_full"), g + 1)
                    e.activation(b_lhs[:, 4 * f:4 * f + 4, r, :], bank(7).rearrange("p (a b) -> p a b", a=4), ACT.Copy)\
                        .then_inc(S("bT_out"), 1)
            elif kind == "xT":
                for k in range(KT):
                    e.wait_ge(S("xT_full"), k + 1)
                    e.activation(yT[:, k, :], banks(6), ACT.Copy).then_inc(S("xT_out"), 1)
            elif kind in ("vtr", "ktr"):
                if kind == "vtr" and n == 0:
                    hi_ahead(9)
                e.wait_ge(S(kind + "_full"), n + 1)
                rows = P if n < 4 else NS_TOK
                if kind == "vtr":
                    dst = v_tok[:, n, :] if n < 4 else v_new[:]
                    e.activation(dst, bank(7)[0:rows, :], ACT.Copy).then_inc(S("v_tok_ready"), 1)
                else:
                    if n >= 1:
                        e.wait_ge(S("k_stored"), 16 * n)
                    e.activation(k_tok[0:rows, :], bank(7)[0:rows, :], ACT.Copy).then_inc(S("k_tok_ready"), 1)
            elif kind == "att":
                h, i = ATT[n]
                nk = (i + 1) * P
                e.wait_ge(S("att_max"), n + 1)
                for c in range(2):
                    ins = e.activation(a_s[:, n % 2, c, 0:nk], a_s[:, n % 2, c, 0:nk], ACT.Exp,
                                       bias=small[:, 28 + 2 * (n % 2) + c:29 + 2 * (n % 2) + c],
                                       accum_out=small[:, 32 + 2 * (n % 2) + c:33 + 2 * (n % 2) + c])
                ins.then_inc(S("att_exp"), 1)
                if n >= 1:
                    att_tail(n - 1)
            elif kind == "att_end":
                att_tail(15)
            elif kind == "s5_end":
                e.wait_ge(S("fin_full"), 1)
                e.activation(W47[0:CT_N, 0, 0:256], bank(7)[0:CT_N, 0:256], ACT.Copy).then_inc(S("fin_ready"), 1)
            elif kind == "s5d":
                e.wait_ge(S("fin_full"), 2)
                e.activation(W47[:, 1, 0:256], bank(7)[:, 0:256], ACT.Copy).then_inc(S("fin_ready"), 1)
            elif kind == "gelu":
                e.wait_ge(S("yssm"), 17)
                for f in range(SF):
                    done(e.activation(uT[:, f, :], uT[:, f, :], ACT.Gelu_apprx_tanh))
                    e.activation(y1_hi[:, f, :], uT[:, f, :], ACT.Copy).then_inc(S("y1_hi"), 1)
            elif kind == "dk":
                for g in range(2):
                    e.wait_ge(S("dkT_full"), 2 * n + g + 1)
                    if n > 0 and g == 0:
                        e.wait_ge(S("ds_done"), n)
                    e.activation(d_kT[:, 2 * g:2 * g + 2, :], bank(6 + g).rearrange("p (a b) -> p a b", a=2), ACT.Copy)\
                        .then_inc(S("dkT_done"), 1)
            elif kind == "dsoft":
                for t in range(2):
                    e.wait_ge(S("ds_max"), t + 1)
                    e.activation(d_p[:, t, :], d_p[:, t, :], ACT.Exp, bias=small[:, 28 + t:29 + t],
                                 accum_out=small[:, 32 + t:33 + t]).then_inc(S("ds_exp"), 1)
            elif kind == "dout":
                for t in range(2):
                    e.wait_ge(S("dv_done"), 4 * (t + 1))
                    e.activation(d_o[:, t, :], bank(4 + t), ACT.Copy).then_inc(S("do_out"), 1)
            elif kind == "subln":
                for h in range(NH):
                    if h == 0:
                        e.wait_ge(S("att_oT"), 4)
                        e.wait_ge(S("dT_out"), 2)
                    if h >= 2:
                        e.wait_ge(S("subln_sum"), h - 1)
                    e.activation(sq[:, h % 2, :], oT[:, h, :], ACT.Square).then_inc(S("subln_sq"), 1)
                    e.wait_ge(S("subln_ms"), h + 1)
                    e.activation(rstd[:], rstd[:], ACT.Sqrt).then_inc(S("subln_root"), 1)
                    e.wait_ge(S("subln_t"), h + 1)
                    e.activation(att_hi[:, h, :], tt[:, h % 2, :], ACT.Copy, scale=small[:, 27:28]).then_inc(S("subln_hi"), 1)
            elif kind == "glu":
                e.wait_ge(S("subln_lo"), NH)
                for m in range(4):
                    if m >= 2:
                        e.wait_ge(S("y2"), m - 1)
                    e.wait_ge(acc_full, J_GLU + m + 1)
                    e.activation(two(tt[:, m % 2, :]), acc(J_GLU + m), ACT.Sigmoid).then_inc(acc_out, 1)
                square_stats("ssmn", uT, SF, lambda k: [(S("y2"), k + 1)])
                root("ssmn")
                scaled_hi("ssmn", ssm_hi, SF, lambda k: par[:, G_SSM + k:G_SSM + k + 1])
            elif kind == "mem_in":
                e.wait_ge(mem_in, 16)
                for t in range(2):
                    e.activation(W47[:, 2 * t:2 * t + 2, :].rearrange("p a b -> p (a b)"), mem_nat[:, t, :], ACT.Square,
                                 accum_out=small[:, t:t + 1]).then_inc(S("m_ss"), 1)
                e.wait_ge(S("m_ms"), 1)
                e.activation(small[:, 8:10], small[:, 8:10], ACT.Sqrt).then_inc(S("m_root"), 1)
                e.wait_ge(S("m_rstd"), 1)
                for t in range(2):
                    e.activation(mem_nat[:, t, :], mem_nat[:, t, :], ACT.Copy, scale=small[:, 16 + t:17 + t]).then_inc(S("ms_ready"), 1)
                for k in range(KT):
                    e.wait_ge(S("mT_full"), k + 1)
                    e.activation(mn_hi[:, k, :], bank(6 + k % 2)[:, 0:NMEM], ACT.Copy,
                                 scale=par[:, G_MEM_KV + k:G_MEM_KV + k + 1]).then_inc(S("mn_hi"), 1)
            elif kind == "out":
                for n_ in range(4):
                    hi_ahead(U_OUT + n_ + 1)
                    for m in range(2):
                        k = 2 * n_ + m
                        if k == 0:
                            e.wait_ge(S("subln_lo"), 4)
                        evac(J_OUT + k, two(z[:, k, :]))
        square_stats("n1", z, KT, lambda k: [(acc_out, J_OUT + k + 1)])
        root("n1")

        def mk_units(lo, hi):
            for n_ in range(lo, hi):
                hi_ahead(U_MK + n_ + 1)
                for m in range(2):
                    j = J_MK + 2 * n_ + m
                    k = 2 * n_ + m
                    if n_ < 4:
                        if k == 0:
                            e.wait_ge(acc_full, used(U_MK - 1))
                        evac(j, mkT[:, k, :], n=NMEM)
                    else:
                        evac(j, mv_tok[:, m, (n_ - 4) * 256:(n_ - 3) * 256], n=256)

        mk_units(0, 2)
        square_stats("n2", yT, KT, lambda k: [counted("n1", "y", k + 1)])
        root("n2")
        mk_units(2, 4)
        scaled_hi("n2", x_hi, KT, lambda k: par[:, G_MEM_PRE + k:G_MEM_PRE + k + 1])
        mk_units(4, 8)
        for g in range(4):
            e.wait_ge(S("mkt_full"), g + 1)
            e.activation(mk_tok[:, g // 2, (g % 2) * 512:(g % 2 + 1) * 512], bank(6 + g % 2), ACT.Copy).then_inc(S("mk_tok_ready"), 1)
        for n_ in range(4):
            hi_ahead(U_MQ + n_ + 1)
            for m in range(2):
                evac(J_MQ + 2 * n_ + m, two(qm[:, 2 * n_ + m, :]))
        for n, (h, i) in enumerate(MATT):
            e.wait_ge(S("ma_max"), n + 1)
            if n >= 2:
                e.wait_ge(S("ma_pT"), n - 1)
            e.activation(m_p[:, n % 2, :], bank(4 + n % 2)[:, 0:NMEM], ACT.Exp, scale=MD ** -0.5,
                         bias=small[:, 28 + n % 2:29 + n % 2], accum_out=small[:, 32 + n % 2:33 + n % 2]).then_inc(S("ma_exp"), 1)
            if n >= 1:
                ma_tail(n - 1)
        ma_tail(15)
        for b in range(DB):
            for g in range(4):
                e.wait_ge(S("dmT_pe"), 4 * b + g + 1)
                if b > 0 and g == 0:
                    e.wait_ge(S("dms"), b)
                e.activation(dm_kT[:, 2 * g:2 * g + 2, :], bank(6 + g % 2).rearrange("p (a b) -> p a b", a=2), ACT.Copy)\
                    .then_inc(S("dmT_out"), 1)
        for t in range(2):
            e.wait_ge(S("dm_max"), t + 1)
            e.activation(dm_p[:, t, :], bank(4 + t)[:, 0:NMEM], ACT.Exp, scale=MD ** -0.5, bias=small[:, 28 + t:29 + t],
                         accum_out=small[:, 32 + t:33 + t]).then_inc(S("dm_exp"), 1)
        for t in range(2):
            for g in range(2):
                e.wait_ge(S("dm_pv"), 4 * (t + 1))
                e.activation(dm_o[:, t, g * 512:(g + 1) * 512], bank(4 + 2 * t + g), ACT.Copy).then_inc(S("dmo_out"), 1)
        for n_ in range(4):
            hi_ahead(U_MO + n_ + 1)
            for m in range(2):
                k = 2 * n_ + m
                evac(J_MO + k, two(z[:, k, :]))
        square_stats("n3", z, KT, lambda k: [(acc_out, J_MO + k + 1)])
        root("n3")
        square_stats("n4", yT, KT, lambda k: [counted("n3", "y", k + 1)])
        root("n4")
        scaled_hi("n4", x_hi, KT, lambda k: par[:, G_FFN_PRE + k:G_FFN_PRE + k + 1])
        split_hi(U_FFN, KT, 256)
        with e.Fori(0, PAIRS) as i:
            split_hi(U_FFN + 1, KT, 256, i, 2)
            for m in range(2):
                e.wait_ge(acc_full, i * 4 + (J_FFN + m + 1))
                e.wait_ge(acc_out, i * 4 + (J_FFN + m))
                e.activation(two(tt[:, m, :]), acc(m), ACT.Silu).then_inc(acc_out, 1)
            split_hi(U_FFN + 2, KT, 256, i, 2)
            for m in range(2):
                e.wait_ge(acc_out, i * 4 + (J_FFN + 2 + m + 1))
                e.activation(g_hi[:, bass.ds(i * 2 + m, 1), :], sq[:, m:m + 1, :], ACT.Copy).then_inc(S("g_hi_ready"), 1)
        for n in range(U_DOWN, N_UNITS):
            if n + 1 < N_UNITS:
                split_hi(n + 1, DOWN_K[(n + 1 - U_DOWN) % 3][1], 256)
            c, part = (n - U_DOWN) // 3, (n - U_DOWN) % 3
            if part == 2:
                for m in range(2):
                    evac(J_DOWN + 2 * c + m, two(z_ffn[:, 2 * c + m, :]), full=used(n) - 1 + m)
        square_stats("n5", z_ffn, KT, lambda k: [(acc_out, J_DOWN + k + 1)])
        root("n5")
        for t in range(5):
            rows = P if t < 4 else NS_TOK
            for g in range(4):
                e.wait_ge(S("yt_full"), 4 * t + g + 1)
                if t >= 2 and g == 0:
                    e.wait_ge(S(f"y_stored{t % 2}"), 16 * (t // 2))
                e.activation(y_out[0:rows, t % 2, g * 256:(g + 1) * 256], bank(4 + g)[0:rows, 0:256], ACT.Copy).then_inc(S("y_out_ready"), 1)

    @block.vector
    def _(dve):
        e = dve
        own = [0]

        def done(ins):
            own[0] += 1
            ins.then_inc(dve_own, 1)
            e.wait_ge(dve_own, own[0])

        def mul(out, a, b):
            return e.tensor_tensor(out, a, b, ALU.mult)

        def add(out, a, b):
            return e.tensor_tensor(out, a, b, ALU.add)

        def sub(out, a, b):
            return e.tensor_tensor(out, a, b, ALU.subtract)

        def sum_squares(name, tiles):
            for k in range(1, tiles):
                e.wait_ge(*counted(name, "sq", k + 1))
                if k == 1:
                    add(sqacc[:], sq[:, 0, :], sq[:, 1, :]).then_inc(S("norm_add"), 1)
                else:
                    e.wait_ge(*counted(name, "add", k - 1))
                    add(sqacc[:], sqacc[:], sq[:, k % 2, :]).then_inc(S("norm_add"), 1)

        def make_rstd(name, width):
            e.wait_ge(*counted(name, "sum", 1))
            e.tensor_scalar(two(rstd[:]), halves(6), 1.0 / width, EPS, ALU.mult, ALU.add).then_inc(S("norm_ms"), 1)
            e.wait_ge(*counted(name, "root", 1))
            done(e.reciprocal(rstd[:], rstd[:]))

        def split_scaled(name, src, lo, hi, tiles, gcol):
            def low(k):
                e.wait_ge(*counted(name, "hi", k + 1))
                e.scalar_tensor_tensor(out=lo[:, k, :], in0=tt[:, k % 2, :], scalar=gcol(k), in1=hi[:, k, :].bitcast(F32),
                                       op0=ALU.mult, op1=ALU.subtract).then_inc(S("norm_lo"), 1)
            for k in range(tiles):
                if k >= 2:
                    e.wait_ge(*counted(name, "lo", k - 1))
                mul(tt[:, k % 2, :], src[:, k, :], rstd[:]).then_inc(S("norm_t"), 1)
                if k >= 1:
                    low(k - 1)
            low(tiles - 1)

        def residual(name, src, gbase):
            for k in range(KT):
                done(mul(tt[:, k % 2, :], src[:, k, :], rstd[:]))
                e.scalar_tensor_tensor(out=yT[:, k, :], in0=tt[:, k % 2, :], scalar=par[:, gbase + k:gbase + k + 1],
                                       in1=yT[:, k, :], op0=ALU.mult, op1=ALU.add).then_inc(S("norm_y"), 1)

        e.wait_ge(S("x_ss"), 5)
        e.tensor_scalar(small[:, 8:12], small[:, 0:4], 1.0 / D, EPS, ALU.mult, ALU.add).then_inc(S("x_ms"), 1)
        e.tensor_scalar(small[0:NS_TOK, 12:13], small[0:NS_TOK, 4:5], 1.0 / D, EPS, ALU.mult, ALU.add).then_inc(S("x_ms"), 1)
        e.wait_ge(S("x_root"), 1)
        e.reciprocal(small[:, 16:20], small[:, 8:12]).then_inc(S("x_rstd"), 1)
        e.reciprocal(small[0:NS_TOK, 20:21], small[0:NS_TOK, 12:13]).then_inc(S("x_rstd"), 1)
        e.wait_ge(S("par_full"), 1)
        e.tensor_copy(par[:], bank(0)[:, 0:N_PAR]).then_inc(S("par_ready"), 1)
        for k in range(KT):
            e.wait_ge(S("xs_hi"), k + 1)
            e.scalar_tensor_tensor(out=x_lo[:, k, :], in0=banks(4 + 2 * (k % 2)), scalar=par[:, G_MIX_PRE + k:G_MIX_PRE + k + 1],
                                   in1=x_hi[:, k, :].bitcast(F32), op0=ALU.mult, op1=ALU.subtract).then_inc(S("xs_lo"), 1)

        def s5_carry(n):
            f, _ = S5_UNITS[n]
            e.wait_ge(S("s5_h"), n + 1)
            for r in range(2):
                ins = e.tensor_copy(carry[:, 4 * f:4 * f + 4, r], W47[:, r, :].rearrange("p (q t) -> p q t", q=4)[:, :, BLK - 1])
            ins.then_inc(S("s5_carry"), 1)

        def s5_out(n):
            f, blk = S5_UNITS[n]
            cols = slice(blk * BLK, (blk + 1) * BLK)
            e.wait_ge(S("s5_y"), n + 1)
            e.scalar_tensor_tensor(out=uT[:, f, cols], in0=uT[:, f, cols], scalar=par[:, SSM_D + f:SSM_D + f + 1],
                                   in1=bank(6)[:, 0:BLK], op0=ALU.mult, op1=ALU.add).then_inc(S("yssm"), 1)

        NM, L, R, MX = 28, 32, 36, 40

        def att_tail(n):
            h, i = ATT[n]
            nk = (i + 1) * P
            o = 2 * (n % 2)
            e.wait_ge(S("att_exp"), n + 1)
            done(e.reciprocal(small[:, R + o:R + o + 2], small[:, L + o:L + o + 2]))
            done(mul(small[:, R + o + 1:R + o + 2], small[:, R + o + 1:R + o + 2], small[:, 26:27]))
            done(e.tensor_scalar(a_s[:, n % 2, 1, 0:nk], a_s[:, n % 2, 1, 0:nk], small[:, R + o + 1:R + o + 2], None, ALU.mult))
            if n >= 2:
                e.wait_ge(S("att_pT"), n - 1)
            e.scalar_tensor_tensor(out=a_p[:, n % 2, 0:nk], in0=a_s[:, n % 2, 0, 0:nk], scalar=small[:, R + o:R + o + 1],
                                   in1=a_s[:, n % 2, 1, 0:nk], op0=ALU.mult, op1=ALU.add).then_inc(S("att_p"), 1)

        for kind, n in order:
            if kind == "par":
                e.wait_ge(par_in, 16 * N_PAR_LOADS)
                e.tensor_copy(dt_rows[:], dt2[:].unsqueeze(2).broadcast_to([CT_N, 2, SP_])).then_inc(S("dt_rows"), 1)
                for i in range(2):
                    e.tensor_tensor_reduce(out=lamp[:, i, :], in0=lamv[:, 2 * i, :], in1=lamv[:, 2 * i + 1, :], scale=1.0,
                                           scalar=0.0, op0=ALU.mult, op1=ALU.add, accum_out=small[:, 24 + i:25 + i])\
                        .then_inc(S("lam_dots"), 1)
                e.memset(b_pad[:], 0.0)
                done(e.memset(c_lhs[:], 0.0))
                e.wait_ge(S("dtT"), 1)
                e.tensor_copy(sp[:, 0], bank(4)[:, 0:CT_N]).then_inc(S("dtT_ready"), 1)
                e.wait_ge(S("stT"), 1)
                e.tensor_copy(st[:].rearrange("p a b -> p (a b)"), bank(5)[:, 0:2 * P]).then_inc(S("st_ready"), 1)
                e.wait_ge(S("lam_exp"), 1)
                done(sub(small[:, 26:27], small[:, 25:26], small[:, 24:25]))
                done(e.tensor_scalar(small[:, 26:27], small[:, 26:27], -LAM_INIT, None, ALU.add))
                e.tensor_scalar(small[:, 27:28], par[:, G_SUB:G_SUB + 1], 1.0 - LAM_INIT, None, ALU.mult)
                done(e.scalar_tensor_tensor(out=small[:, 44:45], in0=sel[:, 1:2], scalar=small[:, 26:27], in1=sel[:, 0:1],
                                            op0=ALU.mult, op1=ALU.add))
                lre, lim = par[:, LAM_RE:LAM_RE + CT_N], par[:, LAM_IM:LAM_IM + CT_N]
                c = lambda i: sp[:, i]
                e.wait_ge(S("p_dt"), 1)
                mul(c(2), lre, c(1)).then_inc(S("p_arg"), 1)
                done(mul(c(7), lim, c(1)))
                done(e.tensor_scalar(c(8), c(7), 1.0 / (2 * math.pi), None, ALU.mult))
                done(e.tensor_scalar(c(8), c(8), 12582912.0, None, ALU.add))
                done(e.tensor_scalar(c(8), c(8), -12582912.0, None, ALU.add))
                c1 = 6.28125
                c2 = float(np.float32(math.floor((2 * math.pi - c1) * 2 ** 21) / 2 ** 21))
                c3 = 2 * math.pi - c1 - c2
                for part in (c1, c2, c3):
                    done(e.scalar_tensor_tensor(out=c(7), in0=c(8), scalar=-part, in1=c(7), op0=ALU.mult, op1=ALU.add))
                e.tensor_scalar(c(3), c(7), 3.1415925, -3.1415925, ALU.min, ALU.max).then_inc(S("p_arg"), 1)
                e.wait_ge(S("p_trig"), 3)
                done(e.tensor_scalar(c(9), c(4), -1.0, 1.0, ALU.mult, ALU.add))
                done(e.reciprocal(c(9), c(9)))
                done(e.tensor_scalar(c(10), c(4), 1.0, None, ALU.add))
                done(mul(lam3[:, 0], c(10), c(9)))
                done(mul(c(11), c(4), c(9)))
                done(mul(c(12), c(6), c(6)))
                done(e.tensor_scalar(c(12), c(12), -2.0, None, ALU.mult))
                done(e.tensor_scalar(c(13), c(12), 1.0, None, ALU.add))
                done(mul(lam3[:, 1], lam3[:, 0], c(13)))
                done(mul(lam3[:, 2], lam3[:, 0], c(5)))
                done(e.scalar_tensor_tensor(out=c(14), in0=c(11), scalar=2.0, in1=c(13), op0=ALU.mult, op1=ALU.mult))
                done(add(c(14), c(14), c(12)))
                done(mul(c(15), lre, lre))
                done(mul(c(16), lim, lim))
                done(add(c(15), c(15), c(16)))
                done(e.reciprocal(c(15), c(15)))
                done(mul(c(16), c(14), lre))
                done(mul(c(17), lam3[:, 2], lim))
                done(add(c(16), c(16), c(17)))
                done(mul(c(18), c(16), c(15)))
                done(mul(c(16), lam3[:, 2], lre))
                done(mul(c(17), c(14), lim))
                done(sub(c(16), c(16), c(17)))
                done(mul(c(19), c(16), c(15)))
                wr, wi = (c(i).unsqueeze(2).broadcast_to([P, CT_N, GH]) for i in (18, 19))
                for r, (x, y, op) in enumerate(((0, 1, ALU.subtract), (1, 0, ALU.add))):
                    done(mul(b_tmp[:, 0], wr, b_nat[:, x]))
                    done(mul(b_tmp[:, 1], wi, b_nat[:, y]))
                    done(e.tensor_tensor(b_bar[:, r], b_tmp[:, 0], b_tmp[:, 1], op))
            elif kind == "mats":
                for r in range(2):
                    if r:
                        e.wait_ge(S("bT_full"), SF)
                    for g in range(2):
                        for q in range(4):
                            rows, cols = slice(64 * g, 64 * g + 64), slice(32 * q + 16 * g, 32 * q + 16 * g + 16)
                            ins = e.tensor_copy(b_pad[rows, q::4, cols], b_bar[rows, r, q::4, :])
                            ins.then_inc(S("b_pad"), 1)
                for g in range(2 * SF):
                    r, f = g // SF, g % SF
                    e.wait_ge(S("cT_full"), g + 1)
                    for d in range(2):
                        rows = slice(64 * d, 64 * d + 64)
                        src = bank(6)[rows, 0:P].rearrange("p (q d h) -> p q d h", q=4, d=2)[:, :, d, :]
                        ins = e.tensor_scalar(c_lhs[rows, 4 * f:4 * f + 4, r, 16 * d:16 * d + 16], src, 1.0 - 2.0 * r, None, ALU.mult)
                    ins.then_inc(S("cT_out"), 1)
                e.wait_ge(S("xsT_full"), KT)
                rc, rs = rot[:, 0], rot[:, 1]
                e.tensor_copy(rc[:, :, 0], sp[:, 13])
                done(e.tensor_copy(rs[:, :, 0], sp[:, 5]))
                m = 1
                while m < BLK:
                    w03 = W03[:].rearrange("p a b -> p (a b)")
                    t0, t1 = w03[:, 0:CT_N * m].rearrange("p (c t) -> p c t", t=m), w03[:, 1024:1024 + CT_N * m].rearrange("p (c t) -> p c t", t=m)
                    ec, es = (x[:, :, m - 1:m].broadcast_to([P, CT_N, m]) for x in (rc, rs))
                    mul(t0, rc[:, :, 0:m], ec)
                    done(mul(t1, rs[:, :, 0:m], es))
                    done(sub(rc[:, :, m:2 * m], t0, t1))
                    mul(t0, rs[:, :, 0:m], ec)
                    done(mul(t1, rc[:, :, 0:m], es))
                    done(add(rs[:, :, m:2 * m], t0, t1))
                    m *= 2
            elif kind == "s5a":
                f, blk = S5_UNITS[n]
                if n >= 1:
                    s5_carry(n - 1)
                e.wait_ge(S("s5_bu"), n + 1)
                rc, rs = (rot[:, r, 4 * f:4 * f + 4, :] for r in range(2))
                w = lambda i: W03[:, i, :].rearrange("p (q t) -> p q t", q=4)
                bu = [bank(4 + r).rearrange("p (q t) -> p q t", q=4) for r in range(2)]
                mul(w(0), bu[0], rc)
                mul(w(1), bu[1], rs)
                mul(w(2), bu[1], rc)
                mul(w(3), bu[0], rs).then_inc(S("s5_in_mul"), 1)
                e.wait_ge(S("s5_in_sum"), n + 1)
                for r in range(2):
                    for q in range(4):
                        ct = 4 * f + q
                        init = carry[:, ct, r:r + 1] if blk else 0.0
                        ins = e.tensor_tensor_scan(W47[:, 2 + r, q * BLK:(q + 1) * BLK], lam3[:, 0, ct:ct + 1].broadcast_to([P, BLK]),
                                                   W47[:, r, q * BLK:(q + 1) * BLK], init, ALU.mult, ALU.add)
                ins.then_inc(S("s5_scan"), 1)
            elif kind == "s5b":
                f, blk = S5_UNITS[n]
                if n >= 1:
                    s5_out(n - 1)
                e.wait_ge(S("s5_scan"), n + 1)
                rc, rs = (rot[:, r, 4 * f:4 * f + 4, :] for r in range(2))
                w = lambda i: W03[:, i, :].rearrange("p (q t) -> p q t", q=4)
                g = [W47[:, 2 + r, :].rearrange("p (q t) -> p q t", q=4) for r in range(2)]
                mul(w(0), g[0], rc)
                mul(w(1), g[1], rs)
                mul(w(2), g[1], rc)
                mul(w(3), g[0], rs).then_inc(S("s5_out_mul"), 1)
            elif kind == "att":
                h, i = ATT[n]
                nk = (i + 1) * P
                e.wait_ge(S("alibi_in"), 32)
                e.wait_ge(S("att_s"), n + 1)
                o = 2 * (n % 2)
                for c in range(2):
                    ins = e.tensor_tensor_reduce(out=a_s[:, n % 2, c, 0:nk], in0=bank(c)[:, 0:nk],
                                                 in1=alibi[:, h, ALIBI_W - nk:ALIBI_W], scale=1.0, scalar=NEG,
                                                 op0=ALU.add, op1=ALU.max, accum_out=small[:, MX + o + c:MX + o + c + 1])
                ins.then_inc(S("att_biased"), 1)
                e.wait_ge(S("att_biased"), n + 1)
                e.tensor_scalar(small[:, NM + o:NM + o + 2], small[:, MX + o:MX + o + 2], -1.0, None, ALU.mult).then_inc(S("att_max"), 1)
                if n >= 1:
                    att_tail(n - 1)
            elif kind == "att_end":
                att_tail(15)
            elif kind == "s5_end":
                s5_carry(15)
                s5_out(15)
            elif kind == "s5d":
                e.wait_ge(S("s5d_bu"), 1)
                e.wait_ge(S("s5_h"), 16)
                lb = [lam3[:, 1 + r].unsqueeze(2).broadcast_to([P, CT_N, DB]) for r in range(2)]
                w = lambda i: W03[:, i, 0:P].rearrange("p (c b) -> p c b", b=DB)
                for t in range(DT):
                    if t == 0:
                        prev = [st[:, r, :].rearrange("p (b c) -> p c b", b=DB) for r in range(2)]
                    else:
                        prev = [H_dec[:, :, r, :].rearrange("p c (b t) -> p c b t", t=DT)[:, :, :, t - 1] for r in range(2)]
                    bu = [bank(4 + r).rearrange("p (c b t) -> p c b t", b=DB, t=DT)[:, :, :, t] for r in range(2)]
                    new = [H_dec[:, :, r, :].rearrange("p c (b t) -> p c b t", t=DT)[:, :, :, t] for r in range(2)]
                    mul(w(0), lb[0], prev[0])
                    mul(w(1), lb[1], prev[1])
                    mul(w(2), lb[0], prev[1])
                    done(mul(w(3), lb[1], prev[0]))
                    sub(w(0), w(0), w(1))
                    done(add(w(2), w(2), w(3)))
                    add(new[0], w(0), bu[0])
                    done(add(new[1], w(2), bu[1]))
                for r in range(2):
                    ins = e.tensor_copy(st[:, r, :].rearrange("p (b c) -> p c b", b=DB),
                                        H_dec[:, :, r, :].rearrange("p c (b t) -> p c b t", t=DT)[:, :, :, DT - 1])
                ins.then_inc(S("s5d_h"), 1)
                e.wait_ge(S("s5d_y"), 1)
                for f in range(SF):
                    ins = e.scalar_tensor_tensor(out=uT[:, f, NP_TOK:TOK], in0=uT[:, f, NP_TOK:TOK], scalar=par[:, SSM_D + f:SSM_D + f + 1],
                                                 in1=bank(6)[:, f * NS_TOK:(f + 1) * NS_TOK], op0=ALU.mult, op1=ALU.add)
                ins.then_inc(S("yssm"), 1)
            elif kind == "gelu":
                for f in range(SF):
                    e.wait_ge(S("y1_hi"), f + 1)
                    sub(y1_lo[:, f, :], uT[:, f, :], y1_hi[:, f, :].bitcast(F32)).then_inc(S("y1_lo"), 1)
                e.wait_ge(S("att_pT"), 16)
                done(e.memset(d_qz[:], 0.0))
                for h in range(NH):
                    for c in range(2):
                        rows = slice(64 * c, 64 * c + 64)
                        ins = e.tensor_copy(d_qz[rows, :, h, c * 16 + h * 4:c * 16 + h * 4 + 4],
                                            qT[rows, h, NP_TOK:TOK].rearrange("p (b t) -> p b t", t=DT))
                        ins.then_inc(S("dqz"), 1)
            elif kind == "dsoft":
                for t in range(2):
                    e.wait_ge(S("ds_done"), 4 * (t + 1))
                    done(e.tensor_tensor_reduce(out=d_p[:, t, :], in0=bank(4 + t)[:, 0:DEC_W], in1=decb[:, t, :], scale=1.0,
                                                scalar=NEG, op0=ALU.add, op1=ALU.max, accum_out=small[:, MX + t:MX + t + 1]))
                    e.tensor_scalar(small[:, NM + t:NM + t + 1], small[:, MX + t:MX + t + 1], -1.0, None, ALU.mult).then_inc(S("ds_max"), 1)
                e.memset(d_pT[:], 0.0)
                done(e.memset(d_pTn[:], 0.0))
                for t in range(2):
                    e.wait_ge(S("ds_exp"), t + 1)
                    done(e.reciprocal(small[:, R + t:R + t + 1], small[:, L + t:L + t + 1]))
                    done(mul(small[:, R + t:R + t + 1], small[:, R + t:R + t + 1], small[:, 44:45]))
                    e.tensor_scalar(d_p[:, t, :], d_p[:, t, :], small[:, R + t:R + t + 1], None, ALU.mult).then_inc(S("dp"), 1)
                for t in range(2):
                    e.wait_ge(S("dpT_full"), t + 1)
                    past = bank(6 + t)[:, 0:PAST].rearrange("p (g b c r) -> p g b c r", g=PAGES, b=4, c=2)
                    new = bank(6 + t)[0:NS_TOK, PAST:PAST + P].rearrange("p (b c r) -> p b c r", b=4, c=2)
                    dst, dstn = d_pT[:, :, 4 * t:4 * t + 4, 0:16], d_pTn[:, 4 * t:4 * t + 4, 0:16]
                    e.tensor_copy(dst, past[:, :, :, 0, :])
                    done(e.tensor_copy(dstn, new[:, :, 0, :]))
                    add(dst, dst, past[:, :, :, 1, :])
                    add(dstn, dstn, new[:, :, 1, :]).then_inc(S("dpT"), 1)
            elif kind == "dout":
                for t in range(2):
                    e.wait_ge(S("doT_full"), t + 1)
                    for h in range(NH):
                        src = bank(6 + t)[:, h * P:(h + 1) * P].rearrange("p (b r) -> p b r", b=4)[:, :, 4 * h:4 * h + 4]
                        ins = e.tensor_copy(oT[:, h, NP_TOK + 16 * t:NP_TOK + 16 * t + 16].rearrange("p (b q) -> p b q", b=4), src)
                    ins.then_inc(S("dT_out"), 1)
            elif kind == "subln":
                for h in range(NH):
                    e.wait_ge(S("subln_sum"), h + 1)
                    if h:
                        e.wait_ge(S("subln_t"), h)
                    e.tensor_scalar(two(rstd[:]), halves(4), 1.0 / P, EPS, ALU.mult, ALU.add).then_inc(S("subln_ms"), 1)
                    e.wait_ge(S("subln_root"), h + 1)
                    done(e.reciprocal(rstd[:], rstd[:]))
                    mul(tt[:, h % 2, :], oT[:, h, :], rstd[:]).then_inc(S("subln_t"), 1)
                    e.wait_ge(S("subln_hi"), h + 1)
                    e.scalar_tensor_tensor(out=att_lo[:, h, :], in0=tt[:, h % 2, :], scalar=small[:, 27:28],
                                           in1=att_hi[:, h, :].bitcast(F32), op0=ALU.mult, op1=ALU.subtract).then_inc(S("subln_lo"), 1)
            elif kind == "glu":
                for m in range(SF):
                    e.wait_ge(acc_out, J_GLU + m + 1)
                    mul(uT[:, m, :], uT[:, m, :], tt[:, m % 2, :]).then_inc(S("y2"), 1)
                sum_squares("ssmn", SF)
                make_rstd("ssmn", SF * P)
                split_scaled("ssmn", uT, ssm_lo, ssm_hi, SF, lambda k: par[:, G_SSM + k:G_SSM + k + 1])
            elif kind == "mem_in":
                e.wait_ge(S("m_ss"), 2)
                e.tensor_scalar(small[:, 8:10], small[:, 0:2], 1.0 / D, EPS, ALU.mult, ALU.add).then_inc(S("m_ms"), 1)
                e.wait_ge(S("m_root"), 1)
                e.reciprocal(small[:, 16:18], small[:, 8:10]).then_inc(S("m_rstd"), 1)
                for k in range(KT):
                    e.wait_ge(S("mn_hi"), k + 1)
                    e.scalar_tensor_tensor(out=mn_lo[:, k, :], in0=bank(6 + k % 2)[:, 0:NMEM], scalar=par[:, G_MEM_KV + k:G_MEM_KV + k + 1],
                                           in1=mn_hi[:, k, :].bitcast(F32), op0=ALU.mult, op1=ALU.subtract).then_inc(S("mn_lo"), 1)

        sum_squares("n1", KT)
        make_rstd("n1", D)
        residual("n1", z, G_MIX_POST)
        sum_squares("n2", KT)
        make_rstd("n2", D)
        split_scaled("n2", yT, x_lo, x_hi, KT, lambda k: par[:, G_MEM_PRE + k:G_MEM_PRE + k + 1])
        e.memset(dm_qz[:], 0.0)
        e.wait_ge(acc_out, J_MO)
        done(e.tensor_copy(small[:, 50:51], small[:, 44:45]))
        for k in range(KT):
            h = k // 2
            e.tensor_copy(dm_qz[:, :, k, 4 * h:4 * h + 4], qm[:, k, NP_TOK:TOK].rearrange("p (b t) -> p b t", t=DT)).then_inc(S("dmqz"), 1)

        def ma_tail(n):
            h, i = MATT[n]
            o = n % 2
            e.wait_ge(S("ma_exp"), n + 1)
            done(e.reciprocal(small[:, R + o:R + o + 1], small[:, L + o:L + o + 1]))
            e.tensor_scalar(m_p[:, o, :], m_p[:, o, :], small[:, R + o:R + o + 1], None, ALU.mult).then_inc(S("ma_p"), 1)

        def ma_out(h):
            for d in range(2):
                e.wait_ge(S("ma_pv"), 2 * h + d + 1)
                done(e.tensor_copy(x_hi[:, 2 * h + d, 0:NP_TOK], bank(d)))
                sub(x_lo[:, 2 * h + d, 0:NP_TOK], bank(d), x_hi[:, 2 * h + d, 0:NP_TOK].bitcast(F32)).then_inc(S("ma_o"), 1)

        for n, (h, i) in enumerate(MATT):
            o = n % 2
            e.wait_ge(S("ma_s"), n + 1)
            done(e.reduce_max(small[:, MX + o:MX + o + 1], bank(4 + o)[:, 0:NMEM], AX_X))
            e.tensor_scalar(small[:, NM + o:NM + o + 1], small[:, MX + o:MX + o + 1], -MD ** -0.5, None, ALU.mult).then_inc(S("ma_max"), 1)
            if n >= 1:
                ma_tail(n - 1)
            if i == 1 and h >= 1:
                ma_out(h - 1)
        ma_tail(15)
        ma_out(3)
        for t in range(2):
            e.wait_ge(S("dms"), 4 * (t + 1))
            done(e.reduce_max(small[:, MX + t:MX + t + 1], bank(4 + t)[:, 0:NMEM], AX_X))
            e.tensor_scalar(small[:, NM + t:NM + t + 1], small[:, MX + t:MX + t + 1], -MD ** -0.5, None, ALU.mult).then_inc(S("dm_max"), 1)
        for t in range(2):
            e.wait_ge(S("dm_exp"), t + 1)
            done(e.reciprocal(small[:, R + t:R + t + 1], small[:, L + t:L + t + 1]))
            e.tensor_scalar(dm_p[:, t, :], dm_p[:, t, :], small[:, R + t:R + t + 1], None, ALU.mult).then_inc(S("dm_pr"), 1)
        for t in range(2):
            e.wait_ge(S("dm_pTf"), t + 1)
            e.tensor_copy(dm_pT[:, :, t, :], bank(6 + t)[:, 0:NMEM].rearrange("p (a b) -> p a b", a=2)).then_inc(S("dm_pTo"), 1)
        for t in range(2):
            e.wait_ge(S("dmoT"), t + 1)
            for h in range(MH):
                src = pall[:, 2 * t:2 * t + 2, :].rearrange("p a b -> p (a b)")[:, 2 * h * P:(2 * h + 2) * P]\
                    .rearrange("p (d b r) -> p d b r", d=2, b=4)[:, :, :, 4 * h:4 * h + 4]
                cols = slice(NP_TOK + 16 * t, NP_TOK + 16 * t + 16)
                hi = x_hi[:, 2 * h:2 * h + 2, cols].rearrange("p d (b q) -> p d b q", b=4)
                lo = x_lo[:, 2 * h:2 * h + 2, cols].rearrange("p d (b q) -> p d b q", b=4)
                done(e.tensor_copy(hi, src))
                sub(lo, src, hi.bitcast(F32)).then_inc(S("dmx"), 1)
        sum_squares("n3", KT)
        make_rstd("n3", D)
        residual("n3", z, G_MEM_POST)
        sum_squares("n4", KT)
        make_rstd("n4", D)
        split_scaled("n4", yT, x_lo, x_hi, KT, lambda k: par[:, G_FFN_PRE + k:G_FFN_PRE + k + 1])
        with e.Fori(0, PAIRS) as i:
            for m in range(2):
                e.wait_ge(acc_full, i * 4 + (J_FFN + 2 + m + 1))
                e.wait_ge(acc_out, i * 4 + (J_FFN + 2 + m))
                e.wait_ge(parts_lo, i * 2 + (LO_FFN))
                mul(two(sq[:, m, :]), acc(m), two(tt[:, m, :])).then_inc(acc_out, 1)
            for m in range(2):
                e.wait_ge(S("g_hi_ready"), i * 2 + (m + 1))
                sub(g_lo[:, bass.ds(i * 2 + m, 1), :], sq[:, m:m + 1, :], g_hi[:, bass.ds(i * 2 + m, 1), :].bitcast(F32))\
                    .then_inc(parts_lo, 1)
        sum_squares("n5", KT)
        make_rstd("n5", D)
        residual("n5", z_ffn, G_FFN_POST)

    @block.tensor
    def _(pe):
        e = pe
        mm = e.matmul

        def transposes_to(e_, dst, src, n, w, idt):
            for h in range(NH):
                ins = e_.transpose(dst[0:w, h * P:(h + 1) * P], src[:, h, n * P:n * P + w], idt[:])
            return ins

        def product(j, w_slot, cols, col, x_h, x_l, k_x, kts, first=True, last=True, k_off=0):
            if first and j >= 2:
                e.wait_ge(acc_out, j - 1)
            for k in range(kts):
                wcol = slice((k_off + k) * cols + col, (k_off + k) * cols + col + P)
                wh, wl = w_hi[:, w_slot, wcol], w_lo[:, w_slot, wcol]
                for w, x, s_, t_ in ((wh, x_h, True, False), (wh, x_l, False, False), (wl, x_h, False, True)):
                    for a in range(2):
                        ins = mm(acc(j)[:, a, :], w, x[:, k_x + k, a * HALF:(a + 1) * HALF],
                                 start=first and k == 0 and s_, stop=last and k == kts - 1 and t_)
            return ins

        def unit(n, j, kts, cols, x_h, x_l, k_x=0, first=True, last=True):
            e.wait_ge(w_lo_ready, n + 1)
            for m in range(cols // P):
                product(j + m, n % 2, cols, m * P, x_h, x_l, k_x, kts, first, last).then_inc(acc_full, 1)

        def spread_sum(name):
            for a in range(2):
                ins = mm(halves(6)[:, a, :], ones[:], sqacc[:, a * HALF:(a + 1) * HALF], start=True, stop=True)
            ins.then_inc(S("norm_sum"), 1)

        def transposes(dst, srcs, rows=P):
            at_ = 0
            for src in srcs:
                w = src.shape[0]
                ins = e.transpose(dst[0:src.shape[1], at_:at_ + w], src, ident[0:w, 0:w])
                at_ += w
            return ins

        e.wait_ge(consts_in, 32)
        e.wait_ge(rows_in, 16 * N_ROW_LOADS)
        transposes(bank(0), [p_rows[:]]).then_inc(S("par_full"), 1)
        for k in range(KT):
            if k == 0:
                e.wait_ge(S("xs_ready"), 5)
            if k >= 2:
                e.wait_ge(S("xs_lo"), k - 1)
            for t in range(5):
                rows = P if t < 4 else NS_TOK
                ins = e.transpose(banks(4 + 2 * (k % 2))[:, t * P:t * P + rows], xs[0:rows, t, k * P:(k + 1) * P], ident[0:rows, 0:rows])
            ins.then_inc(S("xsT_full"), 1)

        def s5_y(n):
            f, _ = S5_UNITS[n]
            e.wait_ge(S("s5_h"), n + 1)
            if n >= 1:
                e.wait_ge(S("yssm"), n)
            for q in range(4):
                for r in range(2):
                    ins = mm(bank(6)[32 * q:32 * q + 32, 0:BLK], c_lhs[:, 4 * f + q, r, :], W47[:, r, q * BLK:(q + 1) * BLK],
                             start=r == 0, stop=r == 1)
            ins.then_inc(S("s5_y"), 1)

        def att_tail(n):
            h, i = ATT[n]
            e.wait_ge(S("att_p"), n + 1)
            if n >= 1:
                e.wait_ge(S("att_pTo"), n)
            transposes(bank(2), [a_p[:, n % 2, k * P:(k + 1) * P] for k in range(i + 1)]).then_inc(S("att_pT"), 1)
            if i == 3:
                e.wait_ge(S("att_pTo"), n + 1)
                if h:
                    e.wait_ge(S("att_oT"), h)
                for k in range(4):
                    ins = mm(bank(3)[:, k * P:512], v_tok[:, k, h * P:(h + 1) * P], a_pT[:, k, k * P:512], start=k == 0, stop=k == 3)
                ins.then_inc(S("att_pv"), 1)

        for kind, n in order:
            if kind == "main":
                if n == 0:
                    e.wait_ge(S("xs_lo"), KT)
                unit(n, J_W_IN + 2 * n, KT, 256, x_hi, x_lo)
            elif kind == "par":
                e.wait_ge(S("dt_rows"), 1)
                transposes(bank(4), [dt_rows[:].rearrange("p a b -> p (a b)")]).then_inc(S("dtT"), 1)
                transposes(bank(5), [st_nat[:, r, :] for r in range(2)]).then_inc(S("stT"), 1)
            elif kind == "mats":
                e.wait_ge(S("par_ready"), 1)
                for g in range(2 * SF):
                    r, f = g // SF, g % SF
                    e.wait_ge(S("b_pad"), 8 * (r + 1))
                    if g >= 1:
                        e.wait_ge(S("bT_out"), g)
                    transposes(bank(7), [b_pad[:, 4 * f + q, :] for q in range(4)]).then_inc(S("bT_full"), 1)
                for g in range(2 * SF):
                    r, f = g // SF, g % SF
                    if g >= 1:
                        e.wait_ge(S("cT_out"), g)
                    transposes(bank(6), [c_nat[:, r, f].rearrange("p a b -> p (a b)")]).then_inc(S("cT_full"), 1)
            elif kind == "xT":
                e.wait_ge(S("cT_out"), 2 * SF)
                e.wait_ge(S("bT_out"), 2 * SF)
                for k in range(KT):
                    if k >= 1:
                        e.wait_ge(S("xT_out"), k)
                    for t in range(5):
                        rows = P if t < 4 else NS_TOK
                        ins = e.transpose(banks(6)[:, t * P:t * P + rows], x_nat[0:rows, t, k * P:(k + 1) * P], ident[0:rows, 0:rows])
                    ins.then_inc(S("xT_full"), 1)
                e.wait_ge(S("xT_out"), KT)
            elif kind == "s5a":
                f, blk = S5_UNITS[n]
                e.wait_ge(acc_out, 4)
                e.wait_ge(S("st_ready"), 1)
                e.wait_ge(S("bT_out"), 2 * SF)
                if n >= 1:
                    e.wait_ge(S("s5_in_mul"), n)
                for r in range(2):
                    for q in range(4):
                        ins = mm(bank(4 + r)[:, q * BLK:(q + 1) * BLK], b_lhs[:, 4 * f + q, r, :], uT[:, f, blk * BLK:(blk + 1) * BLK],
                                 start=True, stop=True)
                ins.then_inc(S("s5_bu"), 1)
                if n >= 1:
                    s5_y(n - 1)
            elif kind == "vtr":
                e.wait_ge(acc_out, 16)
                e.wait_ge(S("v_tok_ready"), n) if n else None
                e.wait_ge(S("k_tok_ready"), n) if n else None
                w = P if n < 4 else NS_TOK
                transposes_to(e, bank(7), vT, n, w, ident).then_inc(S("vtr_full"), 1)
            elif kind == "ktr":
                e.wait_ge(S("v_tok_ready"), n + 1)
                w = P if n < 4 else NS_TOK
                transposes_to(e, bank(7), kT, n, w, ident).then_inc(S("ktr_full"), 1)
            elif kind == "att":
                h, i = ATT[n]
                nk = (i + 1) * P
                if n >= 1:
                    e.wait_ge(S("att_biased"), n)
                for c in range(2):
                    rows = slice(64 * c, 64 * c + 64)
                    ins = mm(bank(c)[:, 0:nk], qT[rows, h, i * P:(i + 1) * P], kT[rows, h, 0:nk], start=True, stop=True)
                ins.then_inc(S("att_s"), 1)
                if n >= 1:
                    att_tail(n - 1)
            elif kind == "att_end":
                att_tail(15)
            elif kind == "s5_end":
                s5_y(15)
                e.wait_ge(S("s5_carry"), 16)
                transposes(bank(7)[:, 0:P], [carry[:, :, 0]])
                transposes(bank(7)[:, P:2 * P], [carry[:, :, 1]]).then_inc(S("fin_full"), 1)
            elif kind == "s5d":
                e.wait_ge(S("s5_in_mul"), 16)
                for r in range(2):
                    for ct in range(CT_N):
                        ins = mm(bank(4 + r)[:, ct * NS_TOK:(ct + 1) * NS_TOK], b_lhs[:, ct, r, :], uT[:, ct // 4, NP_TOK:TOK],
                                 start=True, stop=True)
                ins.then_inc(S("s5d_bu"), 1)
                e.wait_ge(S("s5d_h"), 1)
                e.wait_ge(S("yssm"), 16)
                for ct in range(CT_N):
                    f, q = ct // 4, ct % 4
                    for r in range(2):
                        ins = mm(bank(6)[32 * q:32 * q + 32, f * NS_TOK:(f + 1) * NS_TOK], c_lhs[:, ct, r, :], H_dec[:, ct, r, :],
                                 start=r == 0, stop=r == 1)
                ins.then_inc(S("s5d_y"), 1)
                e.wait_ge(S("fin_ready"), 1)
                transposes(bank(7), [st[:, r, :] for r in range(2)]).then_inc(S("fin_full"), 1)
            elif kind == "dk":
                e.wait_ge(S("yssm"), 17)
                e.wait_ge(S("fin_ready"), 2)
                e.wait_ge(S(f"dk_in{n % 2}"), 32 * (n // 2 + 1))
                for g in range(2):
                    if n >= 1:
                        e.wait_ge(S("dkT_done"), 2 * (n - 1) + g + 1)
                    transposes(bank(6 + g), [d_k[:, n % 2, pg, (2 * g + h) * P:(2 * g + h + 1) * P] for h in range(2) for pg in range(PAGES)])\
                        .then_inc(S("dkT_full"), 1)
                rows = slice(32 * (n % 4), 32 * (n % 4) + 32)
                e.wait_ge(S("dkT_done"), 2 * n + 2)
                e.wait_ge(S("dqz"), 8)
                for h in range(NH):
                    mm(bank(4 + n // 4)[rows, 0:PAST], d_qz[:, n, h, :], d_kT[:, h, :], start=h == 0, stop=h == NH - 1)
                for h in range(NH):
                    ins = mm(bank(4 + n // 4)[rows, PAST:DEC_W], d_qz[:, n, h, :], kT[:, h, NP_TOK:TOK], start=h == 0, stop=h == NH - 1)
                ins.then_inc(S("ds_done"), 1)
            elif kind == "dsoft":
                for t in range(2):
                    e.wait_ge(S("dp"), t + 1)
                    transposes(bank(6 + t), [d_p[:, t, 0:P], d_p[:, t, P:2 * P], d_p[:, t, PAST:DEC_W]]).then_inc(S("dpT_full"), 1)
            elif kind == "dv":
                e.wait_ge(S("dpT"), 2)
                e.wait_ge(S(f"dv_in{n % 2}"), 32 * (n // 2 + 1))
                out = bank(4 + n // 4)[32 * (n % 4):32 * (n % 4) + 32, :]
                for pg in range(PAGES):
                    mm(out, d_pT[:, pg, n, :], d_v[:, n % 2, pg, :], start=pg == 0, stop=False)
                mm(out, d_pTn[:, n, :], v_new[:], start=False, stop=True).then_inc(S("dv_done"), 1)
            elif kind == "dout":
                for t in range(2):
                    e.wait_ge(S("do_out"), t + 1)
                    transposes(bank(6 + t), [d_o[:, t, h * P:(h + 1) * P] for h in range(NH)]).then_inc(S("doT_full"), 1)
            elif kind == "subln":
                e.wait_ge(S("do_out"), 2)
                for h in range(NH):
                    e.wait_ge(S("subln_sq"), h + 1)
                    if h:
                        e.wait_ge(S("subln_ms"), h)
                    for a in range(2):
                        ins = mm(halves(4)[:, a, :], ones[:], sq[:, h % 2, a * HALF:(a + 1) * HALF], start=True, stop=True)
                    ins.then_inc(S("subln_sum"), 1)
            elif kind == "glu":
                e.wait_ge(S("y1_lo"), SF)
                e.wait_ge(S("att_oT"), NH)
                unit(U_GLU, J_GLU, SF, 512, y1_hi, y1_lo)
                e.wait_ge(S("dT_out"), 2)
                e.wait_ge(*counted("ssmn", "add", SF - 1))
                spread_sum("ssmn")
            elif kind == "mem_in":
                e.wait_ge(*counted("ssmn", "ms", 1))
                e.wait_ge(S("ms_ready"), 2)
                for k in range(KT):
                    if k >= 2:
                        e.wait_ge(S("mn_lo"), k - 1)
                    transposes(bank(6 + k % 2), [mem_nat[:, t, k * P:(k + 1) * P] for t in range(2)]).then_inc(S("mT_full"), 1)
            elif kind == "out":
                e.wait_ge(S("subln_lo"), NH)
                e.wait_ge(*counted("ssmn", "lo", SF))
                for u in range(4):
                    n = U_OUT + u
                    e.wait_ge(w_lo_ready, n + 1)
                    for m in range(2):
                        j = J_OUT + 2 * u + m
                        product(j, n % 2, 256, m * P, att_hi, att_lo, 0, 4, True, False)
                        product(j, n % 2, 256, m * P, ssm_hi, ssm_lo, 0, 4, False, True, k_off=4).then_inc(acc_full, 1)

        def mk_unit(u):
            n = U_MK + u
            e.wait_ge(w_lo_ready, n + 1)
            for m in range(2):
                j = J_MK + 2 * u + m
                e.wait_ge(acc_out, j - 1)
                out = bank(2 * (j % 2))[:, 0:256]
                for k in range(KT):
                    if u < 4:
                        wc, xc = slice(k * 256 + m * P, k * 256 + (m + 1) * P), slice(0, NMEM)
                        terms = [(w[:, n % 2, wc], x[:, k, xc]) for w, x in ((w_hi, mn_hi), (w_hi, mn_lo), (w_lo, mn_hi))]
                    else:
                        wc, xc = slice(k * 256, (k + 1) * 256), slice(m * P, (m + 1) * P)
                        terms = [(x[:, k, xc], w[:, n % 2, wc]) for x, w in ((mn_hi, w_hi), (mn_hi, w_lo), (mn_lo, w_hi))]
                    for i, (l, r) in enumerate(terms):
                        ins = mm(out, l, r, start=k == 0 and i == 0, stop=k == KT - 1 and i == 2)
                ins.then_inc(acc_full, 1)

        e.wait_ge(S("mn_lo"), KT)
        mk_unit(0)
        e.wait_ge(*counted("n1", "add", KT - 1))
        spread_sum("n1")
        mk_unit(1)
        mk_unit(2)
        e.wait_ge(*counted("n2", "add", KT - 1))
        e.wait_ge(*counted("n1", "ms", 1))
        spread_sum("n2")
        for u in range(3, 8):
            mk_unit(u)
        for g in range(4):
            t, k0 = g // 2, 4 * (g % 2)
            e.wait_ge(acc_out, J_MQ)
            if g >= 2:
                e.wait_ge(S("mk_tok_ready"), g - 1)
            else:
                e.wait_ge(*counted("n2", "ms", 1))
            transposes(bank(6 + g % 2), [mkT[:, k0 + k, t * P:(t + 1) * P] for k in range(4)]).then_inc(S("mkt_full"), 1)
        e.wait_ge(*counted("n2", "lo", KT))
        for u in range(4):
            unit(U_MQ + u, J_MQ + 2 * u, KT, 256, x_hi, x_lo)

        def ma_tail(n):
            h, i = MATT[n]
            e.wait_ge(S("ma_p"), n + 1)
            if n >= 1:
                e.wait_ge(S("ma_pTo"), n)
            transposes(bank(6), [m_p[:, n % 2, k * P:(k + 1) * P] for k in range(2)]).then_inc(S("ma_pT"), 1)
            if i == 3:
                e.wait_ge(S("ma_pTo"), n + 1)
                for d in range(2):
                    if h:
                        e.wait_ge(S("ma_o"), 2 * (h - 1) + d + 1)
                    for k in range(2):
                        c = (2 * h + d) * P
                        ins = mm(bank(d), mv_tok[:, k, c:c + P], m_pT[:, k, :], start=k == 0, stop=k == 1)
                    ins.then_inc(S("ma_pv"), 1)

        e.wait_ge(acc_out, J_MO)
        e.wait_ge(S("mk_tok_ready"), 4)
        for n, (h, i) in enumerate(MATT):
            if n >= 2:
                e.wait_ge(S("ma_exp"), n - 1)
            for d in range(2):
                ins = mm(bank(4 + n % 2)[:, 0:NMEM], qm[:, 2 * h + d, i * P:(i + 1) * P], mkT[:, 2 * h + d, :], start=d == 0, stop=d == 1)
            ins.then_inc(S("ma_s"), 1)
            if n >= 1:
                ma_tail(n - 1)
        ma_tail(15)
        e.wait_ge(S("dmqz"), KT)
        e.wait_ge(S("ma_pTo"), 16)
        e.wait_ge(S("ma_exp"), 16)
        for b in range(DB):
            e.wait_ge(S(f"kv_in{b % KV_N}"), 16 * (b // KV_N + 1))
            for g in range(4):
                if b or g >= 2:
                    e.wait_ge(S("dmT_out"), 4 * b + g - 1)
                transposes(bank(6 + g % 2), [dm_kv[:, b % KV_N, t, (2 * g + k) * P:(2 * g + k + 1) * P] for k in range(2) for t in range(2)])\
                    .then_inc(S("dmT_pe"), 1)
            rows = slice(32 * (b % 4), 32 * (b % 4) + 32)
            e.wait_ge(S("dmT_out"), 4 * b + 4)
            for k in range(KT):
                ins = mm(bank(4 + b // 4)[rows, 0:NMEM], dm_qz[:, b, k, :], dm_kT[:, k, :], start=k == 0, stop=k == KT - 1)
            ins.then_inc(S("dms"), 1)
        for t in range(2):
            e.wait_ge(S("dm_pr"), t + 1)
            transposes(bank(6 + t), [dm_p[:, t, k * P:(k + 1) * P] for k in range(2)]).then_inc(S("dm_pTf"), 1)
        e.wait_ge(S("dm_pTo"), 2)
        for b in range(DB):
            t, rows = b // 4, slice(32 * (b % 4), 32 * (b % 4) + 32)
            i = DB + b
            e.wait_ge(S(f"kv_in{i % KV_N}"), 16 * (i // KV_N + 1))
            for g in range(2):
                for k in range(2):
                    ins = mm(bank(4 + 2 * t + g)[rows, :], dm_pT[:, k, t, rows], dm_kv[:, i % KV_N, k, g * 512:(g + 1) * 512],
                             start=k == 0, stop=k == 1)
            ins.then_inc(S("dm_pv"), 1)
        for t in range(2):
            e.wait_ge(S("dmo_out"), 2 * t + 2)
            e.wait_ge(S("ma_o"), 8)
            flat = pall[:, 2 * t:2 * t + 2, :].rearrange("p a b -> p (a b)")
            transposes(flat, [dm_o[:, t, k * P:(k + 1) * P] for k in range(KT)]).then_inc(S("dmoT"), 1)
        e.wait_ge(S("dmx"), 8)
        e.wait_ge(S("ma_o"), 8)
        for u in range(4):
            unit(U_MO + u, J_MO + 2 * u, KT, 256, x_hi, x_lo)
        for name in ("n3", "n4"):
            if name == "n3":
                e.wait_ge(S("dmo_out"), 4)
            else:
                e.wait_ge(*counted("n3", "ms", 1))
            e.wait_ge(*counted(name, "add", KT - 1))
            spread_sum(name)
        e.wait_ge(*counted("n4", "lo", KT))
        with e.Fori(0, PAIRS) as i:
            for s_ in range(2):
                slot = (U_FFN + s_) % 2
                e.wait_ge(w_lo_ready, i * 2 + (U_FFN + s_ + 1))
                for m in range(2):
                    j = 2 * s_ + m
                    e.wait_ge(acc_out, i * 4 + (J_FFN + j - 1))
                    product(m, slot, 256, m * P, x_hi, x_lo, 0, KT).then_inc(acc_full, 1)
        for n in range(U_DOWN, N_UNITS):
            c, part = (n - U_DOWN) // 3, (n - U_DOWN) % 3
            k0, kts = DOWN_K[part]
            if n == U_DOWN:
                e.wait_ge(parts_lo, LO_FFN + FT)
            unit(n, J_DOWN + 2 * c, kts, 256, g_hi, g_lo, k0, part == 0, part == 2)
        e.wait_ge(*counted("n5", "add", KT - 1))
        spread_sum("n5")
        e.wait_ge(*counted("n5", "y", KT))
        for t in range(5):
            w = P if t < 4 else NS_TOK
            for g in range(4):
                if t:
                    e.wait_ge(S("y_out_ready"), 4 * (t - 1) + g + 1)
                for k in range(2):
                    ins = e.transpose(bank(4 + g)[0:w, k * P:(k + 1) * P], yT[:, 2 * g + k, t * P:t * P + w], ident[:])
                ins.then_inc(S("yt_full"), 1)

    ctx.close()


_OUTS = [("y_prompt", (1, NP_TOK, D)), ("y_sample", (DB, DT, D)),
         ("new_k_prompt", (1, 1, NP_TOK, NH, 2 * HD)), ("new_v_prompt", (1, 1, NP_TOK, NH, 2 * HD)),
         ("new_k_sample", (1, DB, DT, NH, 2 * HD)), ("new_v_sample", (1, DB, DT, NH, 2 * HD)),
         ("ssm_re_prompt", (1, 1, NG, SP_)), ("ssm_im_prompt", (1, 1, NG, SP_)),
         ("ssm_re_sample", (1, DB, NG, SP_)), ("ssm_im_sample", (1, DB, NG, SP_)),
         ("mem_k_prompt", (1, 1, NMEM, MH, MD)), ("mem_v_prompt", (1, 1, NMEM, MH, MD))]


def kernel(**inputs):
    import concourse.bacc as _bacc
    from concourse.bass_utils import run_bass_kernel_spmd as _run

    nc = _bacc.Bacc("TRN2", target_bir_lowering=False, num_devices=1)
    arrays, A = {}, {}
    for name, a in list(inputs.items()) + list(shape_tables().items()):
        a = np.ascontiguousarray(a)
        arrays[f"in_{name}"] = a
        A[name] = nc.dram_tensor(f"in_{name}", a.shape, mybir.dt.from_np(a.dtype), kind="ExternalInput").ap()
    O = {name: nc.dram_tensor(f"out_{name}", shape, F32, kind="ExternalOutput").ap() for name, shape in _OUTS}
    build(nc, A, O)
    r = _run(nc, [arrays], core_ids=[0])
    return tuple(r.results[0][f"out_{name}"] for name, _ in _OUTS)
```

```python
import math
import numpy as np
import concourse.bass as bass
from concourse import mybir
from concourse.alu_op_type import AluOpType as ALU
from contextlib import ExitStack

F32 = mybir.dt.float32
F32R = mybir.dt.float32r
I32 = mybir.dt.int32
ACT = mybir.ActivationFunctionType
AX_X = mybir.AxisListType.X

P = 128
D = 1024
KT = D // P
NP_TOK = 512
DB, DT = 8, 4
NS_TOK = DB * DT
TOK = NP_TOK + NS_TOK
HALF = TOK // 2
PAGES, PAGE = 2, 128
PAST = PAGES * PAGE
NH, HD = 4, 64
NMEM, MH, MD = 256, 4, 256
NG, GH, SP_ = 32, 16, 64
CT_N = NG * SP_ // P
SF = NG * GH // P
BLK = 128
DFF = 2816
FT = DFF // P
EPS = 1e-6
LAM_INIT = 0.8 - 0.6 * math.exp(-0.3 * 0)
NEG = -1e30
EPS_COL = 51
D_NM, D_L, D_R, D_MX = 52, 54, 56, 58
N_ROW_LOADS = 12
N_PAR_LOADS = 1 + 2 + 4 + 2 + 4 + 1
SLOPES = [2.0 ** (-8.0 * (h + 1) / NH) for h in range(NH)]

G_MIX_PRE, G_MIX_POST, G_MEM_PRE, G_MEM_POST, G_MEM_KV, G_FFN_PRE, G_FFN_POST = range(0, 56, 8)
G_SSM, SSM_D, G_SUB, LAM_RE, LAM_IM, N_PAR = 56, 60, 64, 65, 81, 97

ALIBI_W = NP_TOK
DEC_W = PAST + NS_TOK


def shape_tables():
    ident = np.eye(P, dtype=np.float32)
    ones = np.ones((P, P), np.float32)
    p = np.arange(P)[:, None]
    x = np.arange(ALIBI_W)[None, :]
    dist = (p + (NP_TOK - P) - x).astype(np.float32)
    alibi = np.stack([np.where(dist >= 0, -s * dist, NEG) for s in SLOPES], 1).astype(np.float32)
    dec = np.full((P, 2, DEC_W), NEG, np.float32)
    sel = np.zeros((P, 2), np.float32)
    for r in range(P):
        h, q = (r % 16) // 4, r % 4
        sel[r, (r % 32) // 16] = 1.0
        for t in range(2):
            b = 4 * t + r // 32
            dec[r, t, :PAST] = -SLOPES[h] * (PAST + q - np.arange(PAST)).astype(np.float32)
            for j in range(q + 1):
                dec[r, t, PAST + b * DT + j] = -SLOPES[h] * float(q - j)
    return {"t_ident": ident, "t_ones": ones, "t_alibi": alibi, "t_dec": dec, "t_sel": sel}


def build(nc, A, O):
    ctx = ExitStack()
    sems = {}

    def sem(name):
        if name not in sems:
            sems[name] = ctx.enter_context(nc.semaphore(name))
        return sems[name]

    S = sem

    base = [16512]

    def at(name, shape, dtype, off):
        return nc.alloc_sbuf_tensor_at(name, shape, dtype, offset=off)

    def take(nbytes):
        o = base[0]
        base[0] += (nbytes + 31) // 32 * 32
        return o

    TOKB = TOK * 4
    yT = at("yT", [P, KT, TOK], F32, take(KT * TOKB))
    W_RAW, W_HI, W_LO = take(16384), take(16384), take(16384)
    w_raw = at("w_raw", [P, 2, 2048], F32, W_RAW)
    w_hi = at("w_hi", [P, 2, 2048], F32R, W_HI)
    w_lo = at("w_lo", [P, 2, 2048], F32R, W_LO)
    d_k = at("d_k", [P, 2, PAGES, 512], F32, W_RAW)
    d_p = at("d_p", [P, 2, DEC_W], F32, W_RAW + 8192)
    d_pTn = at("d_pTn", [NS_TOK, DB, 32], F32, W_RAW + 8192 + 2304)
    d_kT = at("d_kT", [P, NH, PAST], F32, W_HI)
    d_qz = at("d_qz", [P, NH, DB, 32], F32, W_HI + 4096)
    d_pT = at("d_pT", [P, PAGES, DB, 32], F32, W_HI + 8192)
    d_o = at("d_o", [P, 2, 512], F32, W_HI + 10240)
    DV_N = 4
    d_v = at("d_v", [P, DV_N, PAGES, 512], F32, W_LO)
    ident = at("ident", [P, P], F32, take(512))
    ones = at("ones", [P, P], F32, take(512))
    TMP = take(4 * TOKB)
    sq = at("sq", [P, 2, TOK], F32, TMP)
    tt = at("tt", [P, 2, TOK], F32, TMP + 2 * TOKB)
    W03 = at("W03", [P, 4, 512], F32, TMP)
    sqacc = at("sqacc", [P, TOK], F32, take(TOKB))
    rstd = at("rstd", [P, TOK], F32, take(TOKB))
    par = at("par", [P, N_PAR], F32, take(N_PAR * 4))
    small = at("small", [P, 64], F32, take(256))
    lam3 = at("lam3", [P, 3, CT_N], F32, take(192))
    sel = at("sel", [P, 2], F32, take(32))
    carry = at("carry", [P, CT_N, 2], F32, take(128))
    B0 = take(2 * KT * TOKB)
    C0 = take(0)
    assert nc.sbuf_usable_end - C0 >= 2 * FT * TOKB, (nc.sbuf_usable_end - C0, 2 * FT * TOKB)

    x_hi = at("x_hi", [P, KT, TOK], F32R, B0)
    x_lo = at("x_lo", [P, KT, TOK], F32R, B0 + KT * TOKB)
    alibi = at("alibi", [P, NH, ALIBI_W], F32, B0)
    decb = at("decb", [P, 2, DEC_W], F32, B0 + 8192)
    a_s = at("a_s", [P, 2, 2, 512], F32, B0 + 10496)
    a_p = at("a_p", [P, 2, 512], F32, B0 + 18688)
    a_pT = at("a_pT", [P, 4, 512], F32, B0 + 22784)
    k_tok = at("k_tok", [P, 2, 512], F32, B0 + 22784)
    z_ffn = at("z_ffn", [P, KT, TOK], F32, B0)
    y_out = at("y_out", [P, 2, D], F32, B0 + KT * TOKB)

    qT = at("qT", [P, NH, TOK], F32, C0)
    kT = at("kT", [P, NH, TOK], F32, C0 + 8704)
    v_tok = at("v_tok", [P, 4, 512], F32, C0 + 17408)
    v_new = at("v_new", [NS_TOK, 512], F32, C0 + 25600)
    vT = at("vT", [P, NH, TOK], F32, C0 + 27648)
    oT = at("oT", [P, NH, TOK], F32, C0 + 27648)
    uT = at("uT", [P, SF, TOK], F32, C0 + 36352)
    rot = at("rot", [P, 2, CT_N, BLK], F32, C0 + 45056)
    b_lhs = at("b_lhs", [P, CT_N, 2, P], F32, C0 + 61440)
    c_lhs = at("c_lhs", [P, CT_N, 2, 32], F32, C0 + 77824)
    W47 = at("W47", [P, 4, 512], F32, C0 + 81920)
    b_pad = at("b_pad", [P, CT_N, P], F32, C0 + 81920)
    H_dec = at("H_dec", [P, CT_N, 2, NS_TOK], F32, C0 + 90112)
    st = at("st", [P, 2, P], F32, C0 + 94208)
    st_nat = at("st_nat", [P, 2, P], F32, C0 + 90112)
    x_nat = at("x_nat", [P, 5, D], F32, C0)
    xs = at("xs", [P, 5, D], F32, C0 + 45056)
    p_rows = at("p_rows", [N_PAR, P], F32, C0 + 20480)
    b_nat = at("b_nat", [P, 2, CT_N, GH], F32, C0 + 20992)
    c_nat = at("c_nat", [P, 2, SF, 2, SP_], F32, C0 + 23040)
    b_bar = at("b_bar", [P, 2, CT_N, GH], F32, C0 + 27136)
    b_tmp = at("b_tmp", [P, 2, CT_N, GH], F32, C0 + 29184)
    sp = at("sp", [P, 28, CT_N], F32, C0 + 31232)
    dt2 = at("dt2", [CT_N, 2], F32, C0 + 33024)
    dt_rows = at("dt_rows", [CT_N, 2, SP_], F32, C0 + 33056)
    lamv = at("lamv", [P, 4, HD], F32, C0 + 33568)
    lamp = at("lamp", [P, 2, HD], F32, C0 + 34592)
    att_hi = at("att_hi", [P, NH, TOK], F32R, C0)
    att_lo = at("att_lo", [P, NH, TOK], F32R, C0 + 8704)
    y1_hi = at("y1_hi", [P, SF, TOK], F32R, C0 + 45056)
    y1_lo = at("y1_lo", [P, SF, TOK], F32R, C0 + 53760)
    ssm_hi = at("ssm_hi", [P, SF, TOK], F32R, C0 + 45056)
    ssm_lo = at("ssm_lo", [P, SF, TOK], F32R, C0 + 53760)
    z = at("z", [P, KT, TOK], F32, C0 + 17408)
    mem_nat = at("mem_nat", [P, 2, D], F32, C0 + 81920)
    mem_sq = at("mem_sq", [P, 2, D], F32, C0 + 62464)
    mn_hi = at("mn_hi", [P, KT, NMEM], F32R, C0 + 62464)
    mn_lo = at("mn_lo", [P, KT, NMEM], F32R, C0 + 70656)
    qm = at("qm", [P, KT, TOK], F32, C0)
    m_p = at("m_p", [P, 2, NMEM], F32, C0 + 17408)
    m_pT = at("m_pT", [P, 2, 512], F32, C0 + 19456)
    dm_p = at("dm_p", [P, 2, NMEM], F32, C0 + 23552)
    dm_pT = at("dm_pT", [P, 2, 2, P], F32, C0 + 25600)
    KV_N = 3
    dm_kv = at("dm_kv", [P, KV_N, 2, D], F32, C0 + 61440)
    mkT = at("mkT", [P, KT, NMEM], F32, C0 + 45056)
    mv_tok = at("mv_tok", [P, 2, D], F32, C0 + 53248)
    mk_tok = at("mk_tok", [P, 2, D], F32, C0 + 34816)
    dm_kT = at("dm_kT", [P, KT, NMEM], F32, C0 + 34816)
    dm_o = at("dm_o", [P, 2, D], F32, C0 + 34816)
    dm_qz = at("dm_qz", [P, DB, KT, 32], F32, C0 + 86016)
    g_hi = at("g_hi", [P, FT, TOK], F32R, C0)
    g_lo = at("g_lo", [P, FT, TOK], F32R, C0 + FT * TOKB)

    pall = ctx.enter_context(nc.psum_tensor("pall", [P, 8, 512], F32))

    def bank(i):
        return pall[:, i, :]

    def banks(i):
        return pall[:, i:i + 2, :].rearrange("p a b -> p (a b)")[:, 0:TOK]

    def halves(i):
        return pall[:, i:i + 2, 0:HALF]

    def acc(j):
        return halves(2 * (j % 2) + (4 if J_GLU <= j < J_GLU + SF else 0))

    def two(ap):
        return ap.rearrange("p (a b) -> p a b", a=2)

    def view(name, k0, kts, c0, cols):
        return A[name][0, k0 * P:(k0 + kts) * P, c0:c0 + cols].rearrange("(k p) c -> p k c", p=P)

    units = []

    def add_units(name, cols_list, kts=KT, cols=256):
        first = len(units)
        for c in cols_list:
            units.append((view(name, 0, kts, c, cols), kts, cols))
        return first

    U_W_IN = add_units("w_in", [1536, 1792] + list(range(0, 1536, 256)))
    U_GLU = add_units("w_glu", [0], kts=SF, cols=512)
    U_OUT = add_units("w_out", range(0, D, 256))
    U_MK = add_units("w_mk", range(0, D, 256))
    U_MV = add_units("w_mv", range(0, D, 256))
    U_MQ = add_units("w_mq", range(0, D, 256))
    U_MO = add_units("w_mo", range(0, D, 256))
    U_FFN = len(units)
    assert U_FFN == 29
    PAIRS = DFF // 256
    U_DOWN = U_FFN + 2 * PAIRS
    DOWN_K = [(0, 8), (8, 8), (16, 6)]
    DOWN_C = D // 256
    N_UNITS = U_DOWN + DOWN_C * len(DOWN_K)

    J_W_IN = 0
    J_GLU = J_W_IN + 16
    J_OUT = J_GLU + 4
    J_MK = J_OUT + 8
    J_MV = J_MK + 8
    J_MQ = J_MV + 8
    J_MO = J_MQ + 8
    J_FFN = J_MO + 8
    J_DOWN = J_FFN + 4 * PAIRS
    assert J_FFN % 2 == 0 and J_DOWN % 2 == 0

    def used(n):
        if n <= U_OUT - 1:
            return J_W_IN + 2 * (n + 1) if n < U_GLU else J_OUT
        return J_OUT + 2 * (n - U_OUT + 1)

    NORMS = [("ssmn", SF), ("n1", KT), ("n2", KT), ("n3", KT), ("n4", KT), ("n5", KT)]
    SPLIT, RESID = ("ssmn", "n2", "n4"), ("n1", "n3", "n5")

    def counted(name, what, n):
        before = NORMS[:[x for x, _ in NORMS].index(name)]
        if what in ("sq", "add"):
            n += sum(t - (what == "add") for _, t in before)
        elif what in ("hi", "lo"):
            n += sum(t for x, t in before if x in SPLIT)
        elif what == "y":
            n += sum(t for x, t in before if x in RESID)
        else:
            n += len(before)
        return S("norm_" + what), n

    READS_RSTD = {"n2": counted("n1", "y", KT), "n3": (S("acc_out"), J_MO), "n4": counted("n3", "y", KT),
                  "n1": (S("subln_t"), NH)}

    parts_lo, LO_FFN = counted("n4", "lo", KT)

    S5_UNITS = [(f, k) for k in range(NP_TOK // BLK) for f in range(SF)]
    ATT = [(h, i) for h in range(NH) for i in range(4)]
    MATT = [(h, i) for h in range(MH) for i in range(4)]

    MEM_TILES = {"mem_b": range(0, KT // 2), "mem_c": range(KT // 2, KT)}

    order = [("main", 0), ("par", 0), ("main", 1), ("mats", 0), ("xT", 0)]
    s5 = [(half, n) for n in range(16) for half in ("s5a", "s5b")]
    for u in range(2, 8):
        order.append(("main", u))
        order += [s5.pop(0), s5.pop(0)]
    for t, between in enumerate((("s5d_bu", 0), s5.pop(0), ("s5d_bu", 1), s5.pop(0), ("s5d_h", 0))):
        order += [("vtr", t), ("ktr", t), between]
    dec = []
    for t in range(2):
        for b in range(4 * t, 4 * t + 4):
            if b != 4:
                dec += [("dkt", 2 * b), ("dkt", 2 * b + 1)]
            dec += [("dks", b)]
        dec.append(("dsm", t))
        if t == 0:
            dec += [("dkt", 8), ("dkt", 9)]
        dec += [("dsc", t), ("dpt", t), ("dpe", t)] + [("dv", b) for b in range(4 * t, 4 * t + 4)] + [("do", t), ("dot", t)]
    order.append(("dqz", 0))
    att = list(range(len(ATT)))

    S5D_STEPS, ATT_PERIOD, ATT_LATE = (1, 3), 99, 5

    def attention():
        n = att.pop(0)
        if n >= 2:
            order.append(("attp", n - 2))
        order.append(("att", n))

    s5d = dict(zip(S5D_STEPS, (("s5d_y", 0), ("s5d_y", 1))))
    step = 0
    while s5 or dec:
        for work in (s5, dec, dec):
            if work:
                order.append(work.pop(0))
        step += 1
        if step in s5d:
            order.append(s5d[step])
        if step > max(s5d) and step % ATT_PERIOD != 1 and len(att) > ATT_LATE:
            attention()
    for work in ("s5_end", "gelu", "glu", "ssm_sq", "mem_a", "ssm_t"):
        if att:
            attention()
        order.append((work, 0))
    while att:
        attention()
    order.append(("attp", 14))
    order += [("att_end", 0), ("attp", 15), ("subln", 0)]
    for u in range(4):
        order += [("out", u)] + ([("mem_b", 0)] if u == 0 else [("mem_c", 0)] if u == 1 else [])

    S5_BEFORE_DECODE = sum(k == "s5b" for k, _ in order[:order.index(("s5d_h", 0))])

    w_loaded = [S("w_loaded0"), S("w_loaded1")]
    w_hi_ready, w_lo_ready = S("w_hi_ready"), S("w_lo_ready")
    acc_full, acc_out = S("acc_full"), S("acc_out")
    consts_in, x_in, rows_in, par_in, mem_in = S("consts_in"), S("x_in"), S("rows_in"), S("par_in"), S("mem_in")
    stored = S("stored")
    act_own, dve_own, pool_own, pe_own = S("act_own"), S("dve_own"), S("pool_own"), S("pe_own")
    n_stores = [0]

    block = ctx.enter_context(nc.Block())

    @block.sync
    def _(sp_eng):
        e = sp_eng

        def load_unit(n):
            dram, kts, cols = units[n]
            if n == U_GLU:
                e.wait_ge(S("dkT_full"), 2 * DB)
            elif n == U_GLU + 1:
                e.wait_ge(S("dv_done"), DB)
            if n >= 2:
                e.wait_ge(w_lo_ready, n - 1)
            e.dma_start(w_raw[:, n % 2, 0:kts * cols].rearrange("p (k c) -> p k c", k=kts), dram)\
                .then_inc(w_loaded[n % 2], 16)

        def store(dst, src):
            n_stores[0] += 1
            e.dma_start(dst, src).then_inc(stored, 16)

        x_view = A["x_prompt"].rearrange("b (t p) d -> p (b t) d", p=P)
        for t in range(4):
            e.dma_start(x_nat[:, t, :], x_view[:, t, :]).then_inc(x_in, 16)
        e.dma_start(x_nat[0:NS_TOK, 4, :], A["x_sample"].rearrange("b t d -> (b t) d")).then_inc(x_in, 16)
        e.dma_start(ident[:], A["t_ident"]).then_inc(consts_in, 16)
        e.dma_start(ones[:], A["t_ones"]).then_inc(consts_in, 16)
        for name, row, n in (("g_mix_pre", G_MIX_PRE, 8), ("g_mix_post", G_MIX_POST, 8), ("g_mem_pre", G_MEM_PRE, 8),
                             ("g_mem_post", G_MEM_POST, 8), ("g_mem_kv", G_MEM_KV, 8), ("g_ffn_pre", G_FFN_PRE, 8),
                             ("g_ffn_post", G_FFN_POST, 8), ("g_ssm_out", G_SSM, 4)):
            e.dma_start(p_rows[row:row + n, :], A[name][0].rearrange("(k p) -> k p", p=P)).then_inc(rows_in, 16)
        e.dma_start(p_rows[SSM_D:SSM_D + 4, :], A["ssm_d"][0].rearrange("(k g) h -> k (g h)", k=4)).then_inc(rows_in, 16)
        e.dma_start(p_rows[G_SUB:G_SUB + 1, :], A["g_subln"]).then_inc(rows_in, 16)
        e.dma_start(p_rows[LAM_RE:LAM_RE + 16, :], A["ssm_lam_re"][0].rearrange("(c g) s -> c (g s)", g=2)).then_inc(rows_in, 16)
        e.dma_start(p_rows[LAM_IM:LAM_IM + 16, :], A["ssm_lam_im"][0].rearrange("(c g) s -> c (g s)", g=2)).then_inc(rows_in, 16)
        e.dma_start(dt2[:], A["ssm_log_dt"][0].rearrange("(c g) -> c g", g=2)).then_inc(par_in, 16)
        load_unit(0)
        load_unit(1)
        for r, name in enumerate(("ssm_b_re", "ssm_b_im")):
            e.dma_start(b_nat[:, r], A[name][0].rearrange("(c g) s h -> (g s) c h", g=2)).then_inc(par_in, 16)
        for r, name in enumerate(("ssm_c_re", "ssm_c_im")):
            for dup in range(2):
                e.dma_start(c_nat[:, r, :, dup, :], A[name][0].rearrange("(f g) h s -> (g h) f s", f=SF)).then_inc(par_in, 16)
        for r, name in enumerate(("state_ssm_re", "state_ssm_im")):
            e.dma_start(st_nat[:, r, :], A[name][0].rearrange("b (c g) s -> (b c) (g s)", g=2)).then_inc(par_in, 16)
        for i, name in enumerate(("lam_q1", "lam_k1", "lam_q2", "lam_k2")):
            e.dma_start(lamv[:, i, :], A[name].broadcast_to([P, HD])).then_inc(par_in, 16)
        e.dma_start(sel[:], A["t_sel"]).then_inc(par_in, 16)
        nxt = [2]

        def ahead(n):
            while nxt[0] <= min(n, U_FFN + 1):
                if nxt[0] < U_FFN:
                    load_unit(nxt[0])
                    nxt[0] += 1
                else:
                    break

        out_kp = O["new_k_prompt"].rearrange("l b (t p) h d -> t p (l b h d)", p=P)
        out_ks = O["new_k_sample"].rearrange("l b t h d -> (l b t) (h d)")
        out_vp = O["new_v_prompt"].rearrange("l b (t p) h d -> t p (l b h d)", p=P)
        out_vs = O["new_v_sample"].rearrange("l b t h d -> (l b t) (h d)")
        ck = A["cache_k"].rearrange("l n t h d -> (l n) t (h d)")
        cv = A["cache_v"].rearrange("l n t h d -> (l n) t (h d)")
        n_phys = ck.shape[0]

        def page_load(dst, slot, cache, b, waits, done):
            for pg in range(PAGES):
                page = e.value_load(A["page_table"][b:b + 1, pg:pg + 1], min_val=0, max_val=n_phys - 1)
                if pg == 0:
                    for s_, v_ in waits:
                        e.wait_ge(s_, v_)
                e.dma_start(dst[:, slot, pg, :], cache[bass.ds(page, 1), :, :].rearrange("n t c -> t (n c)")).then_inc(done, 16)

        for kind, n in order:
            if kind == "main":
                ahead(min(n + 2, U_GLU - 1))
                if n == 7:
                    e.wait_ge(acc_full, used(7))
                    e.dma_start(alibi[:], A["t_alibi"]).then_inc(S("alibi_in"), 16)
                    e.dma_start(decb[:], A["t_dec"]).then_inc(S("alibi_in"), 16)
            elif kind == "vtr":
                e.wait_ge(S("v_tok_ready"), n + 1)
                if n < 4:
                    store(out_vp[n], v_tok[:, n, :])
                else:
                    store(out_vs, v_new[:])
            elif kind == "ktr":
                e.wait_ge(S("k_tok_ready"), n + 1)
                if n < 4:
                    e.dma_start(out_kp[n], k_tok[:, n % 2, :]).then_inc(S(f"k_stored{n % 2}"), 16)
                else:
                    e.dma_start(out_ks, k_tok[0:NS_TOK, 0, :]).then_inc(S(f"k_stored{n % 2}"), 16)
            elif kind == "s5_end":
                e.wait_ge(S("fin_ready"), 2)
                for r, part in enumerate(("re", "im")):
                    cols = slice(r * P, (r + 1) * P)
                    for name, src in ((f"ssm_{part}_prompt", W47[0:CT_N, 0, cols]), (f"ssm_{part}_sample", W47[:, 1, cols])):
                        e.dma_start(O[name].rearrange("l b (c g) s -> (l b c) (g s)", g=2), src).then_inc(S("fin_stored"), 16)
                e.wait_ge(S("fin_stored"), 64)
                e.dma_start(mem_nat[:], A["mem_prompt"].rearrange("b (t p) d -> p (b t) d", p=P)).then_inc(mem_in, 16)
            elif kind == "dqz":
                for b in range(2):
                    page_load(d_k, b, ck, b, [(w_lo_ready, U_GLU)], S(f"dk_in{b}"))
                for b in range(DV_N):
                    page_load(d_v, b, cv, b, [(acc_full, used(U_GLU - 1))], S(f"dv_in{b}"))
            elif kind == "dkt":
                b = n // 2
                if n % 2 and b + 2 < DB:
                    page_load(d_k, b % 2, ck, b + 2, [(S("dkT_full"), n + 1)], S(f"dk_in{b % 2}"))
            elif kind == "dv":
                if n + DV_N < DB:
                    page_load(d_v, n, cv, n + DV_N, [(S("dv_done"), n + 1)], S(f"dv_in{n}"))
            elif kind == "dot" and n == 1:
                ahead(U_GLU + 1)
            elif kind == "ssm_sq":
                ahead(U_OUT + 1)
            elif kind == "out":
                ahead(U_OUT + n + 2)
        ahead(U_MQ + 1)
        e.wait_ge(S("mk_tok_ready"), 4)
        e.dma_start(O["mem_k_prompt"].rearrange("l b (t p) h d -> p (l b t) (h d)", p=P), mk_tok[:]).then_inc(S("mk_stored"), 16)
        e.wait_ge(acc_out, J_MQ)
        store(O["mem_v_prompt"].rearrange("l b (t p) h d -> p (l b t) (h d)", p=P), mv_tok[:])
        ahead(U_MQ + 3)
        mk_view = A["cache_mem_k"].rearrange("l b (t p) h d -> (l b) p t (h d)", p=P)
        mv_view = A["cache_mem_v"].rearrange("l b (t p) h d -> (l b) p t (h d)", p=P)

        def kv_load(i):
            if i == 0:
                e.wait_ge(acc_full, used(U_MQ - 1))
            if i >= KV_N:
                j = i - KV_N
                if j < DB:
                    e.wait_ge(S("dmT_pe"), 4 * (j + 1))
                else:
                    e.wait_ge(S("dm_pv"), j - DB + 1)
            src = mk_view[i] if i < DB else mv_view[i - DB]
            e.dma_start(dm_kv[:, i % KV_N], src).then_inc(S(f"kv_in{i % KV_N}"), 16)

        for i in range(KV_N):
            kv_load(i)
        ahead(U_MO - 1)
        ahead(U_MO + 1)
        for i in range(KV_N, 2 * DB):
            kv_load(i)
        ahead(U_FFN - 1)
        gate = A["w_gate"][0].rearrange("(k p) c -> p k c", p=P)
        up = A["w_up"][0].rearrange("(k p) c -> p k c", p=P)
        with e.Fori(0, PAIRS) as i:
            for s_, w in enumerate((gate, up)):
                slot = (U_FFN + s_) % 2
                e.wait_ge(w_lo_ready, i * 2 + (U_FFN + s_ - 1))
                e.dma_start(w_raw[:, slot, :].rearrange("p (k c) -> p k c", k=KT), w[:, :, bass.ds(i * 256, 256)])\
                    .then_inc(w_loaded[slot], 16)
        down = A["w_down"][0].rearrange("(k p) c -> p k c", p=P)
        for n in range(U_DOWN, N_UNITS):
            c, (k0, kts) = (n - U_DOWN) // 3, DOWN_K[(n - U_DOWN) % 3]
            e.wait_ge(w_lo_ready, n - 1)
            e.dma_start(w_raw[:, n % 2, 0:kts * 256].rearrange("p (k c) -> p k c", k=kts),
                        down[:, k0:k0 + kts, c * 256:(c + 1) * 256]).then_inc(w_loaded[n % 2], 16)
        out_y = O["y_prompt"].rearrange("b (t p) d -> (b t) p d", p=P)
        for t in range(5):
            e.wait_ge(S("y_out_ready"), 4 * (t + 1))
            if t < 4:
                e.dma_start(out_y[t], y_out[:, t % 2, :]).then_inc(S(f"y_stored{t % 2}"), 16)
            else:
                e.dma_start(O["y_sample"].rearrange("b t d -> (b t) d"), y_out[0:NS_TOK, 0, :]).then_inc(S("y_stored0"), 16)
        e.wait_ge(S("y_stored0"), 48)
        e.wait_ge(S("y_stored1"), 32)
        e.wait_ge(S("k_stored0"), 48)
        e.wait_ge(S("k_stored1"), 32)
        e.wait_ge(S("mk_stored"), 16)
        e.wait_ge(stored, 16 * n_stores[0])

    @block.gpsimd
    def _(pool):
        e = pool

        def split_lo(n, kts, cols, i=None, per=0):
            off = 0 if i is None else i * per
            e.wait_ge(w_hi_ready, off + (n + 1))
            w = kts * cols
            e.tensor_tensor(w_lo[:, n % 2, 0:w], w_raw[:, n % 2, 0:w], w_hi[:, n % 2, 0:w].bitcast(F32), ALU.subtract)\
                .then_inc(w_lo_ready, 1)

        todo = [0]

        def lo_ahead(n):
            while todo[0] <= min(n, U_FFN - 1):
                _, kts, cols = units[todo[0]]
                split_lo(todo[0], kts, cols)
                todo[0] += 1

        lo_ahead(1)
        for kind, n in order:
            if kind == "main":
                lo_ahead(min(n + 1, U_GLU - 1))
            elif kind == "gelu":
                lo_ahead(U_GLU + 1)
        lo_ahead(U_FFN - 1)
        with e.Fori(0, PAIRS) as i:
            for s_ in range(2):
                split_lo(U_FFN + s_, KT, 256, i, 2)
        for n in range(U_DOWN, N_UNITS):
            split_lo(n, DOWN_K[(n - U_DOWN) % 3][1], 256)

    @block.scalar
    def _(act):
        e = act
        own = [0]

        def done(ins):
            own[0] += 1
            ins.then_inc(act_own, 1)
            e.wait_ge(act_own, own[0])

        def split_hi(n, kts, cols, i=None, per=0):
            off = 0 if i is None else i * per
            loads = (0 if i is None else i * (8 * per)) + 16 * (n // 2 + 1)
            e.wait_ge(w_loaded[n % 2], loads)
            if n >= 2:
                e.wait_ge(acc_full, off * 2 + used(n - 2))
            if n == U_GLU:
                e.wait_ge(S("dT_out"), 2)
            w = kts * cols
            e.activation(w_hi[:, n % 2, 0:w], w_raw[:, n % 2, 0:w], ACT.Copy).then_inc(w_hi_ready, 1)

        todo = [0]

        def hi_ahead(n):
            while todo[0] <= min(n, U_FFN - 1):
                _, kts, cols = units[todo[0]]
                split_hi(todo[0], kts, cols)
                todo[0] += 1

        def square_stats(name, src, tiles, ready):
            for k in range(tiles):
                for s_, v_ in ready(k):
                    e.wait_ge(s_, v_)
                if k >= 2:
                    e.wait_ge(*counted(name, "add", max(1, k - 2)))
                e.activation(sq[:, k % 2, :], src[:, k, :], ACT.Square, scale=(tiles * P) ** -0.5).then_inc(S("norm_sq"), 1)

        def gained(name, before, gbase, between=lambda k: None):
            for k in range(KT):
                if k:
                    between(k)
                e.wait_ge(*counted(before, "y", k + 1))
                e.activation(x_hi[:, k, :], yT[:, k, :], ACT.Copy, scale=par[:, gbase + k:gbase + k + 1]).then_inc(S("norm_hi"), 1)
                if k >= 2:
                    e.wait_ge(*counted(name, "add", max(1, k - 2)))
                e.activation(sq[:, k % 2, :], yT[:, k, :], ACT.Square, scale=D ** -0.5).then_inc(S("norm_sq"), 1)

        def root(name):
            e.wait_ge(*counted(name, "sum", 1))
            if name in READS_RSTD:
                e.wait_ge(*READS_RSTD[name])
            e.activation(two(rstd[:]), halves(6), ACT.Sqrt, bias=small[:, EPS_COL:EPS_COL + 1]).then_inc(S("norm_root"), 1)

        def scaled_hi(name, hi, tiles, gcol):
            for k in range(tiles):
                e.wait_ge(S("norm_t"), k + 1)
                e.activation(hi[:, k, :], tt[:, k % 2, :], ACT.Copy, scale=gcol(k)).then_inc(S("norm_hi"), 1)

        def evac(j, dst, func=ACT.Copy, scale=1.0, n=HALF, full=None):
            e.wait_ge(acc_full, full or j + 1)
            src = acc(j) if n == HALF else bank(2 * (j % 2))[:, 0:n]
            e.activation(dst, src, func, scale=scale).then_inc(acc_out, 1)

        def att_tail(n):
            h, i = ATT[n]
            e.wait_ge(S("att_pT"), n + 1)
            if n == 0:
                e.wait_ge(S("k_stored0"), 48)
                e.wait_ge(S("k_stored1"), 32)
            e.activation(a_pT[:, 0:i + 1, i * P:(i + 1) * P], bank(2)[:, 0:(i + 1) * P].rearrange("p (a b) -> p a b", b=P), ACT.Copy)\
                .then_inc(S("att_pTo"), 1)
            if i == 3:
                e.wait_ge(S("att_pv"), h + 1)
                e.activation(oT[:, h, 0:NP_TOK], bank(2), ACT.Copy).then_inc(S("att_oT"), 1)

        def ma_tail(n):
            h, i = MATT[n]
            e.wait_ge(S("ma_pT"), n + 1)
            if i == 0 and h > 0:
                e.wait_ge(S("ma_pv"), 2 * h)
            e.activation(m_pT[:, :, i * P:(i + 1) * P], bank(6)[:, 0:NMEM].rearrange("p (a b) -> p a b", a=2), ACT.Copy)\
                .then_inc(S("ma_pTo"), 1)

        for t in range(5):
            rows = P if t < 4 else NS_TOK
            e.wait_ge(x_in, 16 * 5)
            e.activation(xs[0:rows, t, :], x_nat[0:rows, t, :], ACT.Square, accum_out=small[0:rows, t:t + 1]).then_inc(S("x_ss"), 1)
        e.wait_ge(S("x_ms"), 2)
        e.wait_ge(S("eps_ready"), 1)
        e.activation(small[:, 8:12], small[:, 8:12], ACT.Sqrt)
        e.activation(small[0:NS_TOK, 12:13], small[0:NS_TOK, 12:13], ACT.Sqrt).then_inc(S("x_root"), 1)
        e.wait_ge(S("x_rstd"), 2)
        e.wait_ge(S("x_ss"), 5)
        for t in range(5):
            rows = P if t < 4 else NS_TOK
            e.activation(xs[0:rows, t, :], x_nat[0:rows, t, :], ACT.Copy, scale=small[0:rows, 16 + t:17 + t]).then_inc(S("xs_ready"), 1)
        hi_ahead(1)
        e.wait_ge(S("par_ready"), 1)
        for k in range(KT):
            e.wait_ge(S("xsT_full"), k + 1)
            e.activation(x_hi[:, k, :], banks(4 + 2 * (k % 2)), ACT.Copy, scale=par[:, G_MIX_PRE + k:G_MIX_PRE + k + 1])\
                .then_inc(S("xs_hi"), 1)

        for kind, n in order:
            if kind == "main":
                for m in range(2):
                    if m == 0:
                        hi_ahead(min(n + 1, U_GLU - 1))
                    j = J_W_IN + 2 * n + m
                    t = j % 4
                    dst = {0: uT, 1: qT, 2: kT, 3: vT}[j // 4]
                    evac(j, two(dst[:, t, :]), scale=HD ** -0.5 if dst is qT else 1.0)
            elif kind == "par":
                e.wait_ge(S("dtT_ready"), 1)
                e.activation(sp[:, 1], sp[:, 0], ACT.Exp).then_inc(S("p_dt"), 1)
                e.wait_ge(S("lam_dots"), 2)
                e.activation(small[:, 24:26], small[:, 24:26], ACT.Exp).then_inc(S("lam_exp"), 1)
                e.wait_ge(S("p_arg"), 2)
                e.activation(sp[:, 4], sp[:, 2], ACT.Tanh, scale=0.5).then_inc(S("p_trig"), 1)
                e.activation(sp[:, 5], sp[:, 3], ACT.Sin).then_inc(S("p_trig"), 1)
                e.activation(sp[:, 6], sp[:, 3], ACT.Sin, scale=0.5).then_inc(S("p_trig"), 1)
            elif kind == "mats":
                for g in range(2 * SF):
                    r, f = g // SF, g % SF
                    e.wait_ge(S("bT_full"), g + 1)
                    e.activation(b_lhs[:, 4 * f:4 * f + 4, r, :], bank(7).rearrange("p (a b) -> p a b", a=4), ACT.Copy)\
                        .then_inc(S("bT_out"), 1)
            elif kind == "xT":
                for k in range(KT):
                    e.wait_ge(S("xT_full"), k + 1)
                    e.activation(yT[:, k, :], banks(6), ACT.Copy).then_inc(S("xT_out"), 1)
            elif kind in ("vtr", "ktr"):
                e.wait_ge(S(kind + "_full"), n + 1)
                rows = P if n < 4 else NS_TOK
                if kind == "vtr":
                    dst = v_tok[:, n, :] if n < 4 else v_new[:]
                    e.activation(dst, bank(7)[0:rows, :], ACT.Copy).then_inc(S("v_tok_ready"), 1)
                else:
                    if n >= 2:
                        e.wait_ge(S(f"k_stored{n % 2}"), 16 * (n // 2))
                    e.activation(k_tok[0:rows, n % 2, :], bank(3)[0:rows, :], ACT.Copy).then_inc(S("k_tok_ready"), 1)
            elif kind == "att":
                h, i = ATT[n]
                nk = (i + 1) * P
                e.wait_ge(S("att_max"), n + 1)
                for c in range(2):
                    ins = e.activation(a_s[:, n % 2, c, 0:nk], a_s[:, n % 2, c, 0:nk], ACT.Exp,
                                       bias=small[:, 28 + 2 * (n % 2) + c:29 + 2 * (n % 2) + c],
                                       accum_out=small[:, 32 + 2 * (n % 2) + c:33 + 2 * (n % 2) + c])
                ins.then_inc(S("att_exp"), 1)
            elif kind == "attp":
                att_tail(n)
            elif kind == "s5_end":
                e.wait_ge(S("fin_full"), 1)
                e.activation(W47[0:CT_N, 0, 0:256], bank(7)[0:CT_N, 0:256], ACT.Copy).then_inc(S("fin_ready"), 1)
                e.activation(W47[:, 1, 0:256], bank(7)[:, 256:512], ACT.Copy).then_inc(S("fin_ready"), 1)
            elif kind == "gelu":
                hi_ahead(U_GLU)
                e.wait_ge(S("yssm"), 16)
                e.wait_ge(S("yssm_decode"), 1)
                for f in range(SF):
                    done(e.activation(uT[:, f, :], uT[:, f, :], ACT.Gelu_apprx_tanh))
                    e.activation(y1_hi[:, f, :], uT[:, f, :], ACT.Copy).then_inc(S("y1_hi"), 1)
            elif kind == "dkt":
                b, g = n // 2, n % 2
                e.wait_ge(S("dkT_full"), n + 1)
                if b > 0 and g == 0:
                    e.wait_ge(S("ds_done"), b)
                e.activation(d_kT[:, 2 * g:2 * g + 2, :], bank(7).rearrange("p (a b) -> p a b", a=2), ACT.Copy)\
                    .then_inc(S("dkT_done"), 1)
            elif kind == "dsm":
                e.wait_ge(S("ds_max"), n + 1)
                e.activation(d_p[:, n, :], d_p[:, n, :], ACT.Exp, bias=small[:, D_NM + n:D_NM + n + 1],
                             accum_out=small[:, D_L + n:D_L + n + 1]).then_inc(S("ds_exp"), 1)
            elif kind == "do":
                e.wait_ge(S("dv_done"), 4 * (n + 1))
                e.activation(d_o[:, n, :], bank(3), ACT.Copy).then_inc(S("do_out"), 1)
            elif kind == "subln":
                e.wait_ge(S("att_oT"), 4)
                e.wait_ge(S("dT_out"), 2)
                for h in range(NH):
                    if h >= 2:
                        e.wait_ge(S("subln_sum"), h - 1)
                    e.activation(sq[:, h % 2, :], oT[:, h, :], ACT.Square, scale=P ** -0.5).then_inc(S("subln_sq"), 1)
                e.wait_ge(S("subln_sum"), NH)
                e.wait_ge(S("norm_t"), SF)
                e.activation(two(rstd[:]), halves(4), ACT.Sqrt, bias=small[:, EPS_COL:EPS_COL + 1]).then_inc(S("subln_root"), 1)
                for h in range(NH):
                    e.wait_ge(S("subln_t"), h + 1)
                    e.activation(att_hi[:, h, :], tt[:, h % 2, :], ACT.Copy, scale=small[:, 27:28]).then_inc(S("subln_hi"), 1)
            elif kind == "glu":
                for m in range(4):
                    if m >= 2:
                        e.wait_ge(S("y2"), m - 1)
                    e.wait_ge(acc_full, J_GLU + m + 1)
                    e.activation(two(tt[:, m % 2, :]), acc(J_GLU + m), ACT.Sigmoid).then_inc(acc_out, 1)
            elif kind == "ssm_sq":
                square_stats("ssmn", uT, SF, lambda k: [(S("y2"), k + 1)])
                root("ssmn")
            elif kind == "ssm_t":
                hi_ahead(U_GLU + 1)
                scaled_hi("ssmn", ssm_hi, SF, lambda k: par[:, G_SSM + k:G_SSM + k + 1])
            elif kind == "mem_a":
                e.wait_ge(mem_in, 16)
                for t in range(2):
                    e.activation(mem_sq[:, t, :], mem_nat[:, t, :], ACT.Square, accum_out=small[:, t:t + 1]).then_inc(S("m_ss"), 1)
                e.wait_ge(S("m_ms"), 1)
                e.activation(small[:, 8:10], small[:, 8:10], ACT.Sqrt).then_inc(S("m_root"), 1)
                e.wait_ge(S("m_rstd"), 1)
                for t in range(2):
                    e.activation(mem_nat[:, t, :], mem_nat[:, t, :], ACT.Copy, scale=small[:, 16 + t:17 + t]).then_inc(S("ms_ready"), 1)
            elif kind in ("mem_b", "mem_c"):
                for k in MEM_TILES[kind]:
                    e.wait_ge(S("mT_full"), k + 1)
                    e.activation(mn_hi[:, k, :], bank(6 + k % 2)[:, 0:NMEM], ACT.Copy,
                                 scale=par[:, G_MEM_KV + k:G_MEM_KV + k + 1]).then_inc(S("mn_hi"), 1)
            elif kind == "out":
                hi_ahead(U_OUT + n + 1)
                for m in range(2):
                    k = 2 * n + m
                    if k == 0:
                        e.wait_ge(S("subln_lo"), 4)
                    evac(J_OUT + k, two(z[:, k, :]))
        square_stats("n1", z, KT, lambda k: [(acc_out, J_OUT + k + 1)])
        root("n1")

        def memory_tile(k):
            if k % 2 == 0:
                hi_ahead(U_MK + k // 2 + 1)
            if k == 0:
                e.wait_ge(acc_full, used(U_MK - 1))
            if k < KT:
                evac(J_MK + k, mkT[:, k, :], n=NMEM)
            else:
                evac(J_MK + k, mv_tok[:, k % 2, (k - KT) // 2 * 256:((k - KT) // 2 + 1) * 256], n=256)

        for k in range(5):
            memory_tile(k)
        gained("n2", "n1", G_MEM_PRE, lambda k: memory_tile(4 + k))
        root("n2")
        for k in range(12, 16):
            memory_tile(k)
        for g in range(4):
            e.wait_ge(S("mkt_full"), g + 1)
            e.activation(mk_tok[:, g // 2, (g % 2) * 512:(g % 2 + 1) * 512], bank(6 + g % 2), ACT.Copy).then_inc(S("mk_tok_ready"), 1)
        for n_ in range(4):
            hi_ahead(U_MQ + n_ + 1)
        for n, (h, i) in enumerate(MATT):
            e.wait_ge(S("ma_max"), n + 1)
            if n >= 2:
                e.wait_ge(S("ma_pT"), n - 1)
            e.activation(m_p[:, n % 2, :], bank(4 + n % 2)[:, 0:NMEM], ACT.Exp, scale=MD ** -0.5,
                         bias=small[:, 28 + n % 2:29 + n % 2], accum_out=small[:, 32 + n % 2:33 + n % 2]).then_inc(S("ma_exp"), 1)
            if n >= 1:
                ma_tail(n - 1)
        ma_tail(15)
        for b in range(DB):
            for g in range(4):
                e.wait_ge(S("dmT_pe"), 4 * b + g + 1)
                if b == 0 and g == 0:
                    e.wait_ge(S("mk_stored"), 16)
                if b > 0 and g == 0:
                    e.wait_ge(S("dms"), b)
                e.activation(dm_kT[:, 2 * g:2 * g + 2, :], bank(6 + g % 2).rearrange("p (a b) -> p a b", a=2), ACT.Copy)\
                    .then_inc(S("dmT_out"), 1)
        for t in range(2):
            e.wait_ge(S("dm_max"), t + 1)
            e.activation(dm_p[:, t, :], bank(4 + t)[:, 0:NMEM], ACT.Exp, scale=MD ** -0.5, bias=small[:, 28 + t:29 + t],
                         accum_out=small[:, 32 + t:33 + t]).then_inc(S("dm_exp"), 1)
        for t in range(2):
            for g in range(2):
                e.wait_ge(S("dm_pv"), 4 * (t + 1))
                e.activation(dm_o[:, t, g * 512:(g + 1) * 512], bank(4 + 2 * t + g), ACT.Copy).then_inc(S("dmo_out"), 1)
        for n_ in range(4):
            hi_ahead(U_MO + n_ + 1)
            for m in range(2):
                k = 2 * n_ + m
                evac(J_MO + k, two(z[:, k, :]))
        square_stats("n3", z, KT, lambda k: [(acc_out, J_MO + k + 1)])
        root("n3")
        split_hi(U_FFN, KT, 256)
        gained("n4", "n3", G_FFN_PRE)
        root("n4")
        with e.Fori(0, PAIRS) as i:
            split_hi(U_FFN + 1, KT, 256, i, 2)
            for m in range(2):
                e.wait_ge(acc_out, i * 4 + (J_FFN + m + 1))
                e.activation(tt[:, m, :], tt[:, m, :], ACT.Silu).then_inc(S("silu"), 1)
            split_hi(U_FFN + 2, KT, 256, i, 2)
            for m in range(2):
                e.wait_ge(S("gate_up"), i * 2 + (m + 1))
                e.activation(g_hi[:, bass.ds(i * 2 + m, 1), :], sq[:, m:m + 1, :], ACT.Copy).then_inc(S("g_hi_ready"), 1)
        for n in range(U_DOWN, N_UNITS):
            if n + 1 < N_UNITS:
                split_hi(n + 1, DOWN_K[(n + 1 - U_DOWN) % 3][1], 256)
            c, part = (n - U_DOWN) // 3, (n - U_DOWN) % 3
            if part == 2:
                for m in range(2):
                    evac(J_DOWN + 2 * c + m, two(z_ffn[:, 2 * c + m, :]), full=used(n) - 1 + m)
        square_stats("n5", z_ffn, KT, lambda k: [(acc_out, J_DOWN + k + 1)])
        root("n5")
        for t in range(5):
            rows = P if t < 4 else NS_TOK
            for g in range(4):
                e.wait_ge(S("yt_full"), 4 * t + g + 1)
                if t >= 2 and g == 0:
                    e.wait_ge(S(f"y_stored{t % 2}"), 16 * (t // 2))
                e.activation(y_out[0:rows, t % 2, g * 256:(g + 1) * 256], bank(4 + g)[0:rows, 0:256], ACT.Copy).then_inc(S("y_out_ready"), 1)

    @block.vector
    def _(dve):
        e = dve
        own = [0]

        def done(ins):
            own[0] += 1
            ins.then_inc(dve_own, 1)
            e.wait_ge(dve_own, own[0])

        def mul(out, a, b):
            return e.tensor_tensor(out, a, b, ALU.mult)

        def add(out, a, b):
            return e.tensor_tensor(out, a, b, ALU.add)

        def sub(out, a, b):
            return e.tensor_tensor(out, a, b, ALU.subtract)

        def add_square(name, k):
            e.wait_ge(*counted(name, "sq", k + 1))
            if k == 1:
                add(sqacc[:], sq[:, 0, :], sq[:, 1, :]).then_inc(S("norm_add"), 1)
            else:
                e.wait_ge(*counted(name, "add", k - 1))
                add(sqacc[:], sqacc[:], sq[:, k % 2, :]).then_inc(S("norm_add"), 1)

        def sum_squares(name, tiles):
            for k in range(1, tiles):
                add_square(name, k)

        def make_rstd(name):
            e.wait_ge(*counted(name, "root", 1))
            done(e.reciprocal(rstd[:], rstd[:]))

        def split_scaled(name, src, lo, hi, tiles, gcol):
            def low(k):
                e.wait_ge(*counted(name, "hi", k + 1))
                e.scalar_tensor_tensor(out=lo[:, k, :], in0=tt[:, k % 2, :], scalar=gcol(k), in1=hi[:, k, :].bitcast(F32),
                                       op0=ALU.mult, op1=ALU.subtract).then_inc(S("norm_lo"), 1)
            for k in range(tiles):
                if k >= 2:
                    e.wait_ge(*counted(name, "lo", k - 1))
                mul(tt[:, k % 2, :], src[:, k, :], rstd[:]).then_inc(S("norm_t"), 1)
                if k >= 1:
                    low(k - 1)
            low(tiles - 1)

        def residual(name, src, gbase, following=None, gnext=0):
            def parts(k):
                e.wait_ge(*counted(following, "hi", k + 1))
                e.scalar_tensor_tensor(out=x_lo[:, k, :], in0=yT[:, k, :], scalar=par[:, gnext + k:gnext + k + 1],
                                       in1=x_hi[:, k, :].bitcast(F32), op0=ALU.mult, op1=ALU.subtract).then_inc(S("norm_lo"), 1)
                if k >= 1:
                    add_square(following, k)

            for k in range(KT):
                done(mul(tt[:, k % 2, :], src[:, k, :], rstd[:]))
                e.scalar_tensor_tensor(out=yT[:, k, :], in0=tt[:, k % 2, :], scalar=par[:, gbase + k:gbase + k + 1],
                                       in1=yT[:, k, :], op0=ALU.mult, op1=ALU.add).then_inc(S("norm_y"), 1)
                if following and k >= 1:
                    parts(k - 1)
            if following:
                parts(KT - 1)

        e.memset(small[:, EPS_COL:EPS_COL + 1], EPS).then_inc(S("eps_ready"), 1)
        e.wait_ge(S("x_ss"), 5)
        e.tensor_scalar(small[:, 8:12], small[:, 0:4], 1.0 / D, EPS, ALU.mult, ALU.add).then_inc(S("x_ms"), 1)
        e.tensor_scalar(small[0:NS_TOK, 12:13], small[0:NS_TOK, 4:5], 1.0 / D, EPS, ALU.mult, ALU.add).then_inc(S("x_ms"), 1)
        e.wait_ge(S("x_root"), 1)
        e.reciprocal(small[:, 16:20], small[:, 8:12]).then_inc(S("x_rstd"), 1)
        e.reciprocal(small[0:NS_TOK, 20:21], small[0:NS_TOK, 12:13]).then_inc(S("x_rstd"), 1)
        e.wait_ge(S("par_full"), 1)
        e.tensor_copy(par[:], bank(0)[:, 0:N_PAR]).then_inc(S("par_ready"), 1)
        for k in range(KT):
            e.wait_ge(S("xs_hi"), k + 1)
            e.scalar_tensor_tensor(out=x_lo[:, k, :], in0=banks(4 + 2 * (k % 2)), scalar=par[:, G_MIX_PRE + k:G_MIX_PRE + k + 1],
                                   in1=x_hi[:, k, :].bitcast(F32), op0=ALU.mult, op1=ALU.subtract).then_inc(S("xs_lo"), 1)

        def s5_carry(n):
            f, _ = S5_UNITS[n]
            e.wait_ge(S("s5_h"), n + 1)
            for r in range(2):
                ins = e.tensor_copy(carry[:, 4 * f:4 * f + 4, r], W47[:, r, :].rearrange("p (q t) -> p q t", q=4)[:, :, BLK - 1])
            ins.then_inc(S("s5_carry"), 1)

        def s5_out(n):
            f, blk = S5_UNITS[n]
            cols = slice(blk * BLK, (blk + 1) * BLK)
            e.wait_ge(S("s5_y"), n + 1)
            e.scalar_tensor_tensor(out=uT[:, f, cols], in0=uT[:, f, cols], scalar=par[:, SSM_D + f:SSM_D + f + 1],
                                   in1=bank(6)[:, 0:BLK], op0=ALU.mult, op1=ALU.add).then_inc(S("yssm"), 1)

        NM, L, R, MX = 28, 32, 36, 40

        def att_tail(n):
            h, i = ATT[n]
            nk = (i + 1) * P
            o = 2 * (n % 2)
            e.wait_ge(S("att_exp"), n + 1)
            done(e.reciprocal(small[:, R + o:R + o + 2], small[:, L + o:L + o + 2]))
            done(mul(small[:, R + o + 1:R + o + 2], small[:, R + o + 1:R + o + 2], small[:, 26:27]))
            done(e.tensor_scalar(a_s[:, n % 2, 1, 0:nk], a_s[:, n % 2, 1, 0:nk], small[:, R + o + 1:R + o + 2], None, ALU.mult))
            if n >= 2:
                e.wait_ge(S("att_pT"), n - 1)
            e.scalar_tensor_tensor(out=a_p[:, n % 2, 0:nk], in0=a_s[:, n % 2, 0, 0:nk], scalar=small[:, R + o:R + o + 1],
                                   in1=a_s[:, n % 2, 1, 0:nk], op0=ALU.mult, op1=ALU.add).then_inc(S("att_p"), 1)

        for kind, n in order:
            if kind == "par":
                e.wait_ge(par_in, 16 * N_PAR_LOADS)
                e.tensor_copy(dt_rows[:], dt2[:].unsqueeze(2).broadcast_to([CT_N, 2, SP_])).then_inc(S("dt_rows"), 1)
                for i in range(2):
                    e.tensor_tensor_reduce(out=lamp[:, i, :], in0=lamv[:, 2 * i, :], in1=lamv[:, 2 * i + 1, :], scale=1.0,
                                           scalar=0.0, op0=ALU.mult, op1=ALU.add, accum_out=small[:, 24 + i:25 + i])\
                        .then_inc(S("lam_dots"), 1)
                e.memset(b_pad[:], 0.0)
                done(e.memset(c_lhs[:], 0.0))
                e.wait_ge(S("dtT"), 1)
                e.tensor_copy(sp[:, 0], bank(4)[:, 0:CT_N]).then_inc(S("dtT_ready"), 1)
                e.wait_ge(S("stT"), 1)
                e.tensor_copy(st[:].rearrange("p a b -> p (a b)"), bank(5)[:, 0:2 * P]).then_inc(S("st_ready"), 1)
                e.wait_ge(S("lam_exp"), 1)
                done(sub(small[:, 26:27], small[:, 25:26], small[:, 24:25]))
                done(e.tensor_scalar(small[:, 26:27], small[:, 26:27], -LAM_INIT, None, ALU.add))
                e.tensor_scalar(small[:, 27:28], par[:, G_SUB:G_SUB + 1], 1.0 - LAM_INIT, None, ALU.mult)
                done(e.scalar_tensor_tensor(out=small[:, 44:45], in0=sel[:, 1:2], scalar=small[:, 26:27], in1=sel[:, 0:1],
                                            op0=ALU.mult, op1=ALU.add))
                lre, lim = par[:, LAM_RE:LAM_RE + CT_N], par[:, LAM_IM:LAM_IM + CT_N]
                c = lambda i: sp[:, i]
                e.wait_ge(S("p_dt"), 1)
                mul(c(2), lre, c(1)).then_inc(S("p_arg"), 1)
                done(mul(c(7), lim, c(1)))
                done(e.tensor_scalar(c(8), c(7), 1.0 / (2 * math.pi), None, ALU.mult))
                done(e.tensor_scalar(c(8), c(8), 12582912.0, None, ALU.add))
                done(e.tensor_scalar(c(8), c(8), -12582912.0, None, ALU.add))
                c1 = 6.28125
                c2 = float(np.float32(math.floor((2 * math.pi - c1) * 2 ** 21) / 2 ** 21))
                c3 = 2 * math.pi - c1 - c2
                for part in (c1, c2, c3):
                    done(e.scalar_tensor_tensor(out=c(7), in0=c(8), scalar=-part, in1=c(7), op0=ALU.mult, op1=ALU.add))
                e.tensor_scalar(c(3), c(7), 3.1415925, -3.1415925, ALU.min, ALU.max).then_inc(S("p_arg"), 1)
                e.wait_ge(S("p_trig"), 3)
                done(e.tensor_scalar(c(9), c(4), -1.0, 1.0, ALU.mult, ALU.add))
                done(e.reciprocal(c(9), c(9)))
                done(e.tensor_scalar(c(10), c(4), 1.0, None, ALU.add))
                done(mul(lam3[:, 0], c(10), c(9)))
                done(mul(c(11), c(4), c(9)))
                done(mul(c(12), c(6), c(6)))
                done(e.tensor_scalar(c(12), c(12), -2.0, None, ALU.mult))
                done(e.tensor_scalar(c(13), c(12), 1.0, None, ALU.add))
                done(mul(lam3[:, 1], lam3[:, 0], c(13)))
                done(mul(lam3[:, 2], lam3[:, 0], c(5)))
                done(e.scalar_tensor_tensor(out=c(14), in0=c(11), scalar=2.0, in1=c(13), op0=ALU.mult, op1=ALU.mult))
                done(add(c(14), c(14), c(12)))
                done(mul(c(15), lre, lre))
                done(mul(c(16), lim, lim))
                done(add(c(15), c(15), c(16)))
                done(e.reciprocal(c(15), c(15)))
                done(mul(c(16), c(14), lre))
                done(mul(c(17), lam3[:, 2], lim))
                done(add(c(16), c(16), c(17)))
                done(mul(c(18), c(16), c(15)))
                done(mul(c(16), lam3[:, 2], lre))
                done(mul(c(17), c(14), lim))
                done(sub(c(16), c(16), c(17)))
                done(mul(c(19), c(16), c(15)))
                wr, wi = (c(i).unsqueeze(2).broadcast_to([P, CT_N, GH]) for i in (18, 19))
                for r, (x, y, op) in enumerate(((0, 1, ALU.subtract), (1, 0, ALU.add))):
                    done(mul(b_tmp[:, 0], wr, b_nat[:, x]))
                    done(mul(b_tmp[:, 1], wi, b_nat[:, y]))
                    done(e.tensor_tensor(b_bar[:, r], b_tmp[:, 0], b_tmp[:, 1], op))
            elif kind == "mats":
                for r in range(2):
                    if r:
                        e.wait_ge(S("bT_full"), SF)
                    for g in range(2):
                        for q in range(4):
                            rows, cols = slice(64 * g, 64 * g + 64), slice(32 * q + 16 * g, 32 * q + 16 * g + 16)
                            ins = e.tensor_copy(b_pad[rows, q::4, cols], b_bar[rows, r, q::4, :])
                            ins.then_inc(S("b_pad"), 1)
                for g in range(2 * SF):
                    r, f = g // SF, g % SF
                    e.wait_ge(S("cT_full"), g + 1)
                    for d in range(2):
                        rows = slice(64 * d, 64 * d + 64)
                        src = bank(6)[rows, 0:P].rearrange("p (q d h) -> p q d h", q=4, d=2)[:, :, d, :]
                        ins = e.tensor_scalar(c_lhs[rows, 4 * f:4 * f + 4, r, 16 * d:16 * d + 16], src, 1.0 - 2.0 * r, None, ALU.mult)
                    ins.then_inc(S("cT_out"), 1)
                e.wait_ge(S("xsT_full"), KT)
                rc, rs = rot[:, 0], rot[:, 1]
                e.tensor_copy(rc[:, :, 0], sp[:, 13])
                done(e.tensor_copy(rs[:, :, 0], sp[:, 5]))
                m = 1
                while m < BLK:
                    w03 = W03[:].rearrange("p a b -> p (a b)")
                    t0, t1 = w03[:, 0:CT_N * m].rearrange("p (c t) -> p c t", t=m), w03[:, 1024:1024 + CT_N * m].rearrange("p (c t) -> p c t", t=m)
                    ec, es = (x[:, :, m - 1:m].broadcast_to([P, CT_N, m]) for x in (rc, rs))
                    mul(t0, rc[:, :, 0:m], ec)
                    done(mul(t1, rs[:, :, 0:m], es))
                    done(sub(rc[:, :, m:2 * m], t0, t1))
                    mul(t0, rs[:, :, 0:m], ec)
                    done(mul(t1, rc[:, :, 0:m], es))
                    done(add(rs[:, :, m:2 * m], t0, t1))
                    m *= 2
            elif kind == "s5a":
                f, blk = S5_UNITS[n]
                if n >= 1:
                    s5_carry(n - 1)
                e.wait_ge(S("s5_bu"), n + 1)
                rc, rs = (rot[:, r, 4 * f:4 * f + 4, :] for r in range(2))
                w = lambda i: W03[:, i, :].rearrange("p (q t) -> p q t", q=4)
                bu = [bank(4 + r).rearrange("p (q t) -> p q t", q=4) for r in range(2)]
                mul(w(0), bu[0], rc)
                mul(w(1), bu[1], rs)
                mul(w(2), bu[1], rc)
                mul(w(3), bu[0], rs).then_inc(S("s5_in_mul"), 1)
                e.wait_ge(S("s5_in_mul"), n + 1)
                if n > 0:
                    e.wait_ge(S("s5_y"), n)
                    e.wait_ge(S("s5_carry"), n)
                add(W47[:, 0], W03[:, 0], W03[:, 1])
                sub(W47[:, 1], W03[:, 2], W03[:, 3]).then_inc(S("s5_in_sum"), 1)
                e.wait_ge(S("s5_in_sum"), n + 1)
                for r in range(2):
                    for q in range(4):
                        ct = 4 * f + q
                        init = carry[:, ct, r:r + 1] if blk else 0.0
                        ins = e.tensor_tensor_scan(W47[:, 2 + r, q * BLK:(q + 1) * BLK], lam3[:, 0, ct:ct + 1].broadcast_to([P, BLK]),
                                                   W47[:, r, q * BLK:(q + 1) * BLK], init, ALU.mult, ALU.add)
                ins.then_inc(S("s5_scan"), 1)
            elif kind == "s5b":
                f, blk = S5_UNITS[n]
                if n >= 1:
                    s5_out(n - 1)
                e.wait_ge(S("s5_scan"), n + 1)
                rc, rs = (rot[:, r, 4 * f:4 * f + 4, :] for r in range(2))
                w = lambda i: W03[:, i, :].rearrange("p (q t) -> p q t", q=4)
                g = [W47[:, 2 + r, :].rearrange("p (q t) -> p q t", q=4) for r in range(2)]
                mul(w(0), g[0], rc)
                mul(w(1), g[1], rs)
                mul(w(2), g[1], rc)
                mul(w(3), g[0], rs).then_inc(S("s5_out_mul"), 1)
                e.wait_ge(S("s5_out_mul"), n + 1)
                sub(W47[:, 0], W03[:, 0], W03[:, 1])
                add(W47[:, 1], W03[:, 2], W03[:, 3]).then_inc(S("s5_h"), 1)
            elif kind == "att":
                h, i = ATT[n]
                nk = (i + 1) * P
                e.wait_ge(S("alibi_in"), 32)
                e.wait_ge(S("att_s"), n + 1)
                o = 2 * (n % 2)
                for c in range(2):
                    ins = e.tensor_tensor_reduce(out=a_s[:, n % 2, c, 0:nk], in0=bank(c)[:, 0:nk],
                                                 in1=alibi[:, h, ALIBI_W - nk:ALIBI_W], scale=1.0, scalar=NEG,
                                                 op0=ALU.add, op1=ALU.max, accum_out=small[:, MX + o + c:MX + o + c + 1])
                ins.then_inc(S("att_biased"), 1)
                e.wait_ge(S("att_biased"), n + 1)
                e.tensor_scalar(small[:, NM + o:NM + o + 2], small[:, MX + o:MX + o + 2], -1.0, None, ALU.mult).then_inc(S("att_max"), 1)
                if n >= 1:
                    att_tail(n - 1)
            elif kind == "att_end":
                att_tail(15)
            elif kind == "s5_end":
                s5_carry(15)
                s5_out(15)
            elif kind == "s5d_h":
                e.wait_ge(S("s5d_bu"), 2)
                e.wait_ge(S("s5_h"), S5_BEFORE_DECODE)
                lb = [lam3[:, 1 + r].unsqueeze(2).broadcast_to([P, CT_N, DB]) for r in range(2)]
                w = lambda i: W03[:, i, 0:P].rearrange("p (c b) -> p c b", b=DB)
                for t in range(DT):
                    if t == 0:
                        prev = [st[:, r, :].rearrange("p (b c) -> p c b", b=DB) for r in range(2)]
                    else:
                        prev = [H_dec[:, :, r, :].rearrange("p c (b t) -> p c b t", t=DT)[:, :, :, t - 1] for r in range(2)]
                    bu = [bank(r).rearrange("p (c b t) -> p c b t", b=DB, t=DT)[:, :, :, t] for r in range(2)]
                    new = [H_dec[:, :, r, :].rearrange("p c (b t) -> p c b t", t=DT)[:, :, :, t] for r in range(2)]
                    mul(w(0), lb[0], prev[0])
                    mul(w(1), lb[1], prev[1])
                    mul(w(2), lb[0], prev[1])
                    done(mul(w(3), lb[1], prev[0]))
                    sub(w(0), w(0), w(1))
                    done(add(w(2), w(2), w(3)))
                    add(new[0], w(0), bu[0])
                    done(add(new[1], w(2), bu[1]))
                for r in range(2):
                    ins = e.tensor_copy(st[:, r, :].rearrange("p (b c) -> p c b", b=DB),
                                        H_dec[:, :, r, :].rearrange("p c (b t) -> p c b t", t=DT)[:, :, :, DT - 1])
                ins.then_inc(S("s5d_h"), 1)
            elif kind == "s5d_y" and n == 1:
                e.wait_ge(S("s5d_y"), 2)
                for f in range(SF):
                    ins = e.scalar_tensor_tensor(out=uT[:, f, NP_TOK:TOK], in0=uT[:, f, NP_TOK:TOK], scalar=par[:, SSM_D + f:SSM_D + f + 1],
                                                 in1=bank(2)[:, f * NS_TOK:(f + 1) * NS_TOK], op0=ALU.mult, op1=ALU.add)
                ins.then_inc(S("yssm_decode"), 1)
            elif kind == "gelu":
                for f in range(SF):
                    e.wait_ge(S("y1_hi"), f + 1)
                    sub(y1_lo[:, f, :], uT[:, f, :], y1_hi[:, f, :].bitcast(F32)).then_inc(S("y1_lo"), 1)
            elif kind == "dqz":
                e.wait_ge(acc_full, used(U_GLU - 1))
                e.wait_ge(acc_out, 8)
                e.memset(d_pT[:], 0.0)
                e.memset(d_pTn[:], 0.0)
                done(e.memset(d_qz[:], 0.0))
                for h in range(NH):
                    for c in range(2):
                        rows = slice(64 * c, 64 * c + 64)
                        ins = e.tensor_copy(d_qz[rows, h, :, c * 16 + h * 4:c * 16 + h * 4 + 4],
                                            qT[rows, h, NP_TOK:TOK].rearrange("p (b t) -> p b t", t=DT))
                        ins.then_inc(S("dqz"), 1)
            elif kind == "dsm":
                t = n
                e.wait_ge(S("ds_done"), 4 * (t + 1))
                done(e.tensor_tensor_reduce(out=d_p[:, t, :], in0=bank(3)[:, 0:DEC_W], in1=decb[:, t, :], scale=1.0,
                                            scalar=NEG, op0=ALU.add, op1=ALU.max, accum_out=small[:, D_MX + t:D_MX + t + 1]))
                e.tensor_scalar(small[:, D_NM + t:D_NM + t + 1], small[:, D_MX + t:D_MX + t + 1], -1.0, None, ALU.mult)\
                    .then_inc(S("ds_max"), 1)
            elif kind == "dsc":
                t = n
                e.wait_ge(S("ds_exp"), t + 1)
                done(e.reciprocal(small[:, D_R + t:D_R + t + 1], small[:, D_L + t:D_L + t + 1]))
                done(mul(small[:, D_R + t:D_R + t + 1], small[:, D_R + t:D_R + t + 1], small[:, 44:45]))
                e.tensor_scalar(d_p[:, t, :], d_p[:, t, :], small[:, D_R + t:D_R + t + 1], None, ALU.mult).then_inc(S("dp"), 1)
            elif kind == "dpe":
                t = n
                e.wait_ge(S("dpT_full"), t + 1)
                past = bank(7)[:, 0:PAST].rearrange("p (g b c r) -> p g b c r", g=PAGES, b=4, c=2)
                new = bank(7)[0:NS_TOK, PAST:PAST + P].rearrange("p (b c r) -> p b c r", b=4, c=2)
                dst, dstn = d_pT[:, :, 4 * t:4 * t + 4, 0:16], d_pTn[:, 4 * t:4 * t + 4, 0:16]
                e.tensor_copy(dst, past[:, :, :, 0, :])
                done(e.tensor_copy(dstn, new[:, :, 0, :]))
                add(dst, dst, past[:, :, :, 1, :])
                add(dstn, dstn, new[:, :, 1, :]).then_inc(S("dpT"), 1)
            elif kind == "dot":
                t = n
                e.wait_ge(S("doT_full"), t + 1)
                for h in range(NH):
                    src = bank(7)[:, h * P:(h + 1) * P].rearrange("p (b r) -> p b r", b=4)[:, :, 4 * h:4 * h + 4]
                    ins = e.tensor_copy(oT[:, h, NP_TOK + 16 * t:NP_TOK + 16 * t + 16].rearrange("p (b q) -> p b q", b=4), src)
                ins.then_inc(S("dT_out"), 1)
            elif kind == "subln":
                def low(h):
                    e.wait_ge(S("subln_hi"), h + 1)
                    e.scalar_tensor_tensor(out=att_lo[:, h, :], in0=tt[:, h % 2, :], scalar=small[:, 27:28],
                                           in1=att_hi[:, h, :].bitcast(F32), op0=ALU.mult, op1=ALU.subtract).then_inc(S("subln_lo"), 1)
                e.wait_ge(S("subln_root"), 1)
                e.reciprocal(rstd[:], rstd[:]).then_inc(S("subln_r"), 1)
                for h in range(NH):
                    e.wait_ge(S("subln_rb"), h + 1)
                    if h >= 2:
                        e.wait_ge(S("subln_lo"), h - 1)
                    mul(two(tt[:, h % 2, :]), two(oT[:, h, :]), halves(4 + 2 * (h % 2))).then_inc(S("subln_t"), 1)
                    if h:
                        low(h - 1)
                low(NH - 1)
            elif kind == "glu":
                for m in range(SF):
                    e.wait_ge(acc_out, J_GLU + m + 1)
                    mul(uT[:, m, :], uT[:, m, :], tt[:, m % 2, :]).then_inc(S("y2"), 1)
            elif kind == "ssm_sq":
                sum_squares("ssmn", SF)
                make_rstd("ssmn")
            elif kind == "ssm_t":
                split_scaled("ssmn", uT, ssm_lo, ssm_hi, SF, lambda k: par[:, G_SSM + k:G_SSM + k + 1])
            elif kind == "mem_a":
                e.wait_ge(S("m_ss"), 2)
                e.tensor_scalar(small[:, 8:10], small[:, 0:2], 1.0 / D, EPS, ALU.mult, ALU.add).then_inc(S("m_ms"), 1)
                e.wait_ge(S("m_root"), 1)
                e.reciprocal(small[:, 16:18], small[:, 8:10]).then_inc(S("m_rstd"), 1)
            elif kind in ("mem_b", "mem_c"):
                for k in MEM_TILES[kind]:
                    e.wait_ge(S("mn_hi"), k + 1)
                    e.scalar_tensor_tensor(out=mn_lo[:, k, :], in0=bank(6 + k % 2)[:, 0:NMEM], scalar=par[:, G_MEM_KV + k:G_MEM_KV + k + 1],
                                           in1=mn_hi[:, k, :].bitcast(F32), op0=ALU.mult, op1=ALU.subtract).then_inc(S("mn_lo"), 1)

        sum_squares("n1", KT)
        make_rstd("n1")
        residual("n1", z, G_MIX_POST, "n2", G_MEM_PRE)
        make_rstd("n2")
        for k in range(KT):
            e.wait_ge(acc_full, J_MQ + k + 1)
            mul(two(qm[:, k, :]), acc(J_MQ + k), two(rstd[:])).then_inc(acc_out, 1)
        e.memset(dm_qz[:], 0.0)
        e.wait_ge(acc_out, J_MO)
        done(e.tensor_copy(small[:, 50:51], small[:, 44:45]))
        for k in range(KT):
            h = k // 2
            e.tensor_copy(dm_qz[:, :, k, 4 * h:4 * h + 4], qm[:, k, NP_TOK:TOK].rearrange("p (b t) -> p b t", t=DT)).then_inc(S("dmqz"), 1)

        def ma_tail(n):
            h, i = MATT[n]
            o = n % 2
            e.wait_ge(S("ma_exp"), n + 1)
            done(e.reciprocal(small[:, R + o:R + o + 1], small[:, L + o:L + o + 1]))
            e.tensor_scalar(m_p[:, o, :], m_p[:, o, :], small[:, R + o:R + o + 1], None, ALU.mult).then_inc(S("ma_p"), 1)

        def ma_out(h):
            for d in range(2):
                e.wait_ge(S("ma_pv"), 2 * h + d + 1)
                done(e.tensor_copy(x_hi[:, 2 * h + d, 0:NP_TOK], bank(d)))
                sub(x_lo[:, 2 * h + d, 0:NP_TOK], bank(d), x_hi[:, 2 * h + d, 0:NP_TOK].bitcast(F32)).then_inc(S("ma_o"), 1)

        for n, (h, i) in enumerate(MATT):
            o = n % 2
            e.wait_ge(S("ma_s"), n + 1)
            done(e.reduce_max(small[:, MX + o:MX + o + 1], bank(4 + o)[:, 0:NMEM], AX_X))
            e.tensor_scalar(small[:, NM + o:NM + o + 1], small[:, MX + o:MX + o + 1], -MD ** -0.5, None, ALU.mult).then_inc(S("ma_max"), 1)
            if n >= 1:
                ma_tail(n - 1)
            if i == 1 and h >= 1:
                ma_out(h - 1)
        ma_tail(15)
        ma_out(3)
        for t in range(2):
            e.wait_ge(S("dms"), 4 * (t + 1))
            done(e.reduce_max(small[:, MX + t:MX + t + 1], bank(4 + t)[:, 0:NMEM], AX_X))
            e.tensor_scalar(small[:, NM + t:NM + t + 1], small[:, MX + t:MX + t + 1], -MD ** -0.5, None, ALU.mult).then_inc(S("dm_max"), 1)
        for t in range(2):
            e.wait_ge(S("dm_exp"), t + 1)
            done(e.reciprocal(small[:, R + t:R + t + 1], small[:, L + t:L + t + 1]))
            e.tensor_scalar(dm_p[:, t, :], dm_p[:, t, :], small[:, R + t:R + t + 1], None, ALU.mult).then_inc(S("dm_pr"), 1)
        for t in range(2):
            e.wait_ge(S("dm_pTf"), t + 1)
            e.tensor_copy(dm_pT[:, :, t, :], bank(6 + t)[:, 0:NMEM].rearrange("p (a b) -> p a b", a=2)).then_inc(S("dm_pTo"), 1)
        for t in range(2):
            e.wait_ge(S("dmoT"), t + 1)
            for h in range(MH):
                src = pall[:, 2 * t:2 * t + 2, :].rearrange("p a b -> p (a b)")[:, 2 * h * P:(2 * h + 2) * P]\
                    .rearrange("p (d b r) -> p d b r", d=2, b=4)[:, :, :, 4 * h:4 * h + 4]
                cols = slice(NP_TOK + 16 * t, NP_TOK + 16 * t + 16)
                hi = x_hi[:, 2 * h:2 * h + 2, cols].rearrange("p d (b q) -> p d b q", b=4)
                lo = x_lo[:, 2 * h:2 * h + 2, cols].rearrange("p d (b q) -> p d b q", b=4)
                done(e.tensor_copy(hi, src))
                sub(lo, src, hi.bitcast(F32)).then_inc(S("dmx"), 1)
        sum_squares("n3", KT)
        make_rstd("n3")
        residual("n3", z, G_MEM_POST, "n4", G_FFN_PRE)
        make_rstd("n4")
        with e.Fori(0, PAIRS) as i:
            for m in range(2):
                e.wait_ge(acc_full, i * 4 + (J_FFN + m + 1))
                e.wait_ge(parts_lo, i * 2 + LO_FFN)
                mul(two(tt[:, m, :]), acc(m), two(rstd[:])).then_inc(acc_out, 1)
            for m in range(2):
                e.wait_ge(acc_full, i * 4 + (J_FFN + 2 + m + 1))
                mul(two(sq[:, m, :]), acc(m), two(rstd[:])).then_inc(acc_out, 1)
                e.wait_ge(acc_out, i * 4 + (J_FFN + 2 + m + 1))
                e.wait_ge(S("silu"), i * 2 + (m + 1))
                mul(sq[:, m, :], sq[:, m, :], tt[:, m, :]).then_inc(S("gate_up"), 1)
            for m in range(2):
                e.wait_ge(S("g_hi_ready"), i * 2 + (m + 1))
                sub(g_lo[:, bass.ds(i * 2 + m, 1), :], sq[:, m:m + 1, :], g_hi[:, bass.ds(i * 2 + m, 1), :].bitcast(F32))\
                    .then_inc(parts_lo, 1)
        sum_squares("n5", KT)
        make_rstd("n5")
        residual("n5", z_ffn, G_FFN_POST)

    @block.tensor
    def _(pe):
        e = pe
        mm = e.matmul

        def transposes_to(e_, dst, src, n, w, idt):
            for h in range(NH):
                ins = e_.transpose(dst[0:w, h * P:(h + 1) * P], src[:, h, n * P:n * P + w], idt[:])
            return ins

        def product(j, w_slot, cols, col, x_h, x_l, k_x, kts, first=True, last=True, k_off=0):
            if first and j >= 2:
                e.wait_ge(acc_out, j - 1)
            for k in range(kts):
                wcol = slice((k_off + k) * cols + col, (k_off + k) * cols + col + P)
                wh, wl = w_hi[:, w_slot, wcol], w_lo[:, w_slot, wcol]
                for w, x, s_, t_ in ((wh, x_h, True, False), (wh, x_l, False, False), (wl, x_h, False, True)):
                    for a in range(2):
                        ins = mm(acc(j)[:, a, :], w, x[:, k_x + k, a * HALF:(a + 1) * HALF],
                                 start=first and k == 0 and s_, stop=last and k == kts - 1 and t_)
            return ins

        def unit(n, j, kts, cols, x_h, x_l, k_x=0, first=True, last=True):
            e.wait_ge(w_lo_ready, n + 1)
            for m in range(cols // P):
                product(j + m, n % 2, cols, m * P, x_h, x_l, k_x, kts, first, last).then_inc(acc_full, 1)

        def spread_sum(name):
            for a in range(2):
                ins = mm(halves(6)[:, a, :], ones[:], sqacc[:, a * HALF:(a + 1) * HALF], start=True, stop=True)
            ins.then_inc(S("norm_sum"), 1)

        def transposes(dst, srcs, rows=P):
            at_ = 0
            for src in srcs:
                w = src.shape[0]
                ins = e.transpose(dst[0:src.shape[1], at_:at_ + w], src, ident[0:w, 0:w])
                at_ += w
            return ins

        e.wait_ge(consts_in, 32)
        e.wait_ge(rows_in, 16 * N_ROW_LOADS)
        transposes(bank(0), [p_rows[:]]).then_inc(S("par_full"), 1)
        for k in range(KT):
            if k == 0:
                e.wait_ge(S("xs_ready"), 5)
            if k >= 2:
                e.wait_ge(S("xs_lo"), k - 1)
            for t in range(5):
                rows = P if t < 4 else NS_TOK
                ins = e.transpose(banks(4 + 2 * (k % 2))[:, t * P:t * P + rows], xs[0:rows, t, k * P:(k + 1) * P], ident[0:rows, 0:rows])
            ins.then_inc(S("xsT_full"), 1)

        def s5_bu(n):
            f, blk = S5_UNITS[n]
            if n == 0:
                e.wait_ge(acc_out, 4)
                e.wait_ge(S("st_ready"), 1)
                e.wait_ge(S("bT_out"), 2 * SF)
            else:
                e.wait_ge(S("s5_in_mul"), n)
            for r in range(2):
                for q in range(4):
                    ins = mm(bank(4 + r)[:, q * BLK:(q + 1) * BLK], b_lhs[:, 4 * f + q, r, :], uT[:, f, blk * BLK:(blk + 1) * BLK],
                             start=True, stop=True)
            ins.then_inc(S("s5_bu"), 1)

        def s5_y(n):
            f, _ = S5_UNITS[n]
            e.wait_ge(S("s5_h"), n + 1)
            if n >= 1:
                e.wait_ge(S("yssm"), n)
            for q in range(4):
                for r in range(2):
                    ins = mm(bank(6)[32 * q:32 * q + 32, 0:BLK], c_lhs[:, 4 * f + q, r, :], W47[:, r, q * BLK:(q + 1) * BLK],
                             start=r == 0, stop=r == 1)
            ins.then_inc(S("s5_y"), 1)

        def att_tail(n):
            h, i = ATT[n]
            e.wait_ge(S("att_p"), n + 1)
            if n >= 1:
                e.wait_ge(S("att_pTo"), n)
            if i == 0 and h:
                e.wait_ge(S("att_oT"), h)
            transposes(bank(2), [a_p[:, n % 2, k * P:(k + 1) * P] for k in range(i + 1)]).then_inc(S("att_pT"), 1)
            if i == 3:
                e.wait_ge(S("att_pTo"), n + 1)
                for k in range(4):
                    ins = mm(bank(2)[:, k * P:512], v_tok[:, k, h * P:(h + 1) * P], a_pT[:, k, k * P:512], start=k == 0, stop=k == 3)
                ins.then_inc(S("att_pv"), 1)

        for kind, n in order:
            if kind == "main":
                if n == 0:
                    e.wait_ge(S("xs_lo"), KT)
                unit(n, J_W_IN + 2 * n, KT, 256, x_hi, x_lo)
            elif kind == "par":
                e.wait_ge(S("dt_rows"), 1)
                transposes(bank(4), [dt_rows[:].rearrange("p a b -> p (a b)")]).then_inc(S("dtT"), 1)
                transposes(bank(5), [st_nat[:, r, :] for r in range(2)]).then_inc(S("stT"), 1)
            elif kind == "mats":
                e.wait_ge(S("par_ready"), 1)
                for g in range(2 * SF):
                    r, f = g // SF, g % SF
                    e.wait_ge(S("b_pad"), 8 * (r + 1))
                    if g >= 1:
                        e.wait_ge(S("bT_out"), g)
                    transposes(bank(7), [b_pad[:, 4 * f + q, :] for q in range(4)]).then_inc(S("bT_full"), 1)
                for g in range(2 * SF):
                    r, f = g // SF, g % SF
                    if g >= 1:
                        e.wait_ge(S("cT_out"), g)
                    transposes(bank(6), [c_nat[:, r, f].rearrange("p a b -> p (a b)")]).then_inc(S("cT_full"), 1)
            elif kind == "xT":
                e.wait_ge(S("cT_out"), 2 * SF)
                e.wait_ge(S("bT_out"), 2 * SF)
                for k in range(KT):
                    if k >= 1:
                        e.wait_ge(S("xT_out"), k)
                    for t in range(5):
                        rows = P if t < 4 else NS_TOK
                        ins = e.transpose(banks(6)[:, t * P:t * P + rows], x_nat[0:rows, t, k * P:(k + 1) * P], ident[0:rows, 0:rows])
                    ins.then_inc(S("xT_full"), 1)
                e.wait_ge(S("xT_out"), KT)
            elif kind == "s5a":
                if n == 0:
                    s5_bu(0)
                else:
                    s5_y(n - 1)
            elif kind == "s5b":
                if n + 1 < len(S5_UNITS):
                    s5_bu(n + 1)
            elif kind == "vtr":
                e.wait_ge(acc_out, 16)
                if n:
                    e.wait_ge(S("v_tok_ready"), n)
                w = P if n < 4 else NS_TOK
                transposes_to(e, bank(7), vT, n, w, ident).then_inc(S("vtr_full"), 1)
            elif kind == "ktr":
                if n:
                    e.wait_ge(S("k_tok_ready"), n)
                w = P if n < 4 else NS_TOK
                transposes_to(e, bank(3), kT, n, w, ident).then_inc(S("ktr_full"), 1)
            elif kind == "att":
                h, i = ATT[n]
                nk = (i + 1) * P
                if n >= 1:
                    e.wait_ge(S("att_biased"), n)
                else:
                    e.wait_ge(S("yssm_decode"), 1)
                for c in range(2):
                    rows = slice(64 * c, 64 * c + 64)
                    ins = mm(bank(c)[:, 0:nk], qT[rows, h, i * P:(i + 1) * P], kT[rows, h, 0:nk], start=True, stop=True)
                ins.then_inc(S("att_s"), 1)
            elif kind == "attp":
                att_tail(n)
            elif kind == "s5_end":
                s5_y(15)
                e.wait_ge(S("dT_out"), 2)
                e.wait_ge(S("s5_carry"), 16)
                transposes(bank(7)[:, 0:P], [carry[:, :, 0]])
                transposes(bank(7)[:, P:2 * P], [carry[:, :, 1]])
                transposes(bank(7)[:, 2 * P:], [st[:, r, :] for r in range(2)]).then_inc(S("fin_full"), 1)
            elif kind == "s5d_bu":
                e.wait_ge(acc_out, 16)
                for ct in range(CT_N):
                    ins = mm(bank(n)[:, ct * NS_TOK:(ct + 1) * NS_TOK], b_lhs[:, ct, n, :], uT[:, ct // 4, NP_TOK:TOK],
                             start=True, stop=True)
                ins.then_inc(S("s5d_bu"), 1)
            elif kind == "s5d_y":
                e.wait_ge(S("s5d_h"), 1)
                for ct in range(8 * n, 8 * n + 8):
                    f, q = ct // 4, ct % 4
                    for r in range(2):
                        ins = mm(bank(2)[32 * q:32 * q + 32, f * NS_TOK:(f + 1) * NS_TOK], c_lhs[:, ct, r, :], H_dec[:, ct, r, :],
                                 start=r == 0, stop=r == 1)
                ins.then_inc(S("s5d_y"), 1)
            elif kind == "dkt":
                b, g = n // 2, n % 2
                e.wait_ge(S(f"dk_in{b % 2}"), 32 * (b // 2 + 1))
                if n == 0:
                    e.wait_ge(S("v_tok_ready"), 5)
                else:
                    e.wait_ge(S("dkT_done"), n)
                if n == 10:
                    e.wait_ge(S("dT_out"), 1)
                transposes(bank(7), [d_k[:, b % 2, pg, (2 * g + h) * P:(2 * g + h + 1) * P] for h in range(2) for pg in range(PAGES)])\
                    .then_inc(S("dkT_full"), 1)
            elif kind == "dks":
                rows = slice(32 * (n % 4), 32 * (n % 4) + 32)
                e.wait_ge(S("dkT_done"), 2 * n + 2)
                e.wait_ge(S("dqz"), 8)
                if n == 0:
                    e.wait_ge(S("k_tok_ready"), 5)
                if n == 4:
                    e.wait_ge(S("do_out"), 1)
                for h in range(NH):
                    ins = mm(bank(3)[rows, 0:PAST], d_qz[:, h, n, :], d_kT[:, h, :], start=h == 0, stop=h == NH - 1)
                if n % 4 == 3:
                    for h in range(NH):
                        ins = mm(bank(3)[:, PAST:DEC_W], d_qz[:, h, n - 3:n + 1, :].rearrange("p b r -> p (b r)"), kT[:, h, NP_TOK:TOK], start=h == 0, stop=h == NH - 1)
                ins.then_inc(S("ds_done"), 1)
            elif kind == "dpt":
                t = n
                e.wait_ge(S("dp"), t + 1)
                e.wait_ge(S("dkT_done"), 10 if t == 0 else 2 * DB)
                transposes(bank(7), [d_p[:, t, 0:P], d_p[:, t, P:2 * P], d_p[:, t, PAST:DEC_W]]).then_inc(S("dpT_full"), 1)
            elif kind == "dv":
                e.wait_ge(S("dpT"), n // 4 + 1)
                e.wait_ge(S(f"dv_in{n % DV_N}"), 32 * (n // DV_N + 1))
                if n % 4 == 0:
                    mm(bank(3), d_pTn[:, n:n + 4, :].rearrange("p b r -> p (b r)"), v_new[:], start=True, stop=False)
                out = bank(3)[32 * (n % 4):32 * (n % 4) + 32, :]
                for pg in range(PAGES):
                    ins = mm(out, d_pT[:, pg, n, :], d_v[:, n % DV_N, pg, :], start=False, stop=pg == PAGES - 1)
                ins.then_inc(S("dv_done"), 1)
            elif kind == "dot":
                t = n
                e.wait_ge(S("do_out"), t + 1)
                transposes(bank(7), [d_o[:, t, h * P:(h + 1) * P] for h in range(NH)]).then_inc(S("doT_full"), 1)
            elif kind == "subln":
                e.wait_ge(*counted("ssmn", "root", 1))
                for h in range(NH):
                    e.wait_ge(S("subln_sq"), h + 1)
                    for a in range(2):
                        ins = mm(halves(4)[32 * h:32 * h + 32, a, :], ones[:, 0:32], sq[:, h % 2, a * HALF:(a + 1) * HALF], start=True, stop=True)
                    ins.then_inc(S("subln_sum"), 1)
                e.wait_ge(S("subln_r"), 1)
                for h in range(NH):
                    if h >= 2:
                        e.wait_ge(S("subln_t"), h - 1)
                    row = slice(32 * h, 32 * h + 1)
                    for a in range(2):
                        ins = mm(halves(4 + 2 * (h % 2))[:, a, :], ones[row, :], rstd[row, a * HALF:(a + 1) * HALF], start=True, stop=True)
                    ins.then_inc(S("subln_rb"), 1)
            elif kind == "glu":
                e.wait_ge(S("y1_lo"), SF)
                e.wait_ge(S("yssm"), 16)
                e.wait_ge(S("fin_ready"), 2)
                unit(U_GLU, J_GLU, SF, 512, y1_hi, y1_lo)
            elif kind == "ssm_sq":
                e.wait_ge(*counted("ssmn", "add", SF - 1))
                e.wait_ge(acc_out, J_GLU + SF)
                spread_sum("ssmn")
            elif kind in ("mem_b", "mem_c"):
                e.wait_ge(S("ms_ready"), 2)
                e.wait_ge(S("subln_t"), NH)
                for k in MEM_TILES[kind]:
                    if k >= 2:
                        e.wait_ge(S("mn_lo"), k - 1)
                    transposes(bank(6 + k % 2), [mem_nat[:, t, k * P:(k + 1) * P] for t in range(2)]).then_inc(S("mT_full"), 1)
            elif kind == "out":
                u = U_OUT + n
                e.wait_ge(w_lo_ready, u + 1)
                if n == 0:
                    e.wait_ge(*counted("ssmn", "lo", SF))
                for m in range(2):
                    product(J_OUT + 2 * n + m, u % 2, 256, m * P, ssm_hi, ssm_lo, 0, 4, True, False, k_off=4)
                e.wait_ge(S("subln_lo"), NH)
                for m in range(2):
                    product(J_OUT + 2 * n + m, u % 2, 256, m * P, att_hi, att_lo, 0, 4, False, True).then_inc(acc_full, 1)

        def mk_unit(u):
            n = U_MK + u
            e.wait_ge(w_lo_ready, n + 1)
            for m in range(2):
                j = J_MK + 2 * u + m
                e.wait_ge(acc_out, j - 1)
                out = bank(2 * (j % 2))[:, 0:256]
                for k in range(KT):
                    if u < 4:
                        wc, xc = slice(k * 256 + m * P, k * 256 + (m + 1) * P), slice(0, NMEM)
                        terms = [(w[:, n % 2, wc], x[:, k, xc]) for w, x in ((w_hi, mn_hi), (w_hi, mn_lo), (w_lo, mn_hi))]
                    else:
                        wc, xc = slice(k * 256, (k + 1) * 256), slice(m * P, (m + 1) * P)
                        terms = [(x[:, k, xc], w[:, n % 2, wc]) for x, w in ((mn_hi, w_hi), (mn_hi, w_lo), (mn_lo, w_hi))]
                    for i, (l, r) in enumerate(terms):
                        ins = mm(out, l, r, start=k == 0 and i == 0, stop=k == KT - 1 and i == 2)
                ins.then_inc(acc_full, 1)

        e.wait_ge(S("mn_lo"), KT)
        mk_unit(0)
        e.wait_ge(*counted("n1", "add", KT - 1))
        spread_sum("n1")
        for u in range(1, 6):
            mk_unit(u)
        e.wait_ge(*counted("n2", "add", KT - 1))
        e.wait_ge(*counted("n1", "root", 1))
        spread_sum("n2")
        for u in range(6, 8):
            mk_unit(u)
        for g in range(4):
            t, k0 = g // 2, 4 * (g % 2)
            e.wait_ge(acc_out, J_MQ)
            if g >= 2:
                e.wait_ge(S("mk_tok_ready"), g - 1)
            else:
                e.wait_ge(*counted("n2", "root", 1))
            transposes(bank(6 + g % 2), [mkT[:, k0 + k, t * P:(t + 1) * P] for k in range(4)]).then_inc(S("mkt_full"), 1)
        e.wait_ge(*counted("n2", "lo", KT))
        for u in range(4):
            unit(U_MQ + u, J_MQ + 2 * u, KT, 256, x_hi, x_lo)

        def ma_tail(n):
            h, i = MATT[n]
            e.wait_ge(S("ma_p"), n + 1)
            if n >= 1:
                e.wait_ge(S("ma_pTo"), n)
            transposes(bank(6), [m_p[:, n % 2, k * P:(k + 1) * P] for k in range(2)]).then_inc(S("ma_pT"), 1)
            if i == 3:
                e.wait_ge(S("ma_pTo"), n + 1)
                for d in range(2):
                    if h:
                        e.wait_ge(S("ma_o"), 2 * (h - 1) + d + 1)
                    for k in range(2):
                        c = (2 * h + d) * P
                        ins = mm(bank(d), mv_tok[:, k, c:c + P], m_pT[:, k, :], start=k == 0, stop=k == 1)
                    ins.then_inc(S("ma_pv"), 1)

        e.wait_ge(acc_out, J_MO)
        e.wait_ge(S("mk_tok_ready"), 4)
        for n, (h, i) in enumerate(MATT):
            if n >= 2:
                e.wait_ge(S("ma_exp"), n - 1)
            for d in range(2):
                ins = mm(bank(4 + n % 2)[:, 0:NMEM], qm[:, 2 * h + d, i * P:(i + 1) * P], mkT[:, 2 * h + d, :], start=d == 0, stop=d == 1)
            ins.then_inc(S("ma_s"), 1)
            if n >= 1:
                ma_tail(n - 1)
        ma_tail(15)
        e.wait_ge(S("dmqz"), KT)
        e.wait_ge(S("ma_pTo"), 16)
        e.wait_ge(S("ma_exp"), 16)
        for b in range(DB):
            e.wait_ge(S(f"kv_in{b % KV_N}"), 16 * (b // KV_N + 1))
            for g in range(4):
                if b or g >= 2:
                    e.wait_ge(S("dmT_out"), 4 * b + g - 1)
                transposes(bank(6 + g % 2), [dm_kv[:, b % KV_N, t, (2 * g + k) * P:(2 * g + k + 1) * P] for k in range(2) for t in range(2)])\
                    .then_inc(S("dmT_pe"), 1)
            rows = slice(32 * (b % 4), 32 * (b % 4) + 32)
            e.wait_ge(S("dmT_out"), 4 * b + 4)
            for k in range(KT):
                ins = mm(bank(4 + b // 4)[rows, 0:NMEM], dm_qz[:, b, k, :], dm_kT[:, k, :], start=k == 0, stop=k == KT - 1)
            ins.then_inc(S("dms"), 1)
        for t in range(2):
            e.wait_ge(S("dm_pr"), t + 1)
            transposes(bank(6 + t), [dm_p[:, t, k * P:(k + 1) * P] for k in range(2)]).then_inc(S("dm_pTf"), 1)
        e.wait_ge(S("dm_pTo"), 2)
        for b in range(DB):
            t, rows = b // 4, slice(32 * (b % 4), 32 * (b % 4) + 32)
            i = DB + b
            e.wait_ge(S(f"kv_in{i % KV_N}"), 16 * (i // KV_N + 1))
            for g in range(2):
                for k in range(2):
                    ins = mm(bank(4 + 2 * t + g)[rows, :], dm_pT[:, k, t, rows], dm_kv[:, i % KV_N, k, g * 512:(g + 1) * 512],
                             start=k == 0, stop=k == 1)
            ins.then_inc(S("dm_pv"), 1)
        for t in range(2):
            e.wait_ge(S("dmo_out"), 2 * t + 2)
            e.wait_ge(S("ma_o"), 8)
            flat = pall[:, 2 * t:2 * t + 2, :].rearrange("p a b -> p (a b)")
            transposes(flat, [dm_o[:, t, k * P:(k + 1) * P] for k in range(KT)]).then_inc(S("dmoT"), 1)
        e.wait_ge(S("dmx"), 8)
        e.wait_ge(S("ma_o"), 8)
        for u in range(4):
            unit(U_MO + u, J_MO + 2 * u, KT, 256, x_hi, x_lo)
        for name in ("n3", "n4"):
            if name == "n3":
                e.wait_ge(S("dmo_out"), 4)
            else:
                e.wait_ge(*counted("n3", "root", 1))
            e.wait_ge(*counted(name, "add", KT - 1))
            spread_sum(name)
        e.wait_ge(*counted("n4", "lo", KT))
        with e.Fori(0, PAIRS) as i:
            for s_ in range(2):
                slot = (U_FFN + s_) % 2
                e.wait_ge(w_lo_ready, i * 2 + (U_FFN + s_ + 1))
                for m in range(2):
                    j = 2 * s_ + m
                    e.wait_ge(acc_out, i * 4 + (J_FFN + j - 1))
                    product(m, slot, 256, m * P, x_hi, x_lo, 0, KT).then_inc(acc_full, 1)
        for n in range(U_DOWN, N_UNITS):
            c, part = (n - U_DOWN) // 3, (n - U_DOWN) % 3
            k0, kts = DOWN_K[part]
            if n == U_DOWN:
                e.wait_ge(parts_lo, LO_FFN + FT)
            unit(n, J_DOWN + 2 * c, kts, 256, g_hi, g_lo, k0, part == 0, part == 2)
        e.wait_ge(*counted("n5", "add", KT - 1))
        spread_sum("n5")
        e.wait_ge(*counted("n5", "y", KT))
        for t in range(5):
            w = P if t < 4 else NS_TOK
            for g in range(4):
                if t:
                    e.wait_ge(S("y_out_ready"), 4 * (t - 1) + g + 1)
                for k in range(2):
                    ins = e.transpose(bank(4 + g)[0:w, k * P:(k + 1) * P], yT[:, 2 * g + k, t * P:t * P + w], ident[:])
                ins.then_inc(S("yt_full"), 1)

    ctx.close()


_OUTS = [("y_prompt", (1, NP_TOK, D)), ("y_sample", (DB, DT, D)),
         ("new_k_prompt", (1, 1, NP_TOK, NH, 2 * HD)), ("new_v_prompt", (1, 1, NP_TOK, NH, 2 * HD)),
         ("new_k_sample", (1, DB, DT, NH, 2 * HD)), ("new_v_sample", (1, DB, DT, NH, 2 * HD)),
         ("ssm_re_prompt", (1, 1, NG, SP_)), ("ssm_im_prompt", (1, 1, NG, SP_)),
         ("ssm_re_sample", (1, DB, NG, SP_)), ("ssm_im_sample", (1, DB, NG, SP_)),
         ("mem_k_prompt", (1, 1, NMEM, MH, MD)), ("mem_v_prompt", (1, 1, NMEM, MH, MD))]


def kernel(**inputs):
    import concourse.bacc as _bacc
    from concourse.bass_utils import run_bass_kernel_spmd as _run

    nc = _bacc.Bacc("TRN2", target_bir_lowering=False, num_devices=1)
    arrays, A = {}, {}
    for name, a in list(inputs.items()) + list(shape_tables().items()):
        a = np.ascontiguousarray(a)
        arrays[f"in_{name}"] = a
        A[name] = nc.dram_tensor(f"in_{name}", a.shape, mybir.dt.from_np(a.dtype), kind="ExternalInput").ap()
    O = {name: nc.dram_tensor(f"out_{name}", shape, F32, kind="ExternalOutput").ap() for name, shape in _OUTS}
    build(nc, A, O)
    r = _run(nc, [arrays], core_ids=[0])
    return tuple(r.results[0][f"out_{name}"] for name, _ in _OUTS)
```
